# Optimizing a Trainium2 kernel written in Bass

```python
import math
import jax, jax.numpy as jnp
from jax import lax
import numpy as np

D_MODEL = 1024
BATCH = 1
SEQ = 512
DEPTH = 2

HG_HEADS = 4
HG_DK = 128
HG_DV = 128
HG_WIDTH = HG_HEADS * HG_DK
HG_CHUNK = 16
HG_F_MIN = 1e-6
S5_WIDTH = 512
S5_GROUP = 16
S5_GROUPS = S5_WIDTH // S5_GROUP
S5_STATE = 64
RET_HEADS = 4
RET_DK = 128
RET_DV = 128
RET_WIDTH = RET_HEADS * RET_DK
RET_CHUNK = 128
ROPE_BASE = 10000.0
N_BRANCH = 3
MIX_WIDTH = HG_WIDTH + S5_WIDTH + RET_WIDTH
IN_COLS = 4 * HG_WIDTH + S5_WIDTH + 4 * RET_WIDTH + N_BRANCH * D_MODEL
MEM_LEN = 256
XA_HEADS = 4
XA_DH = D_MODEL // XA_HEADS
PEER_HEADS = 8
PEER_NKEYS = 128
PEER_EXPERTS = PEER_NKEYS * PEER_NKEYS
PEER_DQ = 256
PEER_DH = PEER_DQ // 2
PEER_TOPK = 16
PEER_BLOCK = 128
EPS = 1e-6
F32 = jnp.float32

kernel_name = 'hybrid_hgrn2_s5_retnet_peer_block'

def rmsnorm(x, gain):
    xf = x.astype(F32)
    y = xf * lax.rsqrt(jnp.mean(xf * xf, axis=-1, keepdims=True) + EPS)
    return (y * gain.astype(F32)).astype(x.dtype)

def _to_chunks(a, n_heads, chunk):
    b, length, width = a.shape
    return a.reshape(b, length // chunk, chunk, n_heads, width // n_heads).transpose(0, 3, 1, 2, 4)

def _from_chunks(a):
    b, h, n, c, d = a.shape
    return a.transpose(0, 2, 3, 1, 4).reshape(b, n * c, h, d)

def _inter_chunk(q_dec, k_dec, v, chunk_decay):
    bsz, h, _, _, dk = q_dec.shape
    dv = v.shape[-1]
    xs = (jnp.moveaxis(q_dec, 2, 0), jnp.moveaxis(k_dec, 2, 0), jnp.moveaxis(v, 2, 0), jnp.moveaxis(chunk_decay, 2, 0))

    def step(state, inp):
        qd, kd, vv, dec = inp
        out = jnp.einsum('bhck,bhkv->bhcv', qd, state)
        state = dec[..., None] * state + jnp.einsum('bhck,bhcv->bhkv', kd, vv)
        return state, out

    s0 = jnp.zeros((bsz, h, dk, dv), q_dec.dtype)
    _, out = lax.scan(step, s0, xs)
    return jnp.moveaxis(out, 0, 2)

def hgrn2(q, f_logit, inp, gate, lb, norm_g):
    bsz, length, _ = q.shape
    h, dk, dv, c = HG_HEADS, HG_DK, HG_DV, HG_CHUNK
    z = f_logit.astype(F32)
    lbf = lb.astype(F32)
    f = lbf + (1.0 - lbf) * jax.nn.sigmoid(z)
    log_f = jnp.log(jnp.clip(f, HG_F_MIN, 1.0))
    k = (1.0 - lbf) * jax.nn.sigmoid(-z)
    qc = _to_chunks(q.astype(F32) * dk ** -0.5, h, c)
    kc = _to_chunks(k, h, c)
    vc = _to_chunks(inp.astype(F32), h, c)
    b = jnp.cumsum(_to_chunks(log_f, h, c), axis=3)
    causal = jnp.tril(jnp.ones((c, c), bool))[:, :, None]
    diff = b[..., :, None, :] - b[..., None, :, :]
    decay = jnp.where(causal, jnp.exp(jnp.minimum(diff, 0.0)), 0.0)
    att = jnp.einsum('bhntk,bhntsk,bhnsk->bhnts', qc, decay, kc)
    o = jnp.einsum('bhnts,bhnsv->bhntv', att, vc)
    b_last = b[..., -1:, :]
    o = o + _inter_chunk(qc * jnp.exp(b), kc * jnp.exp(b_last - b), vc, jnp.exp(b_last[..., 0, :]))
    o = _from_chunks(o)
    o = o * lax.rsqrt(jnp.mean(o * o, axis=-1, keepdims=True) + EPS) * norm_g.astype(F32).reshape(h, dv)
    return o.reshape(bsz, length, h * dv) * jax.nn.silu(gate.astype(F32))

def s5(u, lam_re, lam_im, log_step, b_re, b_im, c_re, c_im, d, w_glu, b_glu):
    bsz, length, _ = u.shape
    uf = u.astype(F32).reshape(bsz, length, S5_GROUPS, S5_GROUP)
    lr = jnp.minimum(lam_re.astype(F32), -1e-4)
    li = lam_im.astype(F32)
    dt = jnp.exp(log_step.astype(F32))[:, None]
    mag = jnp.exp(lr * dt)
    a_re = mag * jnp.cos(li * dt)
    a_im = mag * jnp.sin(li * dt)
    den = lr * lr + li * li
    z_re = ((a_re - 1.0) * lr + a_im * li) / den
    z_im = (a_im * lr - (a_re - 1.0) * li) / den
    bb_re = z_re[..., None] * b_re.astype(F32) - z_im[..., None] * b_im.astype(F32)
    bb_im = z_re[..., None] * b_im.astype(F32) + z_im[..., None] * b_re.astype(F32)
    bu_re = jnp.einsum('blgc,gpc->blgp', uf, bb_re)
    bu_im = jnp.einsum('blgc,gpc->blgp', uf, bb_im)
    ar_full = jnp.broadcast_to(a_re, bu_re.shape)
    ai_full = jnp.broadcast_to(a_im, bu_re.shape)

    def combine(e1, e2):
        ar1, ai1, br1, bi1 = e1
        ar2, ai2, br2, bi2 = e2
        return (ar2 * ar1 - ai2 * ai1, ar2 * ai1 + ai2 * ar1,
                ar2 * br1 - ai2 * bi1 + br2, ar2 * bi1 + ai2 * br1 + bi2)

    _, _, x_re, x_im = lax.associative_scan(combine, (ar_full, ai_full, bu_re, bu_im), axis=1)
    y = (jnp.einsum('blgp,gcp->blgc', x_re, c_re.astype(F32))
         - jnp.einsum('blgp,gcp->blgc', x_im, c_im.astype(F32))
         + d.astype(F32).reshape(S5_GROUPS, S5_GROUP) * uf)
    y = jax.nn.gelu(y.reshape(bsz, length, S5_WIDTH))
    return y * jax.nn.sigmoid(y @ w_glu.astype(F32) + b_glu.astype(F32))

def rope(x, positions):
    half = x.shape[-1] // 2
    inv = ROPE_BASE ** (-jnp.arange(half, dtype=F32) / half)
    ang = positions.astype(F32)[:, :, None, None] * inv
    cos, sin = jnp.cos(ang), jnp.sin(ang)
    x1, x2 = x[..., :half], x[..., half:]
    return jnp.concatenate([x1 * cos - x2 * sin, x1 * sin + x2 * cos], axis=-1)

def retention(q, k, v, gate, positions):
    bsz, length, _ = q.shape
    h, dk, dv, c = RET_HEADS, RET_DK, RET_DV, RET_CHUNK
    n = length // c
    qh = rope(q.astype(F32).reshape(bsz, length, h, dk), positions).reshape(bsz, length, h * dk)
    kh = (rope(k.astype(F32).reshape(bsz, length, h, dk), positions) * dk ** -0.5).reshape(bsz, length, h * dk)
    qc = _to_chunks(qh, h, c)
    kc = _to_chunks(kh, h, c)
    vc = _to_chunks(v.astype(F32), h, c)
    log_g = jnp.log1p(-jnp.exp2(-5.0 - jnp.arange(h, dtype=F32)))
    idx = jnp.arange(c, dtype=F32)
    rel = idx[:, None] - idx[None, :]
    dmat = jnp.where(rel >= 0, jnp.exp(log_g[:, None, None] * jnp.maximum(rel, 0.0)), 0.0)
    scores = jnp.einsum('bhntd,bhnsd->bhnts', qc, kc) * dmat[None, :, None]
    o = jnp.einsum('bhnts,bhnsv->bhntv', scores, vc)
    q_dec = qc * jnp.exp(log_g[:, None] * (idx + 1.0))[None, :, None, :, None]
    k_dec = kc * jnp.exp(log_g[:, None] * (c - 1.0 - idx))[None, :, None, :, None]
    chunk_decay = jnp.broadcast_to(jnp.exp(log_g * c)[None, :, None, None], (bsz, h, n, dk))
    o = _from_chunks(o + _inter_chunk(q_dec, k_dec, vc, chunk_decay))
    mu = jnp.mean(o, axis=-1, keepdims=True)
    var = jnp.mean((o - mu) ** 2, axis=-1, keepdims=True)
    o = (o - mu) * lax.rsqrt(var + EPS)
    return o.reshape(bsz, length, h * dv) * jax.nn.silu(gate.astype(F32))

def cross_attn(h, mem_n, wq, wkv, wo):
    bsz, length, d = h.shape
    m = mem_n.shape[1]
    q = (h @ wq).reshape(bsz, length, XA_HEADS, XA_DH)
    k, v = jnp.split(mem_n @ wkv, 2, axis=-1)
    k = k.reshape(bsz, m, XA_HEADS, XA_DH)
    v = v.reshape(bsz, m, XA_HEADS, XA_DH)
    s = jnp.einsum('blhd,bmhd->bhlm', q, k).astype(F32) * XA_DH ** -0.5
    p = jax.nn.softmax(s, axis=-1).astype(h.dtype)
    o = jnp.einsum('bhlm,bmhd->blhd', p, v).reshape(bsz, length, d)
    return o @ wo

def peer(h, wq, keys, u_tab, v_tab):
    bsz, length, d = h.shape
    q = (h @ wq).astype(F32).reshape(bsz, length, PEER_HEADS, 2, PEER_DH)
    s = jnp.einsum('blhpd,hpkd->blhpk', q, keys.astype(F32))
    s_top, i_top = lax.top_k(s, PEER_TOPK)
    cand = (s_top[..., 0, :, None] + s_top[..., 1, None, :]).reshape(bsz, length, PEER_HEADS, PEER_TOPK * PEER_TOPK)
    cand_idx = (i_top[..., 0, :, None] * PEER_NKEYS + i_top[..., 1, None, :]).reshape(bsz, length, PEER_HEADS, PEER_TOPK * PEER_TOPK)
    best, pos = lax.top_k(cand, PEER_TOPK)
    idx = jnp.take_along_axis(cand_idx, pos, axis=-1)
    gates = jax.nn.softmax(best, axis=-1)
    nb = length // PEER_BLOCK
    hb = h.reshape(bsz, nb, PEER_BLOCK, d).swapaxes(0, 1)
    ib = idx.reshape(bsz, nb, PEER_BLOCK, PEER_HEADS, PEER_TOPK).swapaxes(0, 1)
    gb = gates.reshape(bsz, nb, PEER_BLOCK, PEER_HEADS, PEER_TOPK).swapaxes(0, 1)

    def block(args):
        hh, ii, gg = args
        u = u_tab[ii]
        act = jax.nn.gelu(jnp.einsum('bthkd,btd->bthk', u, hh).astype(F32)) * gg
        vv = v_tab[ii]
        return jnp.einsum('bthk,bthkd->btd', act.astype(h.dtype), vv)

    y = lax.map(block, (hb, ib, gb))
    return y.swapaxes(0, 1).reshape(bsz, length, d)

def setup_inputs(seed: int = 0) -> dict:
    key = jax.random.key(seed)
    keys = jax.random.split(key, 48)
    ctr = [0]

    def nk():
        k = keys[ctr[0]]
        ctr[0] += 1
        return k

    def nrm(shape, scale):
        return jax.random.normal(nk(), shape, F32) * scale

    def gain(shape):
        return 1.0 + nrm(shape, 0.02)

    L, D = DEPTH, D_MODEL
    x = nrm((BATCH, SEQ, D), 1.0)
    mem = nrm((BATCH, MEM_LEN, D), 1.0)
    offs = jax.random.randint(nk(), (BATCH, 1), 0, 4096, dtype=jnp.int32)
    positions = offs + jnp.arange(SEQ, dtype=jnp.int32)[None, :]
    n_idx = jnp.arange(S5_STATE, dtype=F32)
    return {
        'x': x,
        'mem': mem,
        'positions': positions,
        'norm_mix': gain((L, D)),
        'w_in': nrm((L, D, IN_COLS), D ** -0.5),
        'b_gate': nrm((L, N_BRANCH * D), 0.01),
        'hgrn_lb': nrm((L, HG_WIDTH), 0.1),
        'hgrn_norm': gain((L, HG_WIDTH)),
        's5_lambda_re': -0.5 + nrm((L, S5_GROUPS, S5_STATE), 0.01),
        's5_lambda_im': jnp.pi * n_idx + nrm((L, S5_GROUPS, S5_STATE), 0.01),
        's5_log_step': jax.random.uniform(nk(), (L, S5_GROUPS), F32, math.log(1e-3), math.log(1e-1)),
        's5_b_re': nrm((L, S5_GROUPS, S5_STATE, S5_GROUP), (2.0 * S5_GROUP) ** -0.5),
        's5_b_im': nrm((L, S5_GROUPS, S5_STATE, S5_GROUP), (2.0 * S5_GROUP) ** -0.5),
        's5_c_re': nrm((L, S5_GROUPS, S5_GROUP, S5_STATE), (2.0 * S5_STATE) ** -0.5),
        's5_c_im': nrm((L, S5_GROUPS, S5_GROUP, S5_STATE), (2.0 * S5_STATE) ** -0.5),
        's5_d': nrm((L, S5_WIDTH), 1.0),
        's5_w_glu': nrm((L, S5_WIDTH, S5_WIDTH), S5_WIDTH ** -0.5),
        's5_b_glu': nrm((L, S5_WIDTH), 0.01),
        'w_branch': nrm((L, MIX_WIDTH, D), HG_WIDTH ** -0.5),
        'w_out': nrm((L, D, D), D ** -0.5),
        'norm_cross': gain((L, D)),
        'norm_mem': gain((L, D)),
        'xa_wq': nrm((L, D, D), D ** -0.5),
        'xa_wkv': nrm((L, D, 2 * D), D ** -0.5),
        'xa_wo': nrm((L, D, D), D ** -0.5),
        'norm_ffn': gain((L, D)),
        'peer_wq': nrm((L, D, PEER_HEADS * PEER_DQ), D ** -0.5),
        'peer_keys': nrm((L, PEER_HEADS, 2, PEER_NKEYS, PEER_DH), PEER_DH ** -0.5),
        'peer_u': nrm((L, PEER_EXPERTS, D), D ** -0.5),
        'peer_v': nrm((L, PEER_EXPERTS, D), 0.25),
        'norm_final': gain((D,)),
    }

def reference(x, mem, positions, norm_mix, w_in, b_gate, hgrn_lb, hgrn_norm, s5_lambda_re, s5_lambda_im,
              s5_log_step, s5_b_re, s5_b_im, s5_c_re, s5_c_im, s5_d, s5_w_glu, s5_b_glu, w_branch, w_out,
              norm_cross, norm_mem, xa_wq, xa_wkv, xa_wo, norm_ffn, peer_wq, peer_keys, peer_u, peer_v,
              norm_final):
    bsz, length, d = x.shape
    sm = jax.nn.softmax(hgrn_lb.astype(F32), axis=0)
    lower_bounds = jnp.cumsum(sm, axis=0) - sm[0]
    split_at = np.cumsum([HG_WIDTH] * 4 + [S5_WIDTH] + [RET_WIDTH] * 4).tolist()
    e0, e1 = HG_WIDTH, HG_WIDTH + S5_WIDTH
    for l in range(DEPTH):
        h = rmsnorm(x, norm_mix[l])
        proj = h @ w_in[l]
        hg_q, hg_f, hg_i, hg_g, s5_u, rt_q, rt_k, rt_v, rt_g, gate_logits = jnp.split(proj, split_at, axis=-1)
        o_hg = hgrn2(hg_q, hg_f, hg_i, hg_g, lower_bounds[l], hgrn_norm[l]).astype(h.dtype)
        o_s5 = s5(s5_u, s5_lambda_re[l], s5_lambda_im[l], s5_log_step[l], s5_b_re[l], s5_b_im[l],
                  s5_c_re[l], s5_c_im[l], s5_d[l], s5_w_glu[l], s5_b_glu[l]).astype(h.dtype)
        o_rt = retention(rt_q, rt_k, rt_v, rt_g, positions).astype(h.dtype)
        gates = jax.nn.sigmoid((gate_logits + b_gate[l]).astype(F32)).reshape(bsz, length, N_BRANCH, d).astype(h.dtype)
        wb = w_branch[l]
        merged = (gates[:, :, 0] * (o_hg @ wb[:e0])
                  + gates[:, :, 1] * (o_s5 @ wb[e0:e1])
                  + gates[:, :, 2] * (o_rt @ wb[e1:]))
        x = x + merged @ w_out[l]
        x = x + cross_attn(rmsnorm(x, norm_cross[l]), rmsnorm(mem, norm_mem[l]), xa_wq[l], xa_wkv[l], xa_wo[l])
        x = x + peer(rmsnorm(x, norm_ffn[l]), peer_wq[l], peer_keys[l], peer_u[l], peer_v[l])
    return rmsnorm(x, norm_final)


_drawn_inputs = setup_inputs


def setup_inputs(seed=0):
    import zlib

    import numpy as np

    out = dict(_drawn_inputs(seed))
    spreads = {}
    factors = {'b_gate': 5.43,
     'hgrn_norm': 3.043,
     's5_lambda_re': 64.0,
     's5_b_re': 2.669,
     's5_c_im': 2.725,
     's5_b_glu': 7.892,
     'norm_cross': 5.236,
     'norm_mem': 4.332,
     'norm_final': 7.66,
     'norm_ffn': 3.196}
    for name, (base, spread) in spreads.items():
        noise = np.random.default_rng([zlib.crc32(name.encode()), seed]).standard_normal(out[name].shape)
        drawn = base * np.exp(spread * noise) if base else spread * noise
        out[name] = __import__('jax').numpy.asarray(drawn.astype(out[name].dtype))
    for name, factor in factors.items():
        out[name] = (out[name] * factor).astype(out[name].dtype)
    return out
```

```python
import itertools
from contextlib import ExitStack, contextmanager

import numpy as np

import concourse.bass as bass
from concourse import mybir

P = 128
D = 1024
T = 512
L = 2
TB = T // P
KD = D // P
W = 512
H = 4
MEM = 256
MB = MEM // P
EPS = 1e-6
G5, C5, S5P = 32, 16, 64
J5, N5 = 8, T // 8
PH, PK, TOPK = 8, 128, 16
SLOTS = PH * TOPK
GCH = 64
GSCALE = 4096.0
GE = 4
LEVELS = [64, 32, 16, 8, 4, 2, 1]

F32 = mybir.dt.float32
F32R = mybir.dt.float32r
F16 = mybir.dt.float16
I32 = mybir.dt.int32
U32 = mybir.dt.uint32
ALU = mybir.AluOpType
ACT = mybir.ActivationFunctionType
AX = mybir.AxisListType.X

TWO_PI = 2.0 * np.pi
C1 = 6.28125
C2 = float(np.float32(round((TWO_PI - C1) * 2**21) / 2**21))
C3 = float(np.float32(TWO_PI - C1 - C2))
ROUND = 1.5 * 2.0**23
ROUND13 = 1.5 * 2.0**10
PI_IN = 3.1415925

_SMALL = [("norm_mix", KD), ("norm_cross", KD), ("norm_mem", KD), ("norm_ffn", KD), ("b_gate", 3 * KD),
          ("hgrn_norm", H), ("b_glu", H), ("s5_d", G5), ("lam_re", G5), ("lam_im", G5), ("log_step", G5)]
COL, _n = {}, 0
for _name, _w in _SMALL:
    COL[_name] = (_n, _n + _w)
    _n += _w
NSMALL = _n


_serial = itertools.count()
_pool = []


def buffer(nc, name, shape, dtype):
    return nc.sbuf_tensor(f"{name}_{next(_serial)}", shape, dtype)


@contextmanager
def stage(nc, *names):
    assert len(names) <= len(_pool)
    yield dict(zip(names, _pool))
    with nc.Block() as block:
        @block.sync
        def _(sp):
            sp.sem_clear(range(_pool[0].num, _pool[len(names) - 1].num + 1))


class Resident:
    pass


class SsmTables:

    def __init__(self, sin, cos, decay, gb, pc, c1):
        self.sin, self.cos, self.decay, self.gb, self.pc, self.c1 = sin, cos, decay, gb, pc, c1


class Steps:

    def __init__(self, eng, sem):
        self.eng, self.sem, self.n = eng, sem, 0

    def then(self, ins):
        ins.then_inc(self.sem, 1)
        self.n += 1
        return self.n

    def settle(self):
        self.eng.wait_ge(self.sem, self.n)

    def link(self, ins):
        self.then(ins)
        self.settle()


def tile_at(dram, index):
    return dram[bass.ds(index, 1)].rearrange("a p n -> (a p) n")


def over_pairs(eng, n, body):
    for p in range(min(2, n)):
        body(p, p, True)
    pairs = n // 2
    if pairs > 1:
        with eng.Fori(1, pairs) as i:
            for p in range(2):
                body(i * 2 + p, p, False)
    if n > 2 and n % 2:
        body(n - 1, 0, False)


def over_groups(eng, n, body):
    for p in range(2):
        body(p, p, True, False)
    with eng.Fori(1, n // 2 - 1) as i:
        for p in range(2):
            body(i * 2 + p, p, False, False)
    for p in range(2):
        body(n - 2 + p, p, False, p == 1)


class Linear:

    def __init__(self, nc, s, kind, n_tiles, src, wbufs, act, K, nb, N, psum):
        self.nc, self.s, self.kind, self.n, self.src, self.wb = nc, s, kind, n_tiles, src, wbufs
        self.act, self.K, self.nb, self.N, self.ps = act, K, nb, N, psum

    def sync(self, sp):
        ready = (self.s["w_even"], self.s["w_odd"])

        def load(t, p, first):
            if not first:
                sp.wait_ge(self.s["mm_done"], (t - 1) * self.nb)
            sp.dma_start(self.wb[p][:].rearrange("p k n -> p (k n)"), self.src(t)).then_inc(ready[p], 16)
        over_pairs(sp, self.n, load)

    def tensor(self, pe):
        ready = (self.s["w_even"], self.s["w_odd"])
        nc = self.nc

        def tile(t, p, first):
            pe.wait_ge(ready[p], 16 if first else (t - p) * 8 + 16)
            for b in range(self.nb):
                if not first:
                    pe.wait_ge(self.s["evac_done"], (t - 2) * self.nb + b + 1)
                out = self.ps[:, 4 * p + b, 0:self.N]
                for k in range(self.K):
                    if self.kind == "fm":
                        lhsT = self.wb[p][:, k, b * P:(b + 1) * P]
                        rhs = self.act[:, k, 0:self.N]
                    else:
                        lhsT = self.act[:, k, b * P:(b + 1) * P]
                        rhs = self.wb[p][:, k, :]
                    mm = nc.tensor.matmul(out, lhsT, rhs, start=(k == 0), stop=(k == self.K - 1))
                mm.then_inc(self.s["mm_done"], 1)
        over_pairs(pe, self.n, tile)

    def evacuate(self, eng, copy):
        def tile(t, p, first):
            for b in range(self.nb):
                eng.wait_ge(self.s["mm_done"], t * self.nb + b + 1)
                copy(t, b, self.ps[:, 4 * p + b, 0:self.N]).then_inc(self.s["evac_done"], 1)
        over_pairs(eng, self.n, tile)


LINEAR_SEMS = ("w_even", "w_odd", "mm_done", "evac_done")


def reduce_angle(v, st, out, ang, tmp):
    st.link(v.tensor_scalar(tmp, ang, 1.0 / TWO_PI, ROUND, ALU.mult, ALU.add))
    st.link(v.tensor_scalar(tmp, tmp, -ROUND, None, ALU.add))
    st.link(v.scalar_tensor_tensor(out, tmp, -C1, ang, ALU.mult, ALU.add))
    st.link(v.scalar_tensor_tensor(out, tmp, -C2, out, ALU.mult, ALU.add))
    st.link(v.scalar_tensor_tensor(out, tmp, -C3, out, ALU.mult, ALU.add))
    st.link(v.tensor_scalar(out, out, PI_IN, -PI_IN, ALU.min, ALU.max))


def cos_argument(v, st, out, red, tmp):
    st.link(v.tensor_scalar(out, red, float(np.pi / 2), None, ALU.add))
    st.link(v.tensor_scalar(tmp, out, float(np.pi), -TWO_PI, ALU.is_gt, ALU.mult))
    st.link(v.tensor_tensor(out, out, tmp, ALU.add))
    st.link(v.tensor_scalar(out, out, PI_IN, -PI_IN, ALU.min, ALU.max))


def setup_stage(nc, io, m):
    with ExitStack() as ctx, stage(nc, "loaded", "dve_step", "angles_ready", "trig_ready", "lb_shifted", "lb_exp") as s:
        pos_i = ctx.enter_context(buffer(nc, "pos_i", [P, T], I32))
        ang = ctx.enter_context(buffer(nc, "ang", [P, T], F32))
        tmp = ctx.enter_context(buffer(nc, "tmp", [P, T], F32))
        red = ctx.enter_context(buffer(nc, "red", [P, T], F32))
        cred = ctx.enter_context(buffer(nc, "cred", [P, T], F32))
        lbs = ctx.enter_context(buffer(nc, "lbs", [P, L, H], F32))
        lbt = ctx.enter_context(buffer(nc, "lbt", [P, 2, H], F32))
        loads = [(pos_i[:], io["positions"].partition_broadcast(P)), (m.X[:], io["x"]), (m.ident[:], io["c_ident"]), (m.perm[:], io["c_perm"]),
                 (m.cols[:], io["c_cols"]), (lbs[:], io["hgrn_lb"])]
        with nc.Block() as block:
            @block.sync
            def _(sp):
                for dst, src in loads:
                    sp.dma_start(dst, src).then_inc(s["loaded"], 16)

            @block.vector
            def _(v):
                st = Steps(v, s["dve_step"])
                v.wait_ge(s["loaded"], 16 * len(loads))
                st.then(v.memset(m.ones[:], 1.0))
                st.link(v.tensor_copy(ang[:], pos_i[:]))
                st.link(v.tensor_scalar(ang[:], ang[:], m.cols[:, 0:1], None, ALU.mult))
                reduce_angle(v, st, red[:], ang[:], tmp[:])
                cos_argument(v, st, cred[:], red[:], tmp[:])
                st.link(v.tensor_tensor(lbt[:, 0, :], lbs[:, 0, :], lbs[:, 1, :], ALU.max))
                st.then(v.tensor_tensor(lbs[:, 0, :], lbs[:, 0, :], lbt[:, 0, :], ALU.subtract))
                v.tensor_tensor(lbs[:, 1, :], lbs[:, 1, :], lbt[:, 0, :], ALU.subtract).then_inc(s["angles_ready"], 1)
                v.wait_ge(s["trig_ready"], 4)
                st.link(v.tensor_tensor(lbt[:, 0, :], lbs[:, 0, :], lbs[:, 1, :], ALU.add))
                st.link(v.reciprocal(lbt[:, 1, :], lbt[:, 0, :]))
                st.link(v.memset(m.lb_all[:, 0, :], 0.0))
                st.link(v.tensor_tensor(m.lb_all[:, 1, :], lbs[:, 1, :], lbt[:, 1, :], ALU.mult))
                st.link(v.tensor_scalar(m.sin[:], m.sin[:], m.cols[:, 1:2], None, ALU.mult))

            @block.scalar
            def _(a):
                a.wait_ge(s["angles_ready"], 1)
                a.activation(m.sin[:], red[:], ACT.Sin).then_inc(s["trig_ready"], 1)
                a.activation(m.cos[:], cred[:], ACT.Sin).then_inc(s["trig_ready"], 1)
                a.activation(lbs[:, 0, :], lbs[:, 0, :], ACT.Exp).then_inc(s["trig_ready"], 1)
                a.activation(lbs[:, 1, :], lbs[:, 1, :], ACT.Exp).then_inc(s["trig_ready"], 1)


def norm_stage(nc, m, src, nblk, gain, dst, psum, load=None, small=None):
    with ExitStack() as ctx, stage(nc, "x_ready", "sumsq", "dve_step", "root", "scaled", "turned") as s:
        xn = ctx.enter_context(buffer(nc, "xn", [P, nblk, D], F32))
        ss = ctx.enter_context(buffer(nc, "ss", [P, TB], F32))
        rs = ctx.enter_context(buffer(nc, "rs", [P, TB], F32))
        with nc.Block() as block:
            @block.sync
            def _(sp):
                for dst_, src_ in (load or []):
                    sp.dma_start(dst_, src_).then_inc(s["x_ready"], 16)

            @block.scalar
            def _(a):
                if load:
                    a.wait_ge(s["x_ready"], 16 * len(load))
                for b in range(nblk):
                    a.activation(xn[:, b, :], src[:, b, :], ACT.Square, accum_out=ss[:, b:b + 1]).then_inc(s["sumsq"], 1)
                a.wait_ge(s["dve_step"], 1)
                a.activation(rs[:, 0:nblk], ss[:, 0:nblk], ACT.Sqrt).then_inc(s["root"], 1)

            @block.vector
            def _(v):
                v.wait_ge(s["sumsq"], nblk)
                if load:
                    v.wait_ge(s["x_ready"], 16 * len(load))
                st = Steps(v, s["dve_step"])
                st.then(v.tensor_scalar(ss[:, 0:nblk], ss[:, 0:nblk], 1.0 / D, EPS, ALU.mult, ALU.add))
                v.wait_ge(s["root"], 1)
                st.link(v.reciprocal(ss[:, 0:nblk], rs[:, 0:nblk]))
                for b in range(nblk):
                    v.tensor_scalar(xn[:, b, :], src[:, b, :], ss[:, b:b + 1], None, ALU.mult).then_inc(s["scaled"], 1)
                for k in range(KD):
                    v.wait_ge(s["turned"], k + 1)
                    st.then(v.tensor_scalar(dst[:, k, 0:nblk * P], psum[:, k, 0:nblk * P], gain[:, k:k + 1], None, ALU.mult))

            @block.tensor
            def _(pe):
                pe.wait_ge(s["scaled"], nblk)
                for k in range(KD):
                    for b in range(nblk):
                        mm = nc.tensor.transpose(psum[:, k, b * P:(b + 1) * P], xn[:, b, k * P:(k + 1) * P], m.ident[:])
                    mm.then_inc(s["turned"], 1)


def linear_stage(nc, kind, n_tiles, src, act, K, nb, N, psum, copy, on="scalar", name="w"):
    with ExitStack() as ctx, stage(nc, *LINEAR_SEMS) as s:
        wbufs = [ctx.enter_context(buffer(nc, f"{name}{i}", [P, K, W], F32)) for i in range(2)]
        lin = Linear(nc, s, kind, n_tiles, src, wbufs, act, K, nb, N, psum)
        with nc.Block() as block:
            block.sync(lin.sync)
            block.tensor(lin.tensor)
            if on == "scalar":
                block.scalar(lambda a: lin.evacuate(a, copy))
            else:
                block.vector(lambda v: lin.evacuate(v, copy))


def hgrn_stage(nc, m, l, q, z, g, vtm, out, psum, io, sm):
    n2 = H * T
    with ExitStack() as ctx, stage(nc, "masks_in", "dve_step", "sig_done", "f_ready", "log_done", "exp_in", "exp_done",
                                   "mix_ready", "mm_done", "level_taken", "inter_ready", "inter_mm", "inter_copied",
                                   "o_mm", "o_copied", "sq_done", "ss_mm", "root_in", "root_done", "silu_done") as s:
        sb = lambda n, sh, dt=F32: ctx.enter_context(buffer(nc, n, sh, dt))
        masks = sb("masks", [P, len(LEVELS) + 1, P], I32)
        lb, om = sb("lb", [P, H]), sb("om", [P, H])
        sg, k, b, reset = sb("sg", [P, H, T]), sb("kk", [P, H, T]), sb("bb", [P, H, T]), sb("reset", [P, H, T])
        dlt = [reset, sb("dlt", [P, H, T])]
        mix = [sb("mix0", [P, H, T]), sb("mix1", [P, H, T])]
        att = sb("att", [P, H, T])
        near = sb("near", [P, H, 2, P])
        far = sb("far", [P, H, 2, 2 * P])
        qfar, k0far, eb = sb("qfar", [P, H, 2 * P]), sb("k0far", [P, H, P]), sb("eb", [P, H, TB])
        f2 = lambda t: t[:].rearrange("p h t -> p (h t)")
        NL = len(LEVELS)
        with nc.Block() as block:
            @block.sync
            def _(sp):
                sp.dma_start(masks[:], io["c_masks"]).then_inc(s["masks_in"], 16)

            @block.scalar
            def _(a):
                a.activation(f2(sg), f2(z), ACT.Sigmoid).then_inc(s["sig_done"], 1)
                a.activation(f2(k), f2(z), ACT.Sigmoid, scale=-1.0).then_inc(s["sig_done"], 1)
                a.wait_ge(s["f_ready"], 1)
                a.activation(f2(sg), f2(sg), ACT.Ln).then_inc(s["log_done"], 1)
                for i in range(NL):
                    a.wait_ge(s["exp_in"], i + 1)
                    a.activation(f2(dlt[i % 2]), f2(dlt[i % 2]), ACT.Exp).then_inc(s["exp_done"], 1)
                a.wait_ge(s["exp_in"], NL + 1)
                a.activation(f2(dlt[NL % 2]), f2(dlt[NL % 2]), ACT.Exp).then_inc(s["exp_done"], 1)
                a.activation(f2(b), f2(b), ACT.Exp).then_inc(s["exp_done"], 1)
                for h in range(H):
                    a.wait_ge(s["inter_mm"], 2 * h + 1)
                    a.copy(near[:, h].rearrange("p c t -> p (c t)"), psum[:, 4 + h % 2, 0:2 * P]).then_inc(s["inter_copied"], 1)
                    a.wait_ge(s["inter_mm"], 2 * h + 2)
                    a.copy(far[:, h].rearrange("p c t -> p (c t)"), psum[:, 6 + h % 2, :]).then_inc(s["inter_copied"], 1)
                for h in range(H):
                    a.wait_ge(s["o_mm"], h + 1)
                    a.mul(out[:, h, :], psum[:, h, :], float(P) ** -0.5).then_inc(s["o_copied"], 1)
                    a.wait_ge(s["o_copied"], h + 1)
                    a.activation(mix[0][:, h, :], out[:, h, :], ACT.Square).then_inc(s["sq_done"], 1)
                a.wait_ge(s["root_in"], 1)
                a.activation(f2(mix[1]), f2(mix[1]), ACT.Sqrt).then_inc(s["root_done"], 1)
                a.activation(f2(g), f2(g), ACT.Silu).then_inc(s["silu_done"], 1)

            @block.vector
            def _(v):
                st = Steps(v, s["dve_step"])
                st.link(v.tensor_copy(lb[:].rearrange("p (a h) -> p a h", a=1), m.lb_all[:, bass.ds(l, 1), :]))
                st.link(v.tensor_scalar(om[:], lb[:], -1.0, 1.0, ALU.mult, ALU.add))
                st.link(v.memset(reset[:], 1.0))
                st.link(v.memset(f2(reset)[:, 0:n2:P], 0.0))
                v.wait_ge(s["sig_done"], 2)
                for h in range(H):
                    st.then(v.tensor_scalar(sg[:, h, :], sg[:, h, :], om[:, h:h + 1], lb[:, h:h + 1], ALU.mult, ALU.add))
                    st.then(v.tensor_scalar(k[:, h, :], k[:, h, :], om[:, h:h + 1], None, ALU.mult))
                st.settle()
                v.tensor_scalar(f2(sg), f2(sg), 1e-6, 1.0, ALU.max, ALU.min).then_inc(s["f_ready"], 1)
                v.wait_ge(s["log_done"], 1)
                st.link(v.tensor_tensor_scan(f2(b), f2(reset), f2(sg), 0.0, ALU.mult, ALU.add))
                st.link(v.memset(att[:], 0.0))
                v.wait_ge(s["masks_in"], 16)

                def exponents(i, half):
                    bv = f2(b).rearrange("p (n w) -> p n w", w=2 * half)
                    dv = f2(dlt[i % 2]).rearrange("p (n w) -> p n w", w=2 * half)
                    ref = bv[:, :, half - 1:half].broadcast_to([P, n2 // (2 * half), half])
                    if i >= 2:
                        v.wait_ge(s["mix_ready"], i - 1)
                    st.then(v.tensor_tensor(dv[:, :, 0:half], ref, bv[:, :, 0:half], ALU.subtract))
                    v.tensor_tensor(dv[:, :, half:], bv[:, :, half:], ref, ALU.subtract).then_inc(s["exp_in"], 1)

                def take(i):
                    for h in range(H):
                        v.wait_ge(s["mm_done"], H * i + h + 1)
                        if i:
                            v.wait_ge(s["level_taken"], H * (i - 1) + h + 1)
                        mk = masks[:, i:i + 1, :].broadcast_to([P, TB, P])
                        v.copy_predicated(att[:, h, :].rearrange("p (c t) -> p c t", c=TB), mk,
                                          psum[:, 4 * (i % 2) + h, :].rearrange("p (c t) -> p c t", c=TB)).then_inc(s["level_taken"], 1)

                take(0)
                exponents(0, LEVELS[0])
                for i, half in enumerate(LEVELS):
                    if i + 1 < NL:
                        exponents(i + 1, LEVELS[i + 1])
                    v.wait_ge(s["exp_done"], i + 1)
                    if i >= 2:
                        v.wait_ge(s["mm_done"], H * i)
                    sh = lambda t: f2(t).rearrange("p (n w) -> p n w", w=2 * half)
                    e, mx = sh(dlt[i % 2]), sh(mix[i % 2])
                    st.link(v.tensor_tensor(mx[:, :, 0:half], sh(k)[:, :, 0:half], e[:, :, 0:half], ALU.mult))
                    v.tensor_tensor(mx[:, :, half:], sh(q)[:, :, half:], e[:, :, half:], ALU.mult).then_inc(s["mix_ready"], 1)
                    if i >= 1:
                        take(i)
                d = dlt[NL % 2]
                bv, dv = f2(b).rearrange("p (n w) -> p n w", w=P), f2(d).rearrange("p (n w) -> p n w", w=P)
                v.wait_ge(s["mix_ready"], NL - 1)
                v.tensor_tensor(dv, bv[:, :, P - 1:P].broadcast_to([P, H * TB, P]), bv, ALU.subtract).then_inc(s["exp_in"], 1)
                take(NL)
                v.wait_ge(s["exp_done"], NL + 2)
                st.then(v.tensor_copy(eb[:].rearrange("p h c -> p (h c)"), f2(b)[:, P - 1:n2:P]))
                st.settle()
                v.wait_ge(s["mm_done"], H * (NL + 1))
                st.then(v.tensor_tensor(f2(mix[0]), f2(k), f2(d), ALU.mult))
                st.link(v.tensor_tensor(f2(mix[1]), f2(q), f2(b), ALU.mult))
                for h in range(H):
                    st.then(v.tensor_scalar(k0far[:, h, :], mix[0][:, h, 0:P], eb[:, h, 1:2], None, ALU.mult))
                    st.then(v.tensor_copy(qfar[:, h, 0:P], mix[1][:, h, 2 * P:3 * P]))
                    st.then(v.tensor_scalar(qfar[:, h, P:], mix[1][:, h, 3 * P:], eb[:, h, 2:3], None, ALU.mult))
                st.settle()
                v.engine_nop().then_inc(s["inter_ready"], 1)
                v.wait_ge(s["ss_mm"], H)
                v.wait_ge(s["inter_mm"], 2 * H)
                v.tensor_scalar(f2(mix[1]), psum[:, 4:8, :].rearrange("p h t -> p (h t)"), 1.0 / P, EPS, ALU.mult, ALU.add).then_inc(s["root_in"], 1)
                v.wait_ge(s["root_done"], 1)
                st.link(v.reciprocal(f2(mix[1]), f2(mix[1])))
                st.link(v.tensor_tensor(f2(out), f2(out), f2(mix[1]), ALU.mult))
                c0 = COL["hgrn_norm"][0]
                v.wait_ge(s["silu_done"], 1)
                for h in range(H):
                    st.link(v.scalar_tensor_tensor(out[:, h, :], out[:, h, :], sm[:, c0 + h:c0 + h + 1], g[:, h, :], ALU.mult, ALU.mult))

            @block.tensor
            def _(pe):
                pe.wait_ge(s["f_ready"], 1)
                for i in range(NL + 1):
                    if i:
                        pe.wait_ge(s["mix_ready"], i)
                    for h in range(H):
                        if i >= 2:
                            pe.wait_ge(s["level_taken"], H * (i - 2) + h + 1)
                        for c in range(TB):
                            cs = slice(c * P, (c + 1) * P)
                            lhs, rhs = (k, q) if i == 0 else (mix[(i - 1) % 2], mix[(i - 1) % 2])
                            mm = nc.tensor.matmul(psum[:, 4 * (i % 2) + h, cs], lhs[:, h, cs], rhs[:, h, cs], start=True, stop=True)
                        mm.then_inc(s["mm_done"], 1)
                pe.wait_ge(s["inter_ready"], 1)
                kd, qd = mix
                pe.wait_ge(s["level_taken"], H * (NL + 1))
                for h in range(H):
                    if h >= 2:
                        pe.wait_ge(s["inter_copied"], 2 * (h - 2) + 1)
                    nb_, fb = psum[:, 4 + h % 2, :], psum[:, 6 + h % 2, :]
                    nc.tensor.matmul(nb_[:, 0:P], kd[:, h, 0:P], qd[:, h, P:2 * P], start=True, stop=True)
                    nc.tensor.matmul(nb_[:, P:2 * P], kd[:, h, 2 * P:3 * P], qd[:, h, 3 * P:], start=True, stop=True).then_inc(s["inter_mm"], 1)
                    if h >= 2:
                        pe.wait_ge(s["inter_copied"], 2 * (h - 2) + 2)
                    nc.tensor.matmul(fb[:, 0:2 * P], k0far[:, h, :], qfar[:, h, :], start=True, stop=True)
                    nc.tensor.matmul(fb[:, 2 * P:], kd[:, h, P:2 * P], qfar[:, h, :], start=True, stop=True).then_inc(s["inter_mm"], 1)
                for h in range(H):
                    pe.wait_ge(s["inter_copied"], 2 * h + 2)
                    o = psum[:, h, :]
                    vt = lambda c: vtm[:, c, h * P:(h + 1) * P]
                    prods = [(o[:, c * P:(c + 1) * P], vt(c), att[:, h, c * P:(c + 1) * P]) for c in range(TB)]
                    prods += [(o[:, P:2 * P], vt(0), near[:, h, 0, :]), (o[:, 3 * P:], vt(2), near[:, h, 1, :]),
                              (o[:, 2 * P:], vt(0), far[:, h, 0, :]), (o[:, 2 * P:], vt(1), far[:, h, 1, :])]
                    for n, (dst, lhsT, rhs) in enumerate(prods):
                        mm = nc.tensor.matmul(dst, lhsT, rhs, start=(n == 0), stop=True, skip_group_check=True)
                    mm.then_inc(s["o_mm"], 1)
                pe.wait_ge(s["inter_copied"], 2 * H)
                for h in range(H):
                    pe.wait_ge(s["sq_done"], h + 1)
                    nc.tensor.matmul(psum[:, 4 + h, :], m.ones[:], mix[0][:, h, :], start=True, stop=True).then_inc(s["ss_mm"], 1)


def retention_stage(nc, m, q, k, g, vtm, out, psum, io):
    with ExitStack() as ctx, stage(nc, "dmat_in", "dve_step", "swapped", "rope_done", "score_mm", "decayed", "o_mm", "o_copied",
                                   "mean_mm", "centred", "sq_done", "var_mm", "root_in", "root_done", "silu_done") as s:
        sb = lambda n, sh, dt=F32: ctx.enter_context(buffer(nc, n, sh, dt))
        dmat = sb("dmat", [P, H, T])
        tmp = sb("rtmp", [P, 2, T])
        att = [sb(f"ratt{i}", [P, TB, T]) for i in range(2)]
        sq, rt = sb("sq", [P, H, T]), sb("rt", [P, H, T])
        f2 = lambda t: t[:].rearrange("p h t -> p (h t)")
        rows = [(x, h) for h in range(H) for x in (q, k)]
        with nc.Block() as block:
            @block.sync
            def _(sp):
                sp.dma_start(dmat[:], io["c_dmat"]).then_inc(s["dmat_in"], 16)

            @block.tensor
            def _(pe):
                for n, (x, h) in enumerate(rows):
                    nc.tensor.matmul(psum[:, n, :], m.perm[:], x[:, h, :], start=True, stop=True).then_inc(s["swapped"], 1)
                for h in range(H):
                    pe.wait_ge(s["rope_done"], 2 * h + 2)
                    for c in range(TB):
                        n = H * h + c
                        if n >= 4:
                            pe.wait_ge(s["decayed"], n - 3)
                        else:
                            pe.wait_ge(s["rope_done"], n + 1)
                        nc.tensor.matmul(psum[:, n % 4, 0:T - c * P], k[:, h, c * P:(c + 1) * P], q[:, h, c * P:], start=True, stop=True).then_inc(s["score_mm"], 1)
                    if h == 0:
                        pe.wait_ge(s["rope_done"], 2 * H)
                    pe.wait_ge(s["decayed"], TB * (h + 1))
                    for c in range(TB):
                        mm = nc.tensor.matmul(psum[:, 4 + h, c * P:], vtm[:, c, h * P:(h + 1) * P], att[h % 2][:, c, 0:T - c * P],
                                              start=(c == 0), stop=True, skip_group_check=True)
                    mm.then_inc(s["o_mm"], 1)
                for h in range(H):
                    pe.wait_ge(s["o_copied"], h + 1)
                    nc.tensor.matmul(psum[:, h, :], m.ones[:], out[:, h, :], start=True, stop=True).then_inc(s["mean_mm"], 1)
                for h in range(H):
                    pe.wait_ge(s["sq_done"], h + 1)
                    nc.tensor.matmul(psum[:, 4 + h, :], m.ones[:], sq[:, h, :], start=True, stop=True).then_inc(s["var_mm"], 1)

            @block.scalar
            def _(a):
                for h in range(H):
                    a.wait_ge(s["o_mm"], h + 1)
                    a.copy(out[:, h, :], psum[:, 4 + h, :]).then_inc(s["o_copied"], 1)
                for h in range(H):
                    a.wait_ge(s["centred"], h + 1)
                    a.activation(sq[:, h, :], out[:, h, :], ACT.Square).then_inc(s["sq_done"], 1)
                a.wait_ge(s["root_in"], 1)
                a.activation(f2(rt), f2(rt), ACT.Sqrt).then_inc(s["root_done"], 1)
                a.activation(f2(g), f2(g), ACT.Silu).then_inc(s["silu_done"], 1)

            @block.vector
            def _(v):
                st = Steps(v, s["dve_step"])
                for n, (x, h) in enumerate(rows):
                    v.wait_ge(s["swapped"], n + 1)
                    st.then(v.tensor_tensor(tmp[:, n % 2, :], psum[:, n, :], m.sin[:], ALU.mult))
                    st.link(v.tensor_tensor(x[:, h, :], x[:, h, :], m.cos[:], ALU.mult))
                    v.tensor_tensor(x[:, h, :], x[:, h, :], tmp[:, n % 2, :], ALU.add).then_inc(s["rope_done"], 1)
                v.wait_ge(s["dmat_in"], 16)
                for h in range(H):
                    for c in range(TB):
                        v.wait_ge(s["score_mm"], H * h + c + 1)
                        if h >= 2:
                            v.wait_ge(s["o_mm"], h - 1)
                        w = T - c * P
                        v.tensor_tensor(att[h % 2][:, c, 0:w], psum[:, (H * h + c) % 4, 0:w], dmat[:, h, 0:w], ALU.mult).then_inc(s["decayed"], 1)
                for h in range(H):
                    v.wait_ge(s["mean_mm"], h + 1)
                    v.scalar_tensor_tensor(out[:, h, :], psum[:, h, :], -1.0 / P, out[:, h, :], ALU.mult, ALU.add).then_inc(s["centred"], 1)
                v.wait_ge(s["var_mm"], H)
                v.tensor_scalar(f2(rt), psum[:, 4:8, :].rearrange("p h t -> p (h t)"), 1.0 / P, EPS, ALU.mult, ALU.add).then_inc(s["root_in"], 1)
                v.wait_ge(s["root_done"], 1)
                st.link(v.reciprocal(f2(rt), f2(rt)))
                st.link(v.tensor_tensor(f2(out), f2(out), f2(rt), ALU.mult))
                v.wait_ge(s["silu_done"], 1)
                st.link(v.tensor_tensor(f2(out), f2(out), f2(g), ALU.mult))


def ssm_tables_stage(nc, m, io, l, sm, tabs):
    with ExitStack() as ctx, stage(nc, "bc_in", "dve_step", "dt_in", "exp_in", "exp_done", "sin_in", "sin_done", "tab_in", "tab_done") as s:
        sb = lambda n, sh, dt=F32: ctx.enter_context(buffer(nc, n, sh, dt))
        bc = sb("bc", [P, 4, G5, C5])
        nvec = sb("nvec", [P, N5])
        t = sb("t5", [P, 24, G5])
        pr, pi = sb("pr", [P, J5 + 1, G5]), sb("pi", [P, J5 + 1, G5])
        zr, zi = sb("zr", [P, J5, G5]), sb("zi", [P, J5, G5])
        big = sb("big5", [P, G5, J5, C5])
        col = lambda n: sm[:, COL[n][0]:COL[n][1]]
        sgn = m.cols[:, 1:2]
        nsgn = m.cols[:, 2:3]
        lr, li, dt, th, th8, red, cred, mag, are, aim, den, tmp, r8, fhi, flo, u1, u2, cth, zre, zim = (t[:, i, :] for i in range(20))
        with nc.Block() as block:
            @block.sync
            def _(sp):
                sp.dma_start(bc[:].rearrange("p a g c -> p (a g c)"), tile_at(io["s5_bc"], l)).then_inc(s["bc_in"], 16)
                sp.dma_start(nvec[:], io["c_nvec"]).then_inc(s["bc_in"], 16)

            @block.scalar
            def _(a):
                a.activation(dt, col("log_step"), ACT.Exp).then_inc(s["dt_in"], 1)
                a.wait_ge(s["exp_in"], 1)
                a.activation(mag, u1, ACT.Exp).then_inc(s["exp_done"], 1)
                a.activation(r8, u1, ACT.Exp, scale=float(J5)).then_inc(s["exp_done"], 1)
                a.wait_ge(s["sin_in"], 1)
                a.activation(aim, red, ACT.Sin).then_inc(s["sin_done"], 1)
                a.activation(are, cred, ACT.Sin).then_inc(s["sin_done"], 1)
                a.wait_ge(s["tab_in"], 1)
                a.activation(tabs.sin[:], tabs.sin[:], ACT.Sin, scale=TWO_PI).then_inc(s["tab_done"], 1)
                a.activation(tabs.cos[:], tabs.cos[:], ACT.Sin, scale=TWO_PI).then_inc(s["tab_done"], 1)

            @block.vector
            def _(v):
                st = Steps(v, s["dve_step"])
                tt = lambda o, x, y, op: st.link(v.tensor_tensor(o, x, y, op))
                ts = lambda o, x, c, d, op, op2=ALU.bypass: st.link(v.tensor_scalar(o, x, c, d, op, op2))
                v.wait_ge(s["dt_in"], 1)
                ts(lr, col("lam_re"), -1e-4, None, ALU.min)
                tt(u1, lr, dt, ALU.mult)
                v.engine_nop().then_inc(s["exp_in"], 1)
                tt(th, col("lam_im"), dt, ALU.mult)
                reduce_angle(v, st, red, th, tmp)
                cos_argument(v, st, cred, red, tmp)
                v.engine_nop().then_inc(s["sin_in"], 1)
                ts(th8, red, float(J5), None, ALU.mult)
                reduce_angle(v, st, u2, th8, tmp)
                ts(u2, u2, 1.0 / TWO_PI, None, ALU.mult)
                ts(fhi, u2, ROUND13, None, ALU.add)
                ts(fhi, fhi, -ROUND13, None, ALU.add)
                tt(flo, u2, fhi, ALU.subtract)
                v.wait_ge(s["bc_in"], 32)
                gn = [P, G5, N5]
                per_g = lambda x: x.rearrange("p (g n) -> p g n", n=1).broadcast_to(gn)
                per_n = nvec[:].rearrange("p (g n) -> p g n", g=1).broadcast_to(gn)
                s3 = tabs.sin[:].rearrange("p (g n) -> p g n", n=N5)
                c3 = tabs.cos[:].rearrange("p (g n) -> p g n", n=N5)
                d3 = tabs.decay[:].rearrange("p (g n) -> p g n", n=N5)
                st.link(v.tensor_tensor(s3, per_g(fhi), per_n, ALU.mult))
                st.link(v.tensor_scalar(tabs.cos[:], tabs.sin[:], ROUND, None, ALU.add))
                st.link(v.tensor_scalar(tabs.cos[:], tabs.cos[:], -ROUND, None, ALU.add))
                st.link(v.tensor_tensor(s3, s3, c3, ALU.subtract))
                st.link(v.tensor_tensor(c3, per_g(flo), per_n, ALU.mult))
                st.link(v.tensor_tensor(s3, s3, c3, ALU.add))
                st.link(v.tensor_scalar(tabs.cos[:], tabs.sin[:], 0.25, None, ALU.add))
                st.link(v.tensor_scalar(tabs.decay[:], tabs.cos[:], 0.5, -1.0, ALU.is_gt, ALU.mult))
                st.link(v.tensor_tensor(tabs.cos[:], tabs.cos[:], tabs.decay[:], ALU.add))
                for x in (tabs.sin, tabs.cos):
                    st.link(v.tensor_scalar(x[:], x[:], 0.4999999, -0.4999999, ALU.min, ALU.max))
                v.engine_nop().then_inc(s["tab_in"], 1)
                v.wait_ge(s["exp_done"], 2)
                st.link(v.tensor_copy(d3, per_g(r8)))
                st.link(v.memset(tabs.decay[:, 0:G5 * N5:N5], 0.0))
                v.wait_ge(s["sin_done"], 2)
                tt(are, are, mag, ALU.mult)
                tt(aim, aim, mag, ALU.mult)
                tt(den, lr, lr, ALU.mult)
                tt(tmp, col("lam_im"), col("lam_im"), ALU.mult)
                tt(den, den, tmp, ALU.add)
                st.link(v.reciprocal(den, den))
                ts(u1, are, -1.0, None, ALU.add)
                tt(zre, u1, lr, ALU.mult)
                tt(tmp, aim, col("lam_im"), ALU.mult)
                tt(zre, zre, tmp, ALU.add)
                tt(zim, aim, lr, ALU.mult)
                tt(tmp, u1, col("lam_im"), ALU.mult)
                tt(zim, zim, tmp, ALU.subtract)
                tt(zre, zre, den, ALU.mult)
                tt(zim, zim, den, ALU.mult)
                st.link(v.memset(pr[:, 0, :], 1.0))
                st.link(v.memset(pi[:, 0, :], 0.0))
                st.link(v.tensor_copy(pr[:, 1, :], are))
                st.link(v.tensor_copy(pi[:, 1, :], aim))

                def product(ore, oim, xre, xim, yre, yim, w):
                    wide = t[:, 20:20 + w, :]
                    tt(ore, xre, yre, ALU.mult)
                    tt(wide, xim, yim, ALU.mult)
                    tt(ore, ore, wide, ALU.subtract)
                    tt(oim, xre, yim, ALU.mult)
                    tt(wide, xim, yre, ALU.mult)
                    tt(oim, oim, wide, ALU.add)

                for k in (1, 2, 4):
                    y = lambda z: z[:, k:k + 1, :].broadcast_to([P, k, G5])
                    product(pr[:, k + 1:2 * k + 1, :], pi[:, k + 1:2 * k + 1, :], pr[:, 1:k + 1, :], pi[:, 1:k + 1, :], y(pr), y(pi), k)
                for k in range(J5):
                    product(zr[:, J5 - 1 - k:J5 - k, :], zi[:, J5 - 1 - k:J5 - k, :], pr[:, k:k + 1, :], pi[:, k:k + 1, :],
                            t[:, 18:19, :], t[:, 19:20, :], 1)
                fl = lambda i: bc[:, i].rearrange("p g c -> p (g c)")
                st.link(v.tensor_scalar(fl(1), fl(1), sgn, None, ALU.mult))
                st.link(v.tensor_scalar(fl(2), fl(2), nsgn, None, ALU.mult))
                st.link(v.tensor_scalar(fl(3), fl(3), -1.0, None, ALU.mult))
                gjc = [P, G5, J5, C5]
                coef = lambda x: x.rearrange("p (j c) g -> p g j c", c=1).broadcast_to(gjc)
                base = lambda i: bc[:, i].rearrange("p g (j c) -> p g j c", j=1).broadcast_to(gjc)
                st.then(v.memset(tabs.gb[:, :, J5:, :], 0.0))
                for dst, cr, ci, i in ((tabs.gb[:, :, 0:J5, :], zr[:], zi[:], 0), (tabs.pc[:], pr[:, 1:, :], pi[:, 1:, :], 2)):
                    st.then(v.tensor_tensor(dst, base(i), coef(cr), ALU.mult))
                    st.link(v.tensor_tensor(big[:], base(i + 1), coef(ci), ALU.mult))
                    st.link(v.tensor_tensor(dst, dst, big[:], ALU.add))
                v.tensor_copy(tabs.c1[:], bc[:, 2]).then_inc(s["dve_step"], 1)
                v.wait_ge(s["tab_done"], 2)
                v.tensor_scalar(tabs.sin[:], tabs.sin[:], nsgn, None, ALU.mult).then_inc(s["dve_step"], 1)


def ssm_stage(nc, m, io, sm, tabs, utm, out_tm, work, rows, psum):
    with ExitStack() as ctx, stage(nc, "u_out", "u_in", "u_sorted", "dve_step", "toep_mm", "toep_copied", "turn_mm", "turn_copied", "w_mm", "w_copied",
                                   "inj_mm", "inj_turned", "scanned", "swap_mm", "states_in", "y_mm", "y_taken", "y_done", "yt_mm", "yt_copied",
                                   "y_out", "y_in") as s:
        sb = lambda n, sh, dt=F32: ctx.enter_context(buffer(nc, n, sh, dt))
        u64 = sb("u64", [N5, J5, W])
        y64 = u64
        ug = rows.rearrange("n a f -> n (a f)").rearrange("n (g j c) -> n g j c", g=G5, j=J5)
        uc = sb("uc", [P, G5, N5])
        toep = [sb(f"toep{i}", [P, J5, C5]) for i in range(2)]
        wmat = [sb(f"wmat{i}", [P, 2, P]) for i in range(2)]
        om_, yb, st_ = (x.rearrange("p a t -> p (a t)").rearrange("p (g n) -> p g n", n=N5) for x in work)
        f2 = lambda t: t[:].rearrange("p g n -> p (g n)")
        PER = 8
        with nc.Block() as block:
            @block.sync
            def _(sp):
                sp.dma_start(io["u_scratch"].rearrange("(b p) f -> p b f", p=P), utm).then_inc(s["u_out"], 16)
                sp.wait_ge(s["u_out"], 16)
                sp.dma_start(u64[:], io["u_scratch"].rearrange("(n j) f -> n j f", j=J5)).then_inc(s["u_in"], 16)
                sp.wait_ge(s["yt_copied"], G5 // 4)
                sp.dma_start(io["y_scratch"].rearrange("(n j) f -> n j f", j=J5), y64[:]).then_inc(s["y_out"], 16)
                sp.wait_ge(s["y_out"], 16)
                sp.dma_start(out_tm, io["y_scratch"].rearrange("(b p) f -> p b f", p=P)).then_inc(s["y_in"], 16)
                sp.wait_ge(s["y_in"], 16)

            @block.tensor
            def _(pe):
                pe.wait_ge(s["u_sorted"], 1)
                for g in range(G5):
                    mm = nc.tensor.transpose(psum[:, g // PER, (g % PER) * N5:(g % PER + 1) * N5],
                                             ug[:, g].rearrange("n j c -> n (j c)"), m.ident[0:N5, 0:N5])
                    if g % PER == PER - 1:
                        mm.then_inc(s["turn_mm"], 1)
                for g in range(G5):
                    b = g % 2
                    if g < 2:
                        pe.wait_ge(s["turn_copied"], G5 // PER)
                    else:
                        pe.wait_ge(s["w_copied"], g - 1)
                    wp = psum[:, 6 + b, 0:2 * P]
                    nc.tensor.transpose(wp[:, 0:P], tabs.gb[:, g, 0:J5, :].rearrange("p j c -> p (j c)"), m.ident[:])
                    nc.tensor.matmul(wp[:, P:], tabs.gb[:, g, 0:J5, :].rearrange("p j c -> p (j c)"), m.perm[:], start=True, stop=True).then_inc(s["w_mm"], 1)
                    pe.wait_ge(s["w_copied"], g + 1)
                    if g % 4 == 0 and g >= 8:
                        pe.wait_ge(s["inj_turned"], g // 4 - 1)
                    cols = slice((g % 4) * N5, (g % 4 + 1) * N5)
                    nc.tensor.matmul(psum[:, 0 + (g // 4) % 2, cols], wmat[b][:, 0, :], uc[:, g, :], start=True, stop=True)
                    nc.tensor.matmul(psum[:, 2 + (g // 4) % 2, cols], wmat[b][:, 1, :], uc[:, g, :], start=True, stop=True).then_inc(s["inj_mm"], 1)
                pe.wait_ge(s["scanned"], 1)
                for c in range(4):
                    if c == 0:
                        pe.wait_ge(s["inj_turned"], G5 // 4)
                    nc.tensor.matmul(psum[:, c, :], m.perm[:], f2(om_)[:, c * 512:(c + 1) * 512], start=True, stop=True).then_inc(s["swap_mm"], 1)
                for g in range(G5):
                    b = g % 2
                    if g >= 2:
                        pe.wait_ge(s["toep_copied"], g - 1)
                    for j in range(J5):
                        mm = nc.tensor.matmul(psum[:, 6 + b, j * C5:(j + 1) * C5], tabs.gb[:, g, J5 - 1 - j:2 * J5 - 1 - j, :].rearrange("p j c -> p (j c)"),
                                              tabs.c1[:, g, :], start=True, stop=True)
                    mm.then_inc(s["toep_mm"], 1)
                    pe.wait_ge(s["toep_copied"], g + 1)
                    if g == 0:
                        pe.wait_ge(s["states_in"], 1)
                    if g % PER == 0 and g >= 2 * PER:
                        pe.wait_ge(s["y_taken"], g // PER - 1)
                    yp = psum[:, 4 + (g // PER) % 2, (g % PER) * N5:(g % PER + 1) * N5]
                    nc.tensor.matmul(yp, toep[b][:].rearrange("p j c -> p (j c)"), uc[:, g, :], start=True, stop=True, skip_group_check=True)
                    nc.tensor.matmul(yp[:, 1:], tabs.pc[:, g].rearrange("p j c -> p (j c)"), st_[:, g, 0:N5 - 1], start=False, stop=True, skip_group_check=True).then_inc(s["y_mm"], 1)
                for g in range(G5):
                    k = g // 4
                    pe.wait_ge(s["y_done"], g // PER + 1)
                    if k >= 4:
                        pe.wait_ge(s["yt_copied"], k - 3)
                    mm = nc.tensor.transpose(psum[0:N5, k % 4, (g % 4) * P:(g % 4 + 1) * P], yb[:, g, :], m.ident[:])
                    if g % 4 == 3:
                        mm.then_inc(s["yt_mm"], 1)

            @block.scalar
            def _(a):
                for c in range(4):
                    a.wait_ge(s["turn_mm"], c + 1)
                    a.copy(f2(uc)[:, c * 512:(c + 1) * 512], psum[:, c, :]).then_inc(s["turn_copied"], 1)
                for g in range(G5):
                    a.wait_ge(s["w_mm"], g + 1)
                    if g >= 2:
                        a.wait_ge(s["inj_mm"], g - 1)
                    a.copy(wmat[g % 2][:].rearrange("p a k -> p (a k)"), psum[:, 6 + g % 2, 0:2 * P]).then_inc(s["w_copied"], 1)
                for g in range(G5):
                    a.wait_ge(s["toep_mm"], g + 1)
                    if g >= 2:
                        a.wait_ge(s["y_mm"], g - 1)
                    a.copy(toep[g % 2][:].rearrange("p a k -> p (a k)"), psum[:, 6 + g % 2, 0:P]).then_inc(s["toep_copied"], 1)
                for c in range(4):
                    a.wait_ge(s["y_taken"], c + 1)
                    a.activation(f2(yb)[:, c * 512:(c + 1) * 512], f2(yb)[:, c * 512:(c + 1) * 512], ACT.Gelu_apprx_tanh).then_inc(s["y_done"], 1)
                for k in range(G5 // 4):
                    a.wait_ge(s["yt_mm"], k + 1)
                    a.copy(y64[:, :, k * 64:(k + 1) * 64].rearrange("n j (g c) -> n g j c", c=C5),
                           psum[0:N5, k % 4, :].rearrange("n (g j c) -> n g j c", g=4, j=J5)).then_inc(s["yt_copied"], 1)

            @block.vector
            def _(v):
                st = Steps(v, s["dve_step"])
                v.wait_ge(s["u_in"], 16)
                v.tensor_copy(ug, u64[:].rearrange("n j (g c) -> n g j c", c=C5)).then_inc(s["u_sorted"], 1)
                for c in range(G5 // 4):
                    v.wait_ge(s["inj_mm"], 4 * (c + 1))
                    cs = slice(c * 256, (c + 1) * 256)
                    st.then(v.tensor_tensor(f2(om_)[:, cs], psum[:, c % 2, 0:256], tabs.cos[:, cs], ALU.mult))
                    st.link(v.tensor_tensor(f2(st_)[:, cs], psum[:, 2 + c % 2, 0:256], tabs.sin[:, cs], ALU.mult))
                    v.tensor_tensor(f2(om_)[:, cs], f2(om_)[:, cs], f2(st_)[:, cs], ALU.add).then_inc(s["inj_turned"], 1)
                v.wait_ge(s["inj_turned"], G5 // 4)
                st.link(v.tensor_tensor_scan(f2(st_), tabs.decay[:], f2(om_), 0.0, ALU.mult, ALU.add))
                st.link(v.tensor_copy(f2(om_), f2(st_)))
                v.engine_nop().then_inc(s["scanned"], 1)
                st.link(v.tensor_tensor(f2(st_), f2(st_), tabs.cos[:], ALU.mult))
                for c in range(4):
                    cs = slice(c * 512, (c + 1) * 512)
                    v.wait_ge(s["swap_mm"], c + 1)
                    st.then(v.tensor_tensor(f2(yb)[:, cs], psum[:, c, :], tabs.sin[:, cs], ALU.mult))
                st.settle()
                v.tensor_tensor(f2(st_), f2(st_), f2(yb), ALU.subtract).then_inc(s["states_in"], 1)
                v.wait_ge(s["states_in"], 1)
                d3 = sm[:, COL["s5_d"][0]:COL["s5_d"][1]].rearrange("p (g n) -> p g n", n=1)
                v.wait_ge(s["swap_mm"], 4)
                st.link(v.tensor_tensor(om_[:], uc[:], d3.broadcast_to([P, G5, N5]), ALU.mult))
                for c in range(4):
                    cs = slice(c * 512, (c + 1) * 512)
                    v.wait_ge(s["y_mm"], PER * (c + 1))
                    v.tensor_tensor(f2(yb)[:, cs], psum[:, 4 + c % 2, :], f2(om_)[:, cs], ALU.add).then_inc(s["y_taken"], 1)


def turn_stage(nc, m, src, dst, psum):
    with stage(nc, "turned", "copied") as s:
        with nc.Block() as block:
            @block.tensor
            def _(pe):
                for k in range(W // P):
                    for b in range(TB):
                        mm = nc.tensor.transpose(psum[:, k, b * P:(b + 1) * P], src[:, b, k * P:(k + 1) * P], m.ident[:])
                    mm.then_inc(s["turned"], 1)

            @block.scalar
            def _(a):
                for k in range(W // P):
                    a.wait_ge(s["turned"], k + 1)
                    a.copy(dst[:, k, :], psum[:, k, :]).then_inc(s["copied"], 1)


def glu_stage(nc, io, l, y, out, sm, psum):
    with ExitStack() as ctx, stage(nc, "w_in", "mm_done", "sig_done", "out_done") as s:
        w = ctx.enter_context(buffer(nc, "wglu", [P, 4, W], F32))
        c0 = COL["b_glu"][0]
        with nc.Block() as block:
            @block.sync
            def _(sp):
                sp.dma_start(w[:].rearrange("p k n -> p (k n)"), tile_at(io["w_glu"], l)).then_inc(s["w_in"], 16)

            @block.tensor
            def _(pe):
                pe.wait_ge(s["w_in"], 16)
                for b in range(4):
                    for k in range(4):
                        mm = nc.tensor.matmul(psum[:, b, :], w[:, k, b * P:(b + 1) * P], y[:, k, :], start=(k == 0), stop=(k == 3))
                    mm.then_inc(s["mm_done"], 1)

            @block.scalar
            def _(a):
                for b in range(4):
                    a.wait_ge(s["mm_done"], b + 1)
                    a.activation(out[:, b, :], psum[:, b, :], ACT.Sigmoid, bias=sm[:, c0 + b:c0 + b + 1]).then_inc(s["sig_done"], 1)

            @block.vector
            def _(v):
                for b in range(4):
                    v.wait_ge(s["sig_done"], b + 1)
                    v.tensor_tensor(out[:, b, :], out[:, b, :], y[:, b, :], ALU.mult).then_inc(s["out_done"], 1)


def gates_stage(nc, m, io, l, hT, sm, gates, psum):
    c0 = COL["b_gate"][0]
    with ExitStack() as ctx, stage(nc, *LINEAR_SEMS) as s:
        wbufs = [ctx.enter_context(buffer(nc, f"wg{i}", [P, KD, W], F32)) for i in range(2)]
        lin = Linear(nc, s, "fm", 6, lambda t: tile_at(io["w_gate"], l * 6 + t), wbufs, hT, KD, 4, T, psum)
        with nc.Block() as block:
            block.sync(lin.sync)
            block.tensor(lin.tensor)

            @block.scalar
            def _(a):
                lin.evacuate(a, lambda t, b, bank: a.activation(
                    gates[:, bass.ds(t * 4 + b, 1), :].rearrange("p a n -> p (a n)"), bank, ACT.Sigmoid,
                    bias=sm[:, bass.ds(t * 4 + b + c0, 1)]))


def merge_stage(nc, io, l, branches, gates, merged, psum):
    with ExitStack() as ctx, stage(nc, "w_even", "w_odd", "mm_done", "weighed", "added") as s:
        wb = [ctx.enter_context(buffer(nc, f"wm{i}", [P, 4, W], F32)) for i in range(2)]
        part = ctx.enter_context(buffer(nc, "part", [P, 2, T], F32))
        ready = (s["w_even"], s["w_odd"])
        tiles = [(half, br) for half in range(2) for br in range(3)]
        with nc.Block() as block:
            @block.sync
            def _(sp):
                for t, _ in enumerate(tiles):
                    if t >= 2:
                        sp.wait_ge(s["mm_done"], 4 * (t - 1))
                    sp.dma_start(wb[t % 2][:].rearrange("p k n -> p (k n)"), tile_at(io["w_branch"], l * 6 + t)).then_inc(ready[t % 2], 16)

            @block.tensor
            def _(pe):
                for t, (half, br) in enumerate(tiles):
                    pe.wait_ge(ready[t % 2], 16 * (t // 2 + 1))
                    for b in range(4):
                        if t >= 2:
                            pe.wait_ge(s["weighed"], 4 * (t - 2) + b + 1)
                        for k in range(4):
                            mm = nc.tensor.matmul(psum[:, 4 * (t % 2) + b, :], wb[t % 2][:, k, b * P:(b + 1) * P], branches[br][:, k, :],
                                                  start=(k == 0), stop=(k == 3))
                        mm.then_inc(s["mm_done"], 1)

            @block.vector
            def _(v):
                added = 0
                for t, (half, br) in enumerate(tiles):
                    for b in range(4):
                        n = 4 * t + b
                        v.wait_ge(s["mm_done"], n + 1)
                        d = half * 4 + b
                        bank, gate = psum[:, 4 * (t % 2) + b, :], gates[:, br * KD + d, :]
                        if br == 0:
                            v.tensor_tensor(merged[:, d, :], bank, gate, ALU.mult).then_inc(s["weighed"], 1)
                        else:
                            v.tensor_tensor(part[:, b % 2, :], bank, gate, ALU.mult).then_inc(s["weighed"], 1)
                            v.wait_ge(s["weighed"], n + 1)
                            v.tensor_tensor(merged[:, d, :], merged[:, d, :], part[:, b % 2, :], ALU.add).then_inc(s["added"], 1)
                            added += 1
                            v.wait_ge(s["added"], added)


def attend_stage(nc, m, q, k, v_tm, out, psum):
    XH, XD = 4, 2
    scale = float(XD * P) ** -0.5
    with ExitStack() as ctx, stage(nc, "score_mm", "max_done", "neg_done", "exp_done", "dve_step", "p_ready", "turned", "pt_copied", "o_mm", "o_copied") as s:
        sb = lambda n, sh, dt=F32: ctx.enter_context(buffer(nc, n, sh, dt))
        pr = [sb(f"prob{i}", [P, TB, MEM]) for i in range(2)]
        pt = [sb(f"probT{i}", [P, MB, T]) for i in range(2)]
        mx, sm_, rc = sb("mx", [P, XH, TB]), sb("sme", [P, XH, TB]), sb("rc", [P, XH, TB])
        with nc.Block() as block:
            @block.tensor
            def _(pe):
                def scores(h):
                    if h >= 2:
                        pe.wait_ge(s["exp_done"], TB * (h - 1))
                    for b in range(TB):
                        for kk in range(XD):
                            mm = nc.tensor.matmul(psum[:, 2 * (h % 2) + b // 2, (b % 2) * MEM:(b % 2 + 1) * MEM],
                                                  q[:, XD * h + kk, b * P:(b + 1) * P], k[:, XD * h + kk, 0:MEM], start=(kk == 0), stop=(kk == XD - 1))
                    mm.then_inc(s["score_mm"], 1)

                scores(0)
                for h in range(XH):
                    if h + 1 < XH:
                        scores(h + 1)
                    pe.wait_ge(s["p_ready"], h + 1)
                    if h >= 1:
                        pe.wait_ge(s["pt_copied"], MB * h)
                    for j in range(MB):
                        for b in range(TB):
                            mm = nc.tensor.transpose(psum[:, 4 + j, b * P:(b + 1) * P], pr[h % 2][:, b, j * P:(j + 1) * P], m.ident[:])
                        mm.then_inc(s["turned"], 1)
                    pe.wait_ge(s["pt_copied"], MB * (h + 1))
                    for e in range(XD):
                        if h >= 1:
                            pe.wait_ge(s["o_copied"], XD * (h - 1) + e + 1)
                        for j in range(MB):
                            mm = nc.tensor.matmul(psum[:, 6 + e, :], v_tm[:, j, (XD * h + e) * P:(XD * h + e + 1) * P], pt[h % 2][:, j, :],
                                                  start=(j == 0), stop=(j == MB - 1))
                        mm.then_inc(s["o_mm"], 1)

            @block.vector
            def _(v):
                st = Steps(v, s["dve_step"])
                for h in range(XH):
                    v.wait_ge(s["score_mm"], h + 1)
                    bank = psum[:, 2 * (h % 2):2 * (h % 2) + 2, :].rearrange("p a (b n) -> p (a b) n", n=MEM)
                    st.link(v.tensor_reduce(mx[:, h, :], bank, AX, ALU.max))
                    v.tensor_scalar(mx[:, h, :], mx[:, h, :], -scale, None, ALU.mult).then_inc(s["neg_done"], 1)
                    v.wait_ge(s["exp_done"], TB * (h + 1))
                    st.link(v.reciprocal(rc[:, h, :], sm_[:, h, :]))
                    v.tensor_tensor(pr[h % 2][:], pr[h % 2][:], rc[:, h, :].rearrange("p (b n) -> p b n", n=1).broadcast_to([P, TB, MEM]), ALU.mult).then_inc(s["p_ready"], 1)

            @block.scalar
            def _(a):
                def exps(h):
                    a.wait_ge(s["neg_done"], h + 1)
                    if h >= 2:
                        a.wait_ge(s["turned"], MB * (h - 1))
                    for b in range(TB):
                        a.activation(pr[h % 2][:, b, :], psum[:, 2 * (h % 2) + b // 2, (b % 2) * MEM:(b % 2 + 1) * MEM], ACT.Exp,
                                     bias=mx[:, h, b:b + 1], scale=scale, accum_out=sm_[:, h, b:b + 1]).then_inc(s["exp_done"], 1)

                exps(0)
                for h in range(XH):
                    if h + 1 < XH:
                        exps(h + 1)
                    for j in range(MB):
                        a.wait_ge(s["turned"], MB * h + j + 1)
                        if h >= 2:
                            a.wait_ge(s["o_mm"], XD * (h - 1))
                        a.copy(pt[h % 2][:, j, :], psum[:, 4 + j, :]).then_inc(s["pt_copied"], 1)
                    for e in range(XD):
                        a.wait_ge(s["o_mm"], XD * h + e + 1)
                        a.copy(out[:, XD * h + e, :], psum[:, 6 + e, :]).then_inc(s["o_copied"], 1)


def choose_stage(nc, m, io, l, qT, lists, psum):
    with ExitStack() as ctx, stage(nc, "keys_in", "score_mm", "score_copied", "dve_step", "scored", "best_in", "exp_done", "listed", "turned", "list_copied", "gate_lo") as s:
        sb = lambda n, sh, dt=F32: ctx.enter_context(buffer(nc, n, sh, dt))
        keys = sb("keys", [P, 2 * PH, PK])
        sc = sb("sc", [P, 2 * PH, PK])
        rest = sb("rest", [P, 256])
        cand = sb("cand", [P, PH, TOPK * TOPK])
        val = sb("val", [P, 2 * PH, TOPK])
        idx, pos = sb("idx", [P, 2 * PH, TOPK], U32), sb("pos", [P, PH, TOPK], U32)
        idxf = sb("idxf", [P, PH, 2, TOPK])
        best = sb("best", [P, PH, TOPK])
        ab_i = sb("ab_i", [P, 2, SLOTS], U32)
        ab = sb("ab", [P, 2, SLOTS])
        hot = sb("hot", [P, PH, TOPK, TOPK])
        i16 = sb("i16", [P, TOPK])
        den = sb("den", [P, PH])
        out3 = sb("out3", [P, 3, SLOTS])
        with nc.Block() as block:
            @block.sync
            def _(sp):
                sp.dma_start(keys[:].rearrange("p a k -> p (a k)"), tile_at(io["keys"], l)).then_inc(s["keys_in"], 16)
                sp.dma_start(i16[:], io["c_nvec"][:, 0:TOPK]).then_inc(s["keys_in"], 16)

            @block.tensor
            def _(pe):
                pe.wait_ge(s["keys_in"], 32)
                for tb in range(TB):
                    if tb:
                        pe.wait_ge(s["score_copied"], 4 * tb)
                    for x in range(2 * PH):
                        mm = nc.tensor.matmul(psum[:, x // 4, (x % 4) * PK:(x % 4 + 1) * PK], qT[:, x, tb * P:(tb + 1) * P], keys[:, x, :], start=True, stop=True)
                        if x % 4 == 3:
                            mm.then_inc(s["score_mm"], 1)
                    pe.wait_ge(s["listed"], tb + 1)
                    if tb:
                        pe.wait_ge(s["gate_lo"], tb)
                    for i in range(3):
                        mm = nc.tensor.transpose(psum[:, 4, i * P:(i + 1) * P], out3[:, i, :], m.ident[:])
                    mm.then_inc(s["turned"], 1)

            @block.scalar
            def _(a):
                for tb in range(TB):
                    for i in range(4):
                        a.wait_ge(s["score_mm"], 4 * tb + i + 1)
                        if tb:
                            a.wait_ge(s["scored"], tb)
                        a.copy(sc[:, 4 * i:4 * i + 4, :].rearrange("p a k -> p (a k)"), psum[:, i, :]).then_inc(s["score_copied"], 1)
                    a.wait_ge(s["best_in"], tb + 1)
                    a.activation(best[:], best[:], ACT.Exp).then_inc(s["exp_done"], 1)
                    a.wait_ge(s["turned"], tb + 1)
                    ts = slice(tb * P, (tb + 1) * P)
                    a.copy(lists[:, 0:2, ts], psum[:, 4, 0:2 * P].rearrange("p (a t) -> p a t", a=2)).then_inc(s["list_copied"], 1)
                    a.mul(lists[:, 2, ts], psum[:, 4, 2 * P:3 * P], GSCALE).then_inc(s["list_copied"], 1)

            @block.vector
            def _(v):
                st = Steps(v, s["dve_step"])

                def top16(values, index, src, n):
                    st.link(v.max(values[:, 0:8], src))
                    st.then(v.max_index(index[:, 0:8], values[:, 0:8], src))
                    st.link(v.match_replace(rest[:, 0:n], values[:, 0:8], src, -3.0e38))
                    st.link(v.max(values[:, 8:16], rest[:, 0:n]))
                    st.link(v.max_index(index[:, 8:16], values[:, 8:16], rest[:, 0:n]))

                hkk = [P, PH, TOPK, TOPK]
                for tb in range(TB):
                    for x in range(2 * PH):
                        v.wait_ge(s["score_copied"], 4 * tb + x // 4 + 1)
                        top16(val[:, x, :], idx[:, x, :], sc[:, x, :], PK)
                    v.engine_nop().then_inc(s["scored"], 1)
                    c4 = cand[:].rearrange("p h (a b) -> p h a b", b=TOPK)
                    v4 = val[:].rearrange("p (h s) k -> p h s k", s=2)
                    left = v4[:, :, 0, :].rearrange("p h (a b) -> p h a b", b=1).broadcast_to(hkk)
                    right = v4[:, :, 1, :].rearrange("p h (a b) -> p h a b", a=1).broadcast_to(hkk)
                    st.then(v.tensor_copy(idxf[:].rearrange("p h s k -> p (h s) k"), idx[:]))
                    st.link(v.tensor_tensor(c4, left, right, ALU.add))
                    for h in range(PH):
                        top16(best[:, h, :], pos[:, h, :], cand[:, h, :], TOPK * TOPK)
                    fp = pos[:].rearrange("p h k -> p (h k)")
                    st.then(v.tensor_scalar(ab_i[:, 0, :], fp, 4, None, ALU.logical_shift_right))
                    st.link(v.tensor_scalar(ab_i[:, 1, :], fp, TOPK - 1, None, ALU.bitwise_and))
                    st.then(v.tensor_copy(ab[:], ab_i[:]))
                    st.link(v.tensor_copy(den[:], best[:, :, 0]))
                    v.tensor_tensor(best[:], best[:], den[:].rearrange("p (h k) -> p h k", k=1).broadcast_to([P, PH, TOPK]), ALU.subtract).then_inc(s["best_in"], 1)
                    if tb:
                        v.wait_ge(s["turned"], tb)
                    for i in range(2):
                        want = ab[:, i, :].rearrange("p (h k c) -> p h k c", h=PH, c=1).broadcast_to(hkk)
                        have = i16[:].rearrange("p (h k c) -> p h k c", h=1, k=1).broadcast_to(hkk)
                        index = idxf[:, :, i, :].rearrange("p h (k c) -> p h k c", k=1).broadcast_to(hkk)
                        st.link(v.tensor_tensor(hot[:], want, have, ALU.is_equal))
                        st.link(v.tensor_tensor(hot[:], hot[:], index, ALU.mult))
                        st.link(v.tensor_reduce(out3[:, i, :].rearrange("p (h k) -> p h k", h=PH), hot[:], AX, ALU.add))
                    v.wait_ge(s["exp_done"], tb + 1)
                    st.link(v.tensor_reduce(den[:], best[:], AX, ALU.add))
                    st.link(v.reciprocal(den[:], den[:]))
                    v.tensor_tensor(out3[:, 2, :].rearrange("p (h k) -> p h k", h=PH), best[:],
                                    den[:].rearrange("p (h k) -> p h k", k=1).broadcast_to([P, PH, TOPK]), ALU.mult).then_inc(s["listed"], 1)
                    v.wait_ge(s["list_copied"], 2 * tb + 2)
                    ts = slice(tb * P, (tb + 1) * P)
                    v.scalar_tensor_tensor(lists[:, 3, ts], psum[:, 4, 2 * P:3 * P], GSCALE, lists[:, 2, ts], ALU.mult, ALU.subtract).then_inc(s["gate_lo"], 1)


def expert_gates_stage(nc, m, io, lists, psum):
    BT = 16
    SPC = GCH // BT
    with ExitStack() as ctx, stage(nc, "iota_in", "iota_made", "hot", "weighed", "gate_mm", "gate_copied", "gate_out0", "gate_out1") as s:
        sb = lambda n, sh, dt=F16: ctx.enter_context(buffer(nc, n, sh, dt))
        iota = sb("iota", [P, P], F32)
        ids = sb("ids", [P, P, BT])
        hot_j = [sb(f"hot_j{i}", [P, P, BT]) for i in range(2)]
        hot_i = [sb(f"hot_i{i}", [P, P, BT]) for i in range(2)]
        part = [sb(f"part{i}", [P, 2, P, BT]) for i in range(2)]
        held = [sb(f"held{i}", [P, P, GCH], F32) for i in range(2)]
        out_sem = (s["gate_out0"], s["gate_out1"])
        with nc.Block() as block:
            @block.sync
            def _(sp):
                sp.dma_start(iota[:], io["c_iota"]).then_inc(s["iota_in"], 16)

                def store(c, p, first):
                    sp.wait_ge(s["gate_copied"], (c + 1) * SPC)
                    sp.dma_start(tile_at(io["g_scratch"], c), held[p][:].rearrange("p i t -> p (i t)")).then_inc(out_sem[p], 16)
                over_pairs(sp, T // GCH, store)
                for q in out_sem:
                    sp.wait_ge(q, 16 * (T // GCH // 2))

            @block.vector
            def _(v):
                v.wait_ge(s["iota_in"], 16)
                v.tensor_copy(ids[:], iota[:].rearrange("p (i t) -> p i t", t=1).broadcast_to([P, P, BT])).then_inc(s["iota_made"], 1)
                v.wait_ge(s["iota_made"], 1)

                def make(c, p, first):
                    for k in range(SPC):
                        n, b = c * SPC + k, k % 2
                        if not (first and p == 0 and k < 2):
                            v.wait_ge(s["gate_mm"], n - 1)
                        row = lambda x: lists[:, x:x + 1, bass.ds(c * GCH + k * BT, BT)].broadcast_to([P, P, BT])
                        v.tensor_tensor(hot_i[b][:], ids[:], row(0), ALU.is_equal).then_inc(s["hot"], 1)
                        v.tensor_tensor(hot_j[b][:], ids[:], row(1), ALU.is_equal).then_inc(s["hot"], 1)
                        v.wait_ge(s["hot"], n * 2 + 2)
                        for x in range(2):
                            v.tensor_tensor(part[b][:, x], hot_i[b][:], row(2 + x), ALU.mult).then_inc(s["weighed"], 1)
                over_pairs(v, T // GCH, make)

            @block.tensor
            def _(pe):
                def products(c, p, first):
                    for k in range(SPC):
                        n, b = c * SPC + k, k % 2
                        pe.wait_ge(s["weighed"], n * 2 + 2)
                        if not (first and p == 0 and k < 2):
                            pe.wait_ge(s["gate_copied"], n - 1)
                        for t in range(BT):
                            for x in range(2):
                                mm = nc.tensor.matmul(psum[:, 4 * b + t // 4, (t % 4) * P:(t % 4 + 1) * P], hot_j[b][:, :, t], part[b][:, x, :, t],
                                                      start=(x == 0), stop=(x == 1))
                        mm.then_inc(s["gate_mm"], 1)
                over_pairs(pe, T // GCH, products)

            @block.scalar
            def _(a):
                def copy(c, p, first):
                    if not first:
                        a.wait_ge(out_sem[p], (c - p) * 8)
                    for k in range(SPC):
                        n, b = c * SPC + k, k % 2
                        a.wait_ge(s["gate_mm"], n + 1)
                        a.activation(held[p][:, :, k * BT:(k + 1) * BT].rearrange("p i t -> p t i"),
                                     psum[:, 4 * b:4 * b + 4, :].rearrange("p a (t i) -> p (a t) i", i=P), ACT.Copy, scale=1.0 / GSCALE).then_inc(s["gate_copied"], 1)
                over_pairs(a, T // GCH, copy)


def split_stage(nc, src, hi, lo):
    with stage(nc, "hi_done", "lo_done") as s:
        with nc.Block() as block:
            @block.scalar
            def _(a):
                for k in range(KD):
                    a.copy(hi[:, k, :], src[:, k, :]).then_inc(s["hi_done"], 1)

            @block.vector
            def _(v):
                for k in range(KD):
                    v.wait_ge(s["hi_done"], k + 1)
                    v.tensor_tensor(lo[:, k, :], src[:, k, :], hi[:, k, :].bitcast(F32), ALU.subtract).then_inc(s["lo_done"], 1)


def experts_stage(nc, m, io, l, h_hi, h_lo, psum):
    NG = PK // GE
    with ExitStack() as ctx, stage(nc, "u_in0", "u_in1", "v_in0", "v_in1", "g_in0", "g_in1", "u_hi", "u_lo", "v_hi", "v_lo",
                                   "dot_mm", "gelu_done", "gated", "act_hi", "act_lo", "y_mm", "y_added") as s:
        sb = lambda n, sh, dt=F32: ctx.enter_context(buffer(nc, n, sh, dt))
        u = [sb(f"u{i}", [P, D]) for i in range(2)]
        uh = [sb(f"uh{i}", [P, KD, P], F32R) for i in range(2)]
        ul = [sb(f"ul{i}", [P, KD, P], F32R) for i in range(2)]
        vv = [sb(f"v{i}", [P, D]) for i in range(2)]
        vh = [sb(f"vh{i}", [P, GE, D], F32R) for i in range(2)]
        vl = [sb(f"vl{i}", [P, GE, D], F32R) for i in range(2)]
        ah = [sb(f"ah{i}", [P, GE, T], F32R) for i in range(2)]
        al = [sb(f"al{i}", [P, GE, T], F32R) for i in range(2)]
        ge = [sb(f"ge{i}", [P, T]) for i in range(2)]
        gate = [sb(f"gate{i}", [P, T // GCH, GE, GCH]) for i in range(2)]
        u_in, v_in, g_in = (s["u_in0"], s["u_in1"]), (s["v_in0"], s["v_in1"]), (s["g_in0"], s["g_in1"])
        row0 = l * PK
        fw = lambda t: t[:].rearrange("p k e -> p (k e)")
        flat = lambda t, r: t[:, r, :]
        with nc.Block() as block:
            @block.sync
            def _(sp):
                def load_u(n, early, par):
                    if not early:
                        sp.wait_ge(s["u_lo"], n - 1)
                    sp.dma_start(u[par][:], tile_at(io["peer_u"], row0 + n)).then_inc(u_in[par], 16)

                def load(g, p, first, last):
                    if first and p == 0:
                        load_u(0, True, 0)
                    if not first:
                        sp.wait_ge(s["gated"], (g - 1) * GE)
                    sp.dma_start(gate[p][:].rearrange("p c r t -> p c (r t)"),
                                 io["g_scratch"].rearrange("c p (i t) -> p c i t", t=GCH)[:, :, bass.ds(g * GE, GE), :].rearrange("p c i t -> p c (i t)")
                                 ).then_inc(g_in[p], 16)
                    for r in range(GE):
                        n = g * GE + r
                        if not (last and r == GE - 1):
                            load_u(n + 1, first and p == 0 and r == 0, (r + 1) % 2)
                        if not (first and p == 0 and r < 2):
                            sp.wait_ge(s["v_lo"], n - 1)
                        sp.dma_start(vv[r % 2][:], tile_at(io["peer_v"], row0 + n)).then_inc(v_in[r % 2], 16)
                over_groups(sp, NG, load)

            @block.tensor
            def _(pe):
                def dots(g, p, first):
                    for r in range(GE):
                        n = g * GE + r
                        pe.wait_ge(s["u_lo"], n + 1)
                        if not (first and p == 0):
                            pe.wait_ge(s["gelu_done"], n - 3)
                        three = [(uh, h_lo), (ul, h_hi), (uh, h_hi)]
                        for x, (w, h) in enumerate(three):
                            for k in range(KD):
                                mm = nc.tensor.matmul(psum[:, r, :], w[r % 2][:, k, :], h[:, k, :], start=(x == 0 and k == 0), stop=(x == 2 and k == KD - 1))
                        mm.then_inc(s["dot_mm"], 1)

                def sums(g, p, early):
                    pe.wait_ge(s["v_lo"], g * GE + GE)
                    pe.wait_ge(s["act_lo"], g * GE + GE)
                    for o in range(8):
                        b, half = o // 2, o % 2
                        if not (early and o < 4):
                            pe.wait_ge(s["y_added"], g * 8 + o - 3)
                        for r in range(GE):
                            for x, (w, q) in enumerate([(ah, vl), (al, vh), (ah, vh)]):
                                mm = nc.tensor.matmul(psum[:, 4 + o % 4, :], w[p][:, r, b * P:(b + 1) * P], q[p][:, r, half * W:(half + 1) * W],
                                                      start=(r == 0 and x == 0), stop=(r == GE - 1 and x == 2))
                        mm.then_inc(s["y_mm"], 1)

                def group(g, p, first, last):
                    dots(g, p, first)
                    if not (first and p == 0):
                        sums(g - 1, 1 - p, first)
                over_groups(pe, NG, group)
                sums(NG - 1, (NG - 1) % 2, False)

            @block.scalar
            def _(a):
                def high_u(n, k, early, par):
                    a.wait_ge(u_in[par], k)
                    if not early:
                        a.wait_ge(s["dot_mm"], n - 1)
                    a.copy(fw(uh[par]), u[par][:]).then_inc(s["u_hi"], 1)

                def group(g, p, first, last):
                    if first and p == 0:
                        high_u(0, 16, True, 0)
                    for r in range(GE):
                        n = g * GE + r
                        if not (last and r == GE - 1):
                            high_u(n + 1, g * 32 + 16 * ((r + 1) // 2) + 16, first and p == 0 and r == 0, (r + 1) % 2)
                        a.wait_ge(v_in[r % 2], g * 32 + 16 * (r // 2) + 16)
                        if not first:
                            a.wait_ge(s["y_mm"], (g - 1) * 8)
                        a.copy(vh[p][:, r, :], vv[r % 2][:]).then_inc(s["v_hi"], 1)
                        a.wait_ge(s["dot_mm"], n + 1)
                        if not (first and p == 0 and r < 2):
                            a.wait_ge(s["act_lo"], n - 1)
                        a.activation(ge[r % 2][:], psum[:, r, :], ACT.Gelu_apprx_tanh).then_inc(s["gelu_done"], 1)
                        a.wait_ge(s["gated"], n + 1)
                        a.copy(ah[p][:, r, :], ge[r % 2][:]).then_inc(s["act_hi"], 1)
                over_groups(a, NG, group)

            @block.vector
            def _(v):
                def low_u(n, par):
                    v.wait_ge(s["u_hi"], n + 1)
                    v.tensor_tensor(fw(ul[par]), u[par][:], fw(uh[par]).bitcast(F32), ALU.subtract).then_inc(s["u_lo"], 1)

                def add(g, early):
                    for o in range(8):
                        b, half = o // 2, o % 2
                        v.wait_ge(s["y_mm"], g * 8 + o + 1)
                        if not early:
                            v.wait_ge(s["y_added"], (g - 1) * 8 + o + 1)
                        x = m.X[:, b, half * W:(half + 1) * W]
                        v.tensor_tensor(x, psum[:, 4 + o % 4, :], x, ALU.add).then_inc(s["y_added"], 1)

                def group(g, p, first, last):
                    if first and p == 0:
                        low_u(0, 0)
                    v.wait_ge(g_in[p], 16 if first else (g - p) * 8 + 16)
                    for r in range(GE):
                        n = g * GE + r
                        if not (last and r == GE - 1):
                            low_u(n + 1, (r + 1) % 2)
                        v.wait_ge(s["v_hi"], n + 1)
                        v.tensor_tensor(vl[p][:, r, :], vv[r % 2][:], vh[p][:, r, :].bitcast(F32), ALU.subtract).then_inc(s["v_lo"], 1)
                        v.wait_ge(s["gelu_done"], n + 1)
                        act = ge[r % 2][:].rearrange("p (c t) -> p c t", t=GCH)
                        v.tensor_tensor(act, act, gate[p][:, :, r, :], ALU.mult).then_inc(s["gated"], 1)
                        v.wait_ge(s["act_hi"], n + 1)
                        v.tensor_tensor(al[p][:, r, :], ge[r % 2][:], ah[p][:, r, :].bitcast(F32), ALU.subtract).then_inc(s["act_lo"], 1)
                    if not (first and p == 0):
                        add(g - 1, first)
                over_groups(v, NG, group)
                add(NG - 1, False)


def final_stage(nc, m, io):
    with ExitStack() as ctx, stage(nc, "gain_in", "sumsq", "dve_step", "root", "ready", "stored") as s:
        gain = ctx.enter_context(buffer(nc, "gain", [P, D], F32))
        junk = ctx.enter_context(buffer(nc, "junk", [P, D], F32))
        ss = ctx.enter_context(buffer(nc, "fss", [P, 2, TB], F32))
        with nc.Block() as block:
            @block.sync
            def _(sp):
                sp.dma_start(gain[:], io["norm_final"].partition_broadcast(P)).then_inc(s["gain_in"], 16)
                for b in range(TB):
                    sp.wait_ge(s["ready"], b + 1)
                    sp.dma_start(io["out"][b * P:(b + 1) * P, :], m.X[:, b, :]).then_inc(s["stored"], 16)
                sp.wait_ge(s["stored"], 16 * TB)

            @block.scalar
            def _(a):
                for b in range(TB):
                    if b:
                        a.wait_ge(s["sumsq"], b)
                    a.activation(junk[:], m.X[:, b, :], ACT.Square, accum_out=ss[:, 0, b:b + 1]).then_inc(s["sumsq"], 1)
                a.wait_ge(s["dve_step"], 1)
                a.activation(ss[:, 1, :], ss[:, 0, :], ACT.Sqrt).then_inc(s["root"], 1)

            @block.vector
            def _(v):
                st = Steps(v, s["dve_step"])
                v.wait_ge(s["sumsq"], TB)
                st.then(v.tensor_scalar(ss[:, 0, :], ss[:, 0, :], 1.0 / D, EPS, ALU.mult, ALU.add))
                v.wait_ge(s["root"], 1)
                v.wait_ge(s["gain_in"], 16)
                st.link(v.reciprocal(ss[:, 0, :], ss[:, 1, :]))
                for b in range(TB):
                    v.scalar_tensor_tensor(m.X[:, b, :], m.X[:, b, :], ss[:, 0, b:b + 1], gain[:], ALU.mult, ALU.mult).then_inc(s["ready"], 1)


def copy_to(a, dst):
    def copy(t, b, bank):
        n = bank.shape[-1]
        return a.copy(dst[:, bass.ds(t * 4 + b, 1), 0:n].rearrange("p a n -> p (a n)"), bank)
    return copy


def load_small_stage(nc, io, l, sm):
    with stage(nc, "small_in") as s:
        with nc.Block() as block:
            @block.sync
            def _(sp):
                sp.dma_start(sm[:], tile_at(io["small"], l)).then_inc(s["small_in"], 16)
                sp.wait_ge(s["small_in"], 16)


def mixer_layer(nc, m, io, l, sm, psum):
    a = nc.scalar
    part = lambda t, i: t[:, 4 * i:4 * i + 4, :]
    with buffer(nc, "fm", [P, 24, T], F32) as fm:
        with buffer(nc, "tm", [P, 3 * TB, W], F32) as tm:
            with buffer(nc, "hT", [P, KD, T], F32) as hT:
                norm_stage(nc, m, m.X, TB, sm[:, 0:KD], hT, psum)
                linear_stage(nc, "fm", 6, lambda t: tile_at(io["w_fm"], l * 6 + t), hT, KD, 4, T, psum, copy_to(a, fm))
                linear_stage(nc, "tm", 3, lambda t: tile_at(io["w_tm"], l * 3 + t), hT, KD, 4, T, psum, copy_to(a, tm))
            hgrn_stage(nc, m, l, part(fm, 0), part(fm, 1), part(fm, 2), part(tm, 0), part(fm, 0), psum, io, sm)
            retention_stage(nc, m, part(fm, 3), part(fm, 4), part(fm, 5), part(tm, 1), part(fm, 4), psum, io)
            with ExitStack() as ctx:
                sb = lambda n, sh: ctx.enter_context(buffer(nc, n, sh, F32))
                tabs = SsmTables(sin=sb("tsin", [P, G5 * N5]), cos=sb("tcos", [P, G5 * N5]), decay=sb("tdec", [P, G5 * N5]),
                                       gb=sb("gb", [P, G5, 2 * J5, C5]), pc=sb("pc", [P, G5, J5, C5]), c1=sb("c1", [P, G5, C5]))
                ssm_tables_stage(nc, m, io, l, sm, tabs)
                ssm_stage(nc, m, io, sm, tabs, part(tm, 2), part(tm, 0), [part(fm, i) for i in (1, 3, 5)],
                          tm[0:N5, 0:2 * TB, :], psum)
            turn_stage(nc, m, part(tm, 0), part(fm, 1), psum)
        glu_stage(nc, io, l, part(fm, 1), part(fm, 2), sm, psum)
        with buffer(nc, "merged", [P, KD, T], F32) as merged:
            with buffer(nc, "gates", [P, 3 * KD, T], F32) as gates:
                with buffer(nc, "hT", [P, KD, T], F32) as hT:
                    norm_stage(nc, m, m.X, TB, sm[:, 0:KD], hT, psum)
                    gates_stage(nc, m, io, l, hT, sm, gates, psum)
                merge_stage(nc, io, l, [part(fm, 0), part(fm, 2), part(fm, 4)], gates, merged, psum)
            residual_stage(nc, m, lambda t: tile_at(io["w_out"], l * 2 + t), merged, psum)


def residual_stage(nc, m, src, act, psum):
    v = nc.vector

    def add(t, b, bank):
        x = m.X[:, b, t * W:(t + 1) * W]
        return v.tensor_tensor(x, bank, x, ALU.add)
    linear_stage(nc, "tm", 2, src, act, KD, TB, T, psum, add, on="vector")


def cross_layer(nc, m, io, l, sm, psum):
    a = nc.scalar
    with ExitStack() as ctx:
        sb = lambda n, sh, dt=F32: ctx.enter_context(buffer(nc, n, sh, dt))
        kT = sb("kT", [P, KD, MEM])
        v_tm = sb("v_tm", [P, MB, D])
        qT = sb("qT", [P, KD, T])
        oT = sb("oT", [P, KD, T])
        c = COL["norm_mem"][0]
        with buffer(nc, "memT", [P, KD, MEM], F32) as memT, buffer(nc, "mem", [P, MB, D], F32) as mem:
            norm_stage(nc, m, mem, MB, sm[:, c:c + KD], memT, psum, load=[(mem[:], io["mem"])])
            linear_stage(nc, "fm", 2, lambda t: tile_at(io["xa_k"], l * 2 + t), memT, KD, 4, MEM, psum, copy_to(a, kT))

            def v_copy(t, b, bank):
                return a.copy(v_tm[:, b, t * W:(t + 1) * W], bank)
            linear_stage(nc, "tm", 2, lambda t: tile_at(io["xa_v"], l * 2 + t), memT, KD, MB, T, psum, v_copy, name="x")
        c = COL["norm_cross"][0]
        with buffer(nc, "hTc", [P, KD, T], F32) as hT:
            norm_stage(nc, m, m.X, TB, sm[:, c:c + KD], hT, psum)
            linear_stage(nc, "fm", 2, lambda t: tile_at(io["xa_q"], l * 2 + t), hT, KD, 4, T, psum, copy_to(a, qT))
        attend_stage(nc, m, qT, kT, v_tm, oT, psum)
        residual_stage(nc, m, lambda t: tile_at(io["xa_o"], l * 2 + t), oT, psum)


def expert_layer(nc, m, io, l, sm, psum):
    a = nc.scalar
    c = COL["norm_ffn"][0]
    with buffer(nc, "h_hi", [P, KD, T], F32R) as h_hi, buffer(nc, "h_lo", [P, KD, T], F32R) as h_lo:
        with buffer(nc, "lists", [P, 4, T], F16) as lists:
            with buffer(nc, "hT", [P, KD, T], F32) as hT:
                norm_stage(nc, m, m.X, TB, sm[:, c:c + KD], hT, psum)
                split_stage(nc, hT, h_hi, h_lo)
                with buffer(nc, "qT", [P, 2 * PH, T], F32) as qT:
                    linear_stage(nc, "fm", 4, lambda t: tile_at(io["peer_wq"], l * 4 + t), hT, KD, 4, T, psum, copy_to(a, qT))
                    choose_stage(nc, m, io, l, qT, lists, psum)
            expert_gates_stage(nc, m, io, lists, psum)
        experts_stage(nc, m, io, l, h_hi, h_lo, psum)


def trunk(nc, io):
    m = Resident()
    m.X = nc.alloc_sbuf_tensor("X", [P, TB, D], F32)
    m.ident = nc.alloc_sbuf_tensor("ident", [P, P], F32)
    m.perm = nc.alloc_sbuf_tensor("perm", [P, P], F32)
    m.ones = nc.alloc_sbuf_tensor("ones", [P, P], F32)
    m.cols = nc.alloc_sbuf_tensor("cols", [P, 3], F32)
    m.sin = nc.alloc_sbuf_tensor("sin", [P, T], F32)
    m.cos = nc.alloc_sbuf_tensor("cos", [P, T], F32)
    m.lb_all = nc.alloc_sbuf_tensor("lb_all", [P, L, H], F32)
    sm = nc.alloc_sbuf_tensor("small", [P, NSMALL], F32)
    psum = nc.alloc_psum_tensor("psum", [P, 8, 512], F32)
    _pool[:] = [nc.alloc_semaphore(f"stage_sem{i}") for i in range(28)]
    setup_stage(nc, io, m)
    with nc.Fori(0, L) as l:
        load_small_stage(nc, io, l, sm)
        mixer_layer(nc, m, io, l, sm, psum)
        cross_layer(nc, m, io, l, sm, psum)
        expert_layer(nc, m, io, l, sm, psum)
    final_stage(nc, m, io)



def _constants():
    f = np.float32
    half = P // 2
    inv = (np.float32(10000.0) ** (-np.arange(half, dtype=f) / f(half))).astype(f)
    p = np.arange(P)
    perm = np.zeros((P, P), f)
    perm[p, (p + half) % P] = 1
    sign = np.where(p < half, -1.0, 1.0).astype(f)
    s_, t_ = np.meshgrid(p, p, indexing="ij")
    masks = [s_ == t_]
    for w in LEVELS:
        masks.append((s_ // (2 * w) == t_ // (2 * w)) & (s_ % (2 * w) < w) & (t_ % (2 * w) >= w))
    masks = np.stack(masks, 1).astype(np.int32)
    rel = np.arange(T)[None, :] - p[:, None]
    log_g = np.log1p(-np.exp2(-5.0 - np.arange(H)))
    dmat = np.stack([np.where(rel >= 0, np.exp(lg * np.maximum(rel, 0)), 0.0) for lg in log_g], 1) * P ** -0.5
    return {"c_ident": np.eye(P, dtype=f), "c_perm": perm, "c_cols": np.stack([np.tile(inv, 2), sign, -sign], 1),
            "c_masks": masks, "c_dmat": dmat.astype(f), "c_nvec": np.tile(np.arange(N5, dtype=f), (P, 1)),
            "c_iota": np.tile(np.arange(P, dtype=f), (P, 1))}


def _layout(a):
    def tiles(w, order=None):
        w = w.reshape(L, -1, P, w.shape[2] // W, W).transpose(0, 3, 2, 1, 4)
        w = w if order is None else w[:, order]
        return np.ascontiguousarray(w).reshape(w.shape[0] * w.shape[1], P, -1)

    def cols(v):
        return v.reshape(L, -1, P).transpose(0, 2, 1)
    both = lambda v: np.concatenate([v, v], 1)
    lam = lambda v: both(v.transpose(0, 2, 1))
    small = np.concatenate([
        cols(a["norm_mix"]), cols(a["norm_cross"]), cols(a["norm_mem"]), cols(a["norm_ffn"]), cols(a["b_gate"]),
        cols(a["hgrn_norm"]), cols(a["s5_b_glu"]),
        np.tile(a["s5_d"].reshape(L, G5, C5).transpose(0, 2, 1), (1, J5, 1)),
        lam(a["s5_lambda_re"]), lam(a["s5_lambda_im"]), np.repeat(a["s5_log_step"][:, None, :], P, 1)], 2)
    br, bi = (a[f"s5_b_{x}"].transpose(0, 2, 1, 3) for x in ("re", "im"))
    cr, ci = (a[f"s5_c_{x}"].transpose(0, 3, 1, 2) for x in ("re", "im"))
    cat = lambda x, y: np.concatenate([x, y], 1)
    bc = np.stack([cat(br, bi), cat(bi, br), cat(cr, ci), cat(ci, cr)], 2).reshape(L, P, -1)
    w_in = a["w_in"]
    rows = lambda v: v.reshape(-1, P, v.shape[-1]).transpose(1, 0, 2)
    wbr = a["w_branch"].reshape(L, 3, 4, P, 2, W).transpose(0, 4, 1, 3, 2, 5).reshape(L * 6, P, -1)
    u = a["peer_u"].reshape(L * PK, P, KD, P).transpose(0, 3, 2, 1).reshape(L * PK, P, -1)
    return {
        "x": rows(a["x"][0]), "mem": rows(a["mem"][0]), "positions": a["positions"][0],
        "hgrn_lb": a["hgrn_lb"].reshape(L, H, P).transpose(2, 0, 1), "small": small, "s5_bc": bc,
        "w_fm": tiles(w_in[:, :, :15 * W], [0, 1, 3, 5, 6, 8]), "w_tm": tiles(w_in[:, :, :15 * W], [2, 7, 4]),
        "w_gate": tiles(w_in[:, :, 9 * W:]), "w_glu": tiles(a["s5_w_glu"]), "w_branch": wbr, "w_out": tiles(a["w_out"]),
        "xa_q": tiles(a["xa_wq"]), "xa_k": tiles(a["xa_wkv"][:, :, :D]), "xa_v": tiles(a["xa_wkv"][:, :, D:]),
        "xa_o": tiles(a["xa_wo"]), "peer_wq": tiles(a["peer_wq"]),
        "keys": a["peer_keys"].reshape(L, 2 * PH, PK, P).transpose(0, 3, 1, 2).reshape(L, P, -1),
        "peer_u": u, "peer_v": a["peer_v"].reshape(L * PK, P, D), "norm_final": a["norm_final"],
    }


def kernel(**inputs):
    import concourse.bacc as bacc
    from concourse.bass_utils import run_bass_kernel_spmd

    nc = bacc.Bacc("TRN2", target_bir_lowering=False, num_devices=1)
    arrays = {}
    laid = _layout({k: np.asarray(v) for k, v in inputs.items()})
    laid.update(_constants())
    aps = {}
    for name, a in laid.items():
        a = np.ascontiguousarray(a)
        arrays[f"in_{name}"] = a
        aps[name] = nc.dram_tensor(f"in_{name}", a.shape, mybir.dt.from_np(a.dtype), kind="ExternalInput").ap()
    aps["out"] = nc.dram_tensor("out_x", (T, D), F32, kind="ExternalOutput").ap()
    aps["u_scratch"] = nc.dram_tensor("u_scratch", (T, W), F32, kind="Internal").ap()
    aps["y_scratch"] = nc.dram_tensor("y_scratch", (T, W), F32, kind="Internal").ap()
    aps["g_scratch"] = nc.dram_tensor("g_scratch", (T // GCH, P, P * GCH), F32, kind="Internal").ap()
    trunk(nc, aps)
    r = run_bass_kernel_spmd(nc, [arrays], core_ids=[0])
    return np.asarray(r.results[0]["out_x"]).reshape(1, T, D)
```

```python
import itertools
from contextlib import ExitStack, contextmanager

import numpy as np

import concourse.bass as bass
from concourse import mybir

P = 128
D = 1024
T = 512
L = 2
TB = T // P
KD = D // P
W = 512
H = 4
MEM = 256
MB = MEM // P
EPS = 1e-6
G5, C5, S5P = 32, 16, 64
J5, N5 = 8, T // 8
PH, PK, TOPK = 8, 128, 16
SLOTS = PH * TOPK
GCH = 64
GSCALE = 4096.0
GE = 4
LEVELS = [64, 32, 16, 8, 4, 2, 1]

F32 = mybir.dt.float32
F32R = mybir.dt.float32r
F16 = mybir.dt.float16
I32 = mybir.dt.int32
U32 = mybir.dt.uint32
ALU = mybir.AluOpType
ACT = mybir.ActivationFunctionType
AX = mybir.AxisListType.X

TWO_PI = 2.0 * np.pi
C1 = 6.28125
C2 = float(np.float32(round((TWO_PI - C1) * 2**21) / 2**21))
C3 = float(np.float32(TWO_PI - C1 - C2))
ROUND = 1.5 * 2.0**23
ROUND13 = 1.5 * 2.0**10
PI_IN = 3.1415925

_SMALL = [("norm_mix", KD), ("norm_cross", KD), ("norm_mem", KD), ("norm_ffn", KD), ("b_gate", 3 * KD),
          ("hgrn_norm", H), ("b_glu", H), ("s5_d", G5), ("lam_re", G5), ("lam_im", G5), ("log_step", G5)]
COL, _n = {}, 0
for _name, _w in _SMALL:
    COL[_name] = (_n, _n + _w)
    _n += _w
NSMALL = _n


_serial = itertools.count()
_pool = []


def buffer(nc, name, shape, dtype):
    return nc.sbuf_tensor(f"{name}_{next(_serial)}", shape, dtype)


@contextmanager
def stage(nc, *names, weights=None):
    assert len(names) <= len(_pool)
    yield dict(zip(names, _pool))
    with nc.Block() as block:
        @block.sync
        def _(sp):
            sp.sem_clear(range(_pool[0].num, _pool[len(names) - 1].num + 1))
            if weights is not None:
                sp.sem_clear(range(weights.arrived[0].num, weights.arrived[1].num + 1))


class Resident:
    pass


class SsmTables:

    def __init__(self, sin, cos, decay, gb, pc):
        self.sin, self.cos, self.decay, self.gb, self.pc = sin, cos, decay, gb, pc


class Steps:

    def __init__(self, eng, sem):
        self.eng, self.sem, self.n = eng, sem, 0

    def then(self, ins):
        ins.then_inc(self.sem, 1)
        self.n += 1
        return self.n

    def settle(self):
        self.eng.wait_ge(self.sem, self.n)

    def link(self, ins):
        self.then(ins)
        self.settle()


def tile_at(dram, index):
    return dram[bass.ds(index, 1)].rearrange("a p n -> (a p) n")


def over_pairs(eng, n, body):
    for p in range(min(2, n)):
        body(p, p, True)
    pairs = n // 2
    if pairs > 1:
        with eng.Fori(1, pairs) as i:
            for p in range(2):
                body(i * 2 + p, p, False)
    if n > 2 and n % 2:
        body(n - 1, 0, False)


def over_groups(eng, n, body):
    for p in range(2):
        body(p, p, True, False)
    with eng.Fori(1, n // 2 - 1) as i:
        for p in range(2):
            body(i * 2 + p, p, False, False)
    for p in range(2):
        body(n - 2 + p, p, False, p == 1)


class Weights:

    def __init__(self, m, raw, turn, n, src):
        self.raw, self.arrived, self.n, self.src = raw, m.weights_in[turn % 2], n, src

    def load(self, sp, t, p):
        sp.dma_start(self.raw[p][:].rearrange("p k n -> p (k n)"), self.src(t)).then_inc(self.arrived[p], 16)

    def start(self, sp):
        for p in range(2):
            self.load(sp, p, p)


def two_tiles(nc, ctx):
    return [ctx.enter_context(buffer(nc, f"w{i}", [P, KD, W], F32)) for i in range(2)]


class Linear:

    def __init__(self, nc, ctx, s, kind, weights, act, nb, N, psum):
        self.nc, self.s, self.kind, self.n, self.weights = nc, s, kind, weights.n, weights
        self.act, self.nb, self.N, self.ps = act, nb, N, psum
        self.raw, self.ready = weights.raw, weights.arrived
        self.hi = [ctx.enter_context(buffer(nc, f"w_hi{i}", [P, KD * P], F32R)) for i in range(2)]
        self.lo = [ctx.enter_context(buffer(nc, f"w_lo{i}", [P, KD * P], F32R)) for i in range(2)]

    def unit_of(self, p, q):
        return self.raw[p][:, :, q * P:(q + 1) * P] if self.kind == "fm" else self.raw[p][:, 2 * q:2 * q + 2, :]

    def shaped(self, x):
        return x[:].rearrange("p (k n) -> p k n", n=P if self.kind == "fm" else W)

    def arrivals(self, t, p, first):
        return 16 if first else (t - p) * 8 + 16

    def sync(self, sp, following=None):
        def load(t, p, first):
            if not first:
                sp.wait_ge(self.s["lo_done"], (t - 1) * 4)
                self.weights.load(sp, t, p)
        over_pairs(sp, self.n, load)
        if following is not None:
            for t in (self.n, self.n + 1):
                sp.wait_ge(self.s["lo_done"], (t - 1) * 4)
                following.load(sp, t % 2, t % 2)

    def tensor(self, pe):
        def tile(t, p, first):
            for q in range(4):
                self.unit(pe, t, p, first, q)
        over_pairs(pe, self.n, tile)

    def unit(self, pe, t, p, first, q):
        matmul = self.nc.tensor.matmul
        a_hi, a_lo = self.act
        pe.wait_ge(self.s["lo_done"], t * 4 + q + 1)
        w_hi, w_lo = self.shaped(self.hi[q % 2]), self.shaped(self.lo[q % 2])
        if self.kind == "fm":
            if not (first and p == 0):
                pe.wait_ge(self.s["evac_done"], (t - 1) * 4 + q + 1)
            three = [(w_hi, a_lo), (w_lo, a_hi), (w_hi, a_hi)]
            for x, (w, a) in enumerate(three):
                for k in range(KD):
                    mm = matmul(self.ps[:, q, 0:self.N], w[:, k, :], a[:, k, 0:self.N],
                                start=(x == 0 and k == 0), stop=(x == 2 and k == KD - 1))
        else:
            three = [(w_lo, a_hi), (w_hi, a_lo), (w_hi, a_hi)]
            for b in range(self.nb):
                if q == 0 and not first:
                    pe.wait_ge(self.s["evac_done"], (t - 2) * self.nb + b + 1)
                for x, (w, a) in enumerate(three):
                    for k in range(2):
                        mm = matmul(self.ps[:, 4 * p + b, :], a[:, 2 * q + k, b * P:(b + 1) * P], w[:, k, :],
                                    start=(q == 0 and x == 0 and k == 0), stop=(q == 3 and x == 2 and k == 1))
        mm.then_inc(self.s["unit_mm"], 1)

    def high(self, a, t, p, first, q):
        if q == 0:
            a.wait_ge(self.ready[p], self.arrivals(t, p, first))
        if not (first and p == 0 and q < 2):
            a.wait_ge(self.s["unit_mm"], t * 4 + q - 1)
        a.copy(self.shaped(self.hi[q % 2]), self.unit_of(p, q)).then_inc(self.s["hi_done"], 1)

    def low(self, v, t, p, first, q):
        v.wait_ge(self.s["hi_done"], t * 4 + q + 1)
        v.tensor_tensor(self.shaped(self.lo[q % 2]), self.unit_of(p, q), self.shaped(self.hi[q % 2]).bitcast(F32),
                        ALU.subtract).then_inc(self.s["lo_done"], 1)

    def block_out(self, eng, t, p, b, copy):
        eng.wait_ge(self.s["unit_mm"], t * 4 + (b + 1 if self.kind == "fm" else 4))
        bank = b if self.kind == "fm" else 4 * p + b
        copy(t, b, self.ps[:, bank, 0:self.N]).then_inc(self.s["evac_done"], 1)

    def blocks_behind(self, eng, t, p, first, q, copy):
        if copy is None:
            return
        if self.kind == "fm" and q:
            self.block_out(eng, t, p, q - 1, copy)
        elif not (first and p == 0):
            if self.kind == "fm":
                self.block_out(eng, t - 1, 1 - p, 3, copy)
            elif q < self.nb:
                self.block_out(eng, t - 1, 1 - p, q, copy)

    def last_blocks(self, eng, copy):
        if copy is not None:
            for b in range(3 if self.kind == "fm" else 0, self.nb):
                self.block_out(eng, self.n - 1, (self.n - 1) % 2, b, copy)

    def scalar(self, a, copy=None):
        def tile(t, p, first):
            for q in range(4):
                self.high(a, t, p, first, q)
                self.blocks_behind(a, t, p, first, q, copy)
        over_pairs(a, self.n, tile)
        self.last_blocks(a, copy)

    def vector(self, v, copy=None):
        def tile(t, p, first):
            for q in range(4):
                self.low(v, t, p, first, q)
                self.blocks_behind(v, t, p, first, q, copy)
        over_pairs(v, self.n, tile)
        self.last_blocks(v, copy)


LINEAR_SEMS = ("hi_done", "lo_done", "unit_mm", "evac_done")


def reduce_angle(v, st, out, ang, tmp):
    st.link(v.tensor_scalar(tmp, ang, 1.0 / TWO_PI, ROUND, ALU.mult, ALU.add))
    st.link(v.tensor_scalar(tmp, tmp, -ROUND, None, ALU.add))
    st.link(v.scalar_tensor_tensor(out, tmp, -C1, ang, ALU.mult, ALU.add))
    st.link(v.scalar_tensor_tensor(out, tmp, -C2, out, ALU.mult, ALU.add))
    st.link(v.scalar_tensor_tensor(out, tmp, -C3, out, ALU.mult, ALU.add))
    st.link(v.tensor_scalar(out, out, PI_IN, -PI_IN, ALU.min, ALU.max))


def cos_argument(v, st, out, red, tmp):
    st.link(v.tensor_scalar(out, red, float(np.pi / 2), None, ALU.add))
    st.link(v.tensor_scalar(tmp, out, float(np.pi), -TWO_PI, ALU.is_gt, ALU.mult))
    st.link(v.tensor_tensor(out, out, tmp, ALU.add))
    st.link(v.tensor_scalar(out, out, PI_IN, -PI_IN, ALU.min, ALU.max))


def setup_stage(nc, io, m):
    with ExitStack() as ctx, stage(nc, "loaded", "dve_step", "angles_ready", "trig_ready", "lb_shifted", "lb_exp") as s:
        pos_i = ctx.enter_context(buffer(nc, "pos_i", [P, T], I32))
        ang = ctx.enter_context(buffer(nc, "ang", [P, T], F32))
        tmp = ctx.enter_context(buffer(nc, "tmp", [P, T], F32))
        red = ctx.enter_context(buffer(nc, "red", [P, T], F32))
        cred = ctx.enter_context(buffer(nc, "cred", [P, T], F32))
        lbs = ctx.enter_context(buffer(nc, "lbs", [P, L, H], F32))
        lbt = ctx.enter_context(buffer(nc, "lbt", [P, 2, H], F32))
        loads = [(pos_i[:], io["positions"].partition_broadcast(P)), (m.X[:], io["x"]), (m.ident[:], io["c_ident"]), (m.perm[:], io["c_perm"]),
                 (m.cols[:], io["c_cols"]), (lbs[:], io["hgrn_lb"])]
        with nc.Block() as block:
            @block.sync
            def _(sp):
                for dst, src in loads:
                    sp.dma_start(dst, src).then_inc(s["loaded"], 16)

            @block.vector
            def _(v):
                st = Steps(v, s["dve_step"])
                v.wait_ge(s["loaded"], 16 * len(loads))
                st.then(v.memset(m.ones[:], 1.0))
                st.link(v.tensor_copy(ang[:], pos_i[:]))
                st.link(v.tensor_scalar(ang[:], ang[:], m.cols[:, 0:1], None, ALU.mult))
                reduce_angle(v, st, red[:], ang[:], tmp[:])
                cos_argument(v, st, cred[:], red[:], tmp[:])
                st.link(v.tensor_tensor(lbt[:, 0, :], lbs[:, 0, :], lbs[:, 1, :], ALU.max))
                st.then(v.tensor_tensor(lbs[:, 0, :], lbs[:, 0, :], lbt[:, 0, :], ALU.subtract))
                v.tensor_tensor(lbs[:, 1, :], lbs[:, 1, :], lbt[:, 0, :], ALU.subtract).then_inc(s["angles_ready"], 1)
                v.wait_ge(s["trig_ready"], 4)
                st.link(v.tensor_tensor(lbt[:, 0, :], lbs[:, 0, :], lbs[:, 1, :], ALU.add))
                st.link(v.reciprocal(lbt[:, 1, :], lbt[:, 0, :]))
                st.link(v.memset(m.lb_all[:, 0, :], 0.0))
                st.link(v.tensor_tensor(m.lb_all[:, 1, :], lbs[:, 1, :], lbt[:, 1, :], ALU.mult))
                st.link(v.tensor_scalar(m.sin[:], m.sin[:], m.cols[:, 1:2], None, ALU.mult))

            @block.scalar
            def _(a):
                a.wait_ge(s["angles_ready"], 1)
                a.activation(m.sin[:], red[:], ACT.Sin).then_inc(s["trig_ready"], 1)
                a.activation(m.cos[:], cred[:], ACT.Sin).then_inc(s["trig_ready"], 1)
                a.activation(lbs[:, 0, :], lbs[:, 0, :], ACT.Exp).then_inc(s["trig_ready"], 1)
                a.activation(lbs[:, 1, :], lbs[:, 1, :], ACT.Exp).then_inc(s["trig_ready"], 1)


def norm_stage(nc, m, src, nblk, gain, dst, psum, weights, load=()):
    d_hi, d_lo = dst
    with ExitStack() as ctx, stage(nc, "x_ready", "sumsq", "dve_step", "root", "scaled", "turned", "hi_done") as s:
        xn = ctx.enter_context(buffer(nc, "xn", [P, nblk, D], F32))
        ss = ctx.enter_context(buffer(nc, "ss", [P, TB], F32))
        rs = ctx.enter_context(buffer(nc, "rs", [P, TB], F32))
        with nc.Block() as block:
            @block.sync
            def _(sp):
                for dst_, src_ in load:
                    sp.dma_start(dst_, src_).then_inc(s["x_ready"], 16)
                if weights is not None:
                    weights.start(sp)

            @block.scalar
            def _(a):
                if load:
                    a.wait_ge(s["x_ready"], 16 * len(load))
                for b in range(nblk):
                    a.activation(xn[:, b, :], src[:, b, :], ACT.Square, accum_out=ss[:, b:b + 1]).then_inc(s["sumsq"], 1)
                a.wait_ge(s["dve_step"], 1)
                a.activation(rs[:, 0:nblk], ss[:, 0:nblk], ACT.Sqrt).then_inc(s["root"], 1)
                for k in range(KD):
                    a.wait_ge(s["turned"], k + 1)
                    a.activation(d_hi[:, k, 0:nblk * P], psum[:, k, 0:nblk * P], ACT.Copy, scale=gain[:, k:k + 1]).then_inc(s["hi_done"], 1)

            @block.vector
            def _(v):
                v.wait_ge(s["sumsq"], nblk)
                if load:
                    v.wait_ge(s["x_ready"], 16 * len(load))
                st = Steps(v, s["dve_step"])
                st.then(v.tensor_scalar(ss[:, 0:nblk], ss[:, 0:nblk], 1.0 / D, EPS, ALU.mult, ALU.add))
                v.wait_ge(s["root"], 1)
                st.link(v.reciprocal(ss[:, 0:nblk], rs[:, 0:nblk]))
                for b in range(nblk):
                    v.tensor_scalar(xn[:, b, :], src[:, b, :], ss[:, b:b + 1], None, ALU.mult).then_inc(s["scaled"], 1)
                for k in range(KD):
                    v.wait_ge(s["hi_done"], k + 1)
                    st.then(v.scalar_tensor_tensor(d_lo[:, k, 0:nblk * P], psum[:, k, 0:nblk * P], gain[:, k:k + 1],
                                                   d_hi[:, k, 0:nblk * P].bitcast(F32), ALU.mult, ALU.subtract))

            @block.tensor
            def _(pe):
                pe.wait_ge(s["scaled"], nblk)
                for k in range(KD):
                    for b in range(nblk):
                        mm = nc.tensor.transpose(psum[:, k, b * P:(b + 1) * P], xn[:, b, k * P:(k + 1) * P], m.ident[:])
                    mm.then_inc(s["turned"], 1)


def linear_stage(nc, kind, weights, act, nb, N, psum, copy, on="scalar", following=None):
    with ExitStack() as ctx, stage(nc, *LINEAR_SEMS, weights=weights) as s:
        lin = Linear(nc, ctx, s, kind, weights, act, nb, N, psum)
        with nc.Block() as block:
            block.sync(lambda sp: lin.sync(sp, following))
            block.tensor(lin.tensor)
            block.scalar(lambda a: lin.scalar(a, copy if on == "scalar" else None))
            block.vector(lambda v: lin.vector(v, copy if on == "vector" else None))


def hgrn_stage(nc, m, l, q, z, g, vtm, out, psum, io, sm):
    n2 = H * T
    with ExitStack() as ctx, stage(nc, "masks_in", "dve_step", "sig_done", "f_ready", "log_done", "exp_in", "exp_done",
                                   "mix_ready", "mm_done", "level_taken", "inter_ready", "inter_mm", "inter_copied",
                                   "o_mm", "o_copied", "sq_done", "ss_mm", "root_in", "root_done", "silu_done") as s:
        sb = lambda n, sh, dt=F32: ctx.enter_context(buffer(nc, n, sh, dt))
        masks = sb("masks", [P, len(LEVELS) + 1, P], I32)
        lb, om = sb("lb", [P, H]), sb("om", [P, H])
        sg, k, b, reset = sb("sg", [P, H, T]), sb("kk", [P, H, T]), sb("bb", [P, H, T]), sb("reset", [P, H, T])
        dlt = [reset, sb("dlt", [P, H, T])]
        mix = [sb("mix0", [P, H, T]), sb("mix1", [P, H, T])]
        att = sb("att", [P, H, T])
        near = sb("near", [P, H, 2, P])
        far = sb("far", [P, H, 2, 2 * P])
        qfar, k0far, eb = sb("qfar", [P, H, 2 * P]), sb("k0far", [P, H, P]), sb("eb", [P, H, TB])
        f2 = lambda t: t[:].rearrange("p h t -> p (h t)")
        NL = len(LEVELS)
        with nc.Block() as block:
            @block.sync
            def _(sp):
                sp.dma_start(masks[:], io["c_masks"]).then_inc(s["masks_in"], 16)

            @block.scalar
            def _(a):
                a.activation(f2(sg), f2(z), ACT.Sigmoid).then_inc(s["sig_done"], 1)
                a.activation(f2(k), f2(z), ACT.Sigmoid, scale=-1.0).then_inc(s["sig_done"], 1)
                a.wait_ge(s["f_ready"], 1)
                a.activation(f2(sg), f2(sg), ACT.Ln).then_inc(s["log_done"], 1)
                for i in range(NL):
                    a.wait_ge(s["exp_in"], i + 1)
                    a.activation(f2(dlt[i % 2]), f2(dlt[i % 2]), ACT.Exp).then_inc(s["exp_done"], 1)
                a.wait_ge(s["exp_in"], NL + 1)
                a.activation(f2(dlt[NL % 2]), f2(dlt[NL % 2]), ACT.Exp).then_inc(s["exp_done"], 1)
                a.activation(f2(b), f2(b), ACT.Exp).then_inc(s["exp_done"], 1)
                for h in range(H):
                    a.wait_ge(s["inter_mm"], 2 * h + 1)
                    a.copy(near[:, h].rearrange("p c t -> p (c t)"), psum[:, 4 + h % 2, 0:2 * P]).then_inc(s["inter_copied"], 1)
                    a.wait_ge(s["inter_mm"], 2 * h + 2)
                    a.copy(far[:, h].rearrange("p c t -> p (c t)"), psum[:, 6 + h % 2, :]).then_inc(s["inter_copied"], 1)
                for h in range(H):
                    a.wait_ge(s["o_mm"], h + 1)
                    a.mul(out[:, h, :], psum[:, h, :], float(P) ** -0.5).then_inc(s["o_copied"], 1)
                    a.wait_ge(s["o_copied"], h + 1)
                    a.activation(mix[0][:, h, :], out[:, h, :], ACT.Square).then_inc(s["sq_done"], 1)
                a.wait_ge(s["root_in"], 1)
                a.activation(f2(mix[1]), f2(mix[1]), ACT.Sqrt).then_inc(s["root_done"], 1)
                a.activation(f2(g), f2(g), ACT.Silu).then_inc(s["silu_done"], 1)

            @block.vector
            def _(v):
                st = Steps(v, s["dve_step"])
                st.link(v.tensor_copy(lb[:].rearrange("p (a h) -> p a h", a=1), m.lb_all[:, bass.ds(l, 1), :]))
                st.link(v.tensor_scalar(om[:], lb[:], -1.0, 1.0, ALU.mult, ALU.add))
                st.link(v.memset(reset[:], 1.0))
                st.link(v.memset(f2(reset)[:, 0:n2:P], 0.0))
                v.wait_ge(s["sig_done"], 2)
                for h in range(H):
                    st.then(v.tensor_scalar(sg[:, h, :], sg[:, h, :], om[:, h:h + 1], lb[:, h:h + 1], ALU.mult, ALU.add))
                    st.then(v.tensor_scalar(k[:, h, :], k[:, h, :], om[:, h:h + 1], None, ALU.mult))
                st.settle()
                v.tensor_scalar(f2(sg), f2(sg), 1e-6, 1.0, ALU.max, ALU.min).then_inc(s["f_ready"], 1)
                v.wait_ge(s["log_done"], 1)
                st.link(v.tensor_tensor_scan(f2(b), f2(reset), f2(sg), 0.0, ALU.mult, ALU.add))
                st.link(v.memset(att[:], 0.0))
                v.wait_ge(s["masks_in"], 16)

                def exponents(i, half):
                    bv = f2(b).rearrange("p (n w) -> p n w", w=2 * half)
                    dv = f2(dlt[i % 2]).rearrange("p (n w) -> p n w", w=2 * half)
                    ref = bv[:, :, half - 1:half].broadcast_to([P, n2 // (2 * half), half])
                    if i >= 2:
                        v.wait_ge(s["mix_ready"], i - 1)
                    st.then(v.tensor_tensor(dv[:, :, 0:half], ref, bv[:, :, 0:half], ALU.subtract))
                    v.tensor_tensor(dv[:, :, half:], bv[:, :, half:], ref, ALU.subtract).then_inc(s["exp_in"], 1)

                def take(i):
                    for h in range(H):
                        v.wait_ge(s["mm_done"], H * i + h + 1)
                        if i:
                            v.wait_ge(s["level_taken"], H * (i - 1) + h + 1)
                        mk = masks[:, i:i + 1, :].broadcast_to([P, TB, P])
                        v.copy_predicated(att[:, h, :].rearrange("p (c t) -> p c t", c=TB), mk,
                                          psum[:, 4 * (i % 2) + h, :].rearrange("p (c t) -> p c t", c=TB)).then_inc(s["level_taken"], 1)

                take(0)
                exponents(0, LEVELS[0])
                for i, half in enumerate(LEVELS):
                    if i + 1 < NL:
                        exponents(i + 1, LEVELS[i + 1])
                    v.wait_ge(s["exp_done"], i + 1)
                    if i >= 2:
                        v.wait_ge(s["mm_done"], H * i)
                    sh = lambda t: f2(t).rearrange("p (n w) -> p n w", w=2 * half)
                    e, mx = sh(dlt[i % 2]), sh(mix[i % 2])
                    st.link(v.tensor_tensor(mx[:, :, 0:half], sh(k)[:, :, 0:half], e[:, :, 0:half], ALU.mult))
                    v.tensor_tensor(mx[:, :, half:], sh(q)[:, :, half:], e[:, :, half:], ALU.mult).then_inc(s["mix_ready"], 1)
                    if i >= 1:
                        take(i)
                d = dlt[NL % 2]
                bv, dv = f2(b).rearrange("p (n w) -> p n w", w=P), f2(d).rearrange("p (n w) -> p n w", w=P)
                v.wait_ge(s["mix_ready"], NL - 1)
                v.tensor_tensor(dv, bv[:, :, P - 1:P].broadcast_to([P, H * TB, P]), bv, ALU.subtract).then_inc(s["exp_in"], 1)
                take(NL)
                v.wait_ge(s["exp_done"], NL + 2)
                st.then(v.tensor_copy(eb[:].rearrange("p h c -> p (h c)"), f2(b)[:, P - 1:n2:P]))
                st.settle()
                v.wait_ge(s["mm_done"], H * (NL + 1))
                st.then(v.tensor_tensor(f2(mix[0]), f2(k), f2(d), ALU.mult))
                st.link(v.tensor_tensor(f2(mix[1]), f2(q), f2(b), ALU.mult))
                for h in range(H):
                    st.then(v.tensor_scalar(k0far[:, h, :], mix[0][:, h, 0:P], eb[:, h, 1:2], None, ALU.mult))
                    st.then(v.tensor_copy(qfar[:, h, 0:P], mix[1][:, h, 2 * P:3 * P]))
                    st.then(v.tensor_scalar(qfar[:, h, P:], mix[1][:, h, 3 * P:], eb[:, h, 2:3], None, ALU.mult))
                st.settle()
                v.engine_nop().then_inc(s["inter_ready"], 1)
                v.wait_ge(s["ss_mm"], H)
                v.wait_ge(s["inter_mm"], 2 * H)
                v.tensor_scalar(f2(mix[1]), psum[:, 4:8, :].rearrange("p h t -> p (h t)"), 1.0 / P, EPS, ALU.mult, ALU.add).then_inc(s["root_in"], 1)
                v.wait_ge(s["root_done"], 1)
                st.link(v.reciprocal(f2(mix[1]), f2(mix[1])))
                st.link(v.tensor_tensor(f2(out), f2(out), f2(mix[1]), ALU.mult))
                c0 = COL["hgrn_norm"][0]
                v.wait_ge(s["silu_done"], 1)
                for h in range(H):
                    st.link(v.scalar_tensor_tensor(out[:, h, :], out[:, h, :], sm[:, c0 + h:c0 + h + 1], g[:, h, :], ALU.mult, ALU.mult))

            @block.tensor
            def _(pe):
                pe.wait_ge(s["f_ready"], 1)
                for i in range(NL + 1):
                    if i:
                        pe.wait_ge(s["mix_ready"], i)
                    for h in range(H):
                        if i >= 2:
                            pe.wait_ge(s["level_taken"], H * (i - 2) + h + 1)
                        for c in range(TB):
                            cs = slice(c * P, (c + 1) * P)
                            lhs, rhs = (k, q) if i == 0 else (mix[(i - 1) % 2], mix[(i - 1) % 2])
                            mm = nc.tensor.matmul(psum[:, 4 * (i % 2) + h, cs], lhs[:, h, cs], rhs[:, h, cs], start=True, stop=True)
                        mm.then_inc(s["mm_done"], 1)
                pe.wait_ge(s["inter_ready"], 1)
                kd, qd = mix
                pe.wait_ge(s["level_taken"], H * (NL + 1))
                for h in range(H):
                    if h >= 2:
                        pe.wait_ge(s["inter_copied"], 2 * (h - 2) + 1)
                    nb_, fb = psum[:, 4 + h % 2, :], psum[:, 6 + h % 2, :]
                    nc.tensor.matmul(nb_[:, 0:P], kd[:, h, 0:P], qd[:, h, P:2 * P], start=True, stop=True)
                    nc.tensor.matmul(nb_[:, P:2 * P], kd[:, h, 2 * P:3 * P], qd[:, h, 3 * P:], start=True, stop=True).then_inc(s["inter_mm"], 1)
                    if h >= 2:
                        pe.wait_ge(s["inter_copied"], 2 * (h - 2) + 2)
                    nc.tensor.matmul(fb[:, 0:2 * P], k0far[:, h, :], qfar[:, h, :], start=True, stop=True)
                    nc.tensor.matmul(fb[:, 2 * P:], kd[:, h, P:2 * P], qfar[:, h, :], start=True, stop=True).then_inc(s["inter_mm"], 1)
                for h in range(H):
                    pe.wait_ge(s["inter_copied"], 2 * h + 2)
                    o = psum[:, h, :]
                    vt = lambda c: vtm[:, c, h * P:(h + 1) * P]
                    prods = [(o[:, c * P:(c + 1) * P], vt(c), att[:, h, c * P:(c + 1) * P]) for c in range(TB)]
                    prods += [(o[:, P:2 * P], vt(0), near[:, h, 0, :]), (o[:, 3 * P:], vt(2), near[:, h, 1, :]),
                              (o[:, 2 * P:], vt(0), far[:, h, 0, :]), (o[:, 2 * P:], vt(1), far[:, h, 1, :])]
                    for n, (dst, lhsT, rhs) in enumerate(prods):
                        mm = nc.tensor.matmul(dst, lhsT, rhs, start=(n == 0), stop=True, skip_group_check=True)
                    mm.then_inc(s["o_mm"], 1)
                pe.wait_ge(s["inter_copied"], 2 * H)
                for h in range(H):
                    pe.wait_ge(s["sq_done"], h + 1)
                    nc.tensor.matmul(psum[:, 4 + h, :], m.ones[:], mix[0][:, h, :], start=True, stop=True).then_inc(s["ss_mm"], 1)


def retention_stage(nc, m, q, k, g, vtm, out, psum, io):
    with ExitStack() as ctx, stage(nc, "dmat_in", "dve_step", "swapped", "rope_done", "score_mm", "decayed", "o_mm", "o_copied",
                                   "mean_mm", "centred", "sq_done", "var_mm", "root_in", "root_done", "silu_done") as s:
        sb = lambda n, sh, dt=F32: ctx.enter_context(buffer(nc, n, sh, dt))
        dmat = sb("dmat", [P, H, T])
        tmp = sb("rtmp", [P, 2, T])
        att = [sb(f"ratt{i}", [P, TB, T]) for i in range(2)]
        sq, rt = sb("sq", [P, H, T]), sb("rt", [P, H, T])
        f2 = lambda t: t[:].rearrange("p h t -> p (h t)")
        rows = [(x, h) for h in range(H) for x in (q, k)]
        with nc.Block() as block:
            @block.sync
            def _(sp):
                sp.dma_start(dmat[:], io["c_dmat"]).then_inc(s["dmat_in"], 16)

            @block.tensor
            def _(pe):
                for n, (x, h) in enumerate(rows):
                    nc.tensor.matmul(psum[:, n, :], m.perm[:], x[:, h, :], start=True, stop=True).then_inc(s["swapped"], 1)
                for h in range(H):
                    pe.wait_ge(s["rope_done"], 2 * h + 2)
                    for c in range(TB):
                        n = H * h + c
                        if n >= 4:
                            pe.wait_ge(s["decayed"], n - 3)
                        else:
                            pe.wait_ge(s["rope_done"], n + 1)
                        nc.tensor.matmul(psum[:, n % 4, 0:T - c * P], k[:, h, c * P:(c + 1) * P], q[:, h, c * P:], start=True, stop=True).then_inc(s["score_mm"], 1)
                    if h == 0:
                        pe.wait_ge(s["rope_done"], 2 * H)
                    pe.wait_ge(s["decayed"], TB * (h + 1))
                    for c in range(TB):
                        mm = nc.tensor.matmul(psum[:, 4 + h, c * P:], vtm[:, c, h * P:(h + 1) * P], att[h % 2][:, c, 0:T - c * P],
                                              start=(c == 0), stop=True, skip_group_check=True)
                    mm.then_inc(s["o_mm"], 1)
                for h in range(H):
                    pe.wait_ge(s["o_copied"], h + 1)
                    nc.tensor.matmul(psum[:, h, :], m.ones[:], out[:, h, :], start=True, stop=True).then_inc(s["mean_mm"], 1)
                for h in range(H):
                    pe.wait_ge(s["sq_done"], h + 1)
                    nc.tensor.matmul(psum[:, 4 + h, :], m.ones[:], sq[:, h, :], start=True, stop=True).then_inc(s["var_mm"], 1)

            @block.scalar
            def _(a):
                for h in range(H):
                    a.wait_ge(s["o_mm"], h + 1)
                    a.copy(out[:, h, :], psum[:, 4 + h, :]).then_inc(s["o_copied"], 1)
                for h in range(H):
                    a.wait_ge(s["centred"], h + 1)
                    a.activation(sq[:, h, :], out[:, h, :], ACT.Square).then_inc(s["sq_done"], 1)
                a.wait_ge(s["root_in"], 1)
                a.activation(f2(rt), f2(rt), ACT.Sqrt).then_inc(s["root_done"], 1)
                a.activation(f2(g), f2(g), ACT.Silu).then_inc(s["silu_done"], 1)

            @block.vector
            def _(v):
                st = Steps(v, s["dve_step"])
                for n, (x, h) in enumerate(rows):
                    v.wait_ge(s["swapped"], n + 1)
                    st.then(v.tensor_tensor(tmp[:, n % 2, :], psum[:, n, :], m.sin[:], ALU.mult))
                    st.link(v.tensor_tensor(x[:, h, :], x[:, h, :], m.cos[:], ALU.mult))
                    v.tensor_tensor(x[:, h, :], x[:, h, :], tmp[:, n % 2, :], ALU.add).then_inc(s["rope_done"], 1)
                v.wait_ge(s["dmat_in"], 16)
                for h in range(H):
                    for c in range(TB):
                        v.wait_ge(s["score_mm"], H * h + c + 1)
                        if h >= 2:
                            v.wait_ge(s["o_mm"], h - 1)
                        w = T - c * P
                        v.tensor_tensor(att[h % 2][:, c, 0:w], psum[:, (H * h + c) % 4, 0:w], dmat[:, h, 0:w], ALU.mult).then_inc(s["decayed"], 1)
                for h in range(H):
                    v.wait_ge(s["mean_mm"], h + 1)
                    v.scalar_tensor_tensor(out[:, h, :], psum[:, h, :], -1.0 / P, out[:, h, :], ALU.mult, ALU.add).then_inc(s["centred"], 1)
                v.wait_ge(s["var_mm"], H)
                v.tensor_scalar(f2(rt), psum[:, 4:8, :].rearrange("p h t -> p (h t)"), 1.0 / P, EPS, ALU.mult, ALU.add).then_inc(s["root_in"], 1)
                v.wait_ge(s["root_done"], 1)
                st.link(v.reciprocal(f2(rt), f2(rt)))
                st.link(v.tensor_tensor(f2(out), f2(out), f2(rt), ALU.mult))
                v.wait_ge(s["silu_done"], 1)
                st.link(v.tensor_tensor(f2(out), f2(out), f2(g), ALU.mult))


def ssm_tables_stage(nc, m, io, l, sm, tabs):
    with ExitStack() as ctx, stage(nc, "bc_in", "dve_step", "dt_in", "exp_in", "exp_done", "sin_in", "sin_done", "tab_in", "tab_done") as s:
        sb = lambda n, sh, dt=F32: ctx.enter_context(buffer(nc, n, sh, dt))
        bc = sb("bc", [P, 4, G5, C5])
        nvec = sb("nvec", [P, N5])
        t = sb("t5", [P, 20 + J5, G5])
        pr, pi = sb("pr", [P, J5 + 1, G5]), sb("pi", [P, J5 + 1, G5])
        fr, fi = sb("fr", [P, J5 + 1, G5]), sb("fi", [P, J5 + 1, G5])
        zr, zi = sb("zr", [P, J5, G5]), sb("zi", [P, J5, G5])
        big = sb("big5", [P, G5, J5, C5])
        col = lambda n: sm[:, COL[n][0]:COL[n][1]]
        sgn = m.cols[:, 1:2]
        nsgn = m.cols[:, 2:3]
        lr, li, dt, th, th8, red, cred, mag, are, aim, den, tmp, r8, fhi, flo, u1, u2, cth, zre, zim = (t[:, i, :] for i in range(20))
        with nc.Block() as block:
            @block.sync
            def _(sp):
                sp.dma_start(bc[:].rearrange("p a g c -> p (a g c)"), tile_at(io["s5_bc"], l)).then_inc(s["bc_in"], 16)
                sp.dma_start(nvec[:], io["c_nvec"]).then_inc(s["bc_in"], 16)

            @block.scalar
            def _(a):
                a.activation(dt, col("log_step"), ACT.Exp).then_inc(s["dt_in"], 1)
                a.wait_ge(s["exp_in"], 1)
                a.activation(mag, u1, ACT.Exp).then_inc(s["exp_done"], 1)
                a.activation(r8, u1, ACT.Exp, scale=float(J5)).then_inc(s["exp_done"], 1)
                a.wait_ge(s["sin_in"], 1)
                a.activation(aim, red, ACT.Sin).then_inc(s["sin_done"], 1)
                a.activation(are, cred, ACT.Sin).then_inc(s["sin_done"], 1)
                a.wait_ge(s["tab_in"], 1)
                a.activation(tabs.sin[:], tabs.sin[:], ACT.Sin, scale=TWO_PI).then_inc(s["tab_done"], 1)
                a.activation(tabs.cos[:], tabs.cos[:], ACT.Sin, scale=TWO_PI).then_inc(s["tab_done"], 1)

            @block.vector
            def _(v):
                st = Steps(v, s["dve_step"])
                tt = lambda o, x, y, op: st.link(v.tensor_tensor(o, x, y, op))
                ts = lambda o, x, c, d, op, op2=ALU.bypass: st.link(v.tensor_scalar(o, x, c, d, op, op2))
                v.wait_ge(s["dt_in"], 1)
                ts(lr, col("lam_re"), -1e-4, None, ALU.min)
                tt(u1, lr, dt, ALU.mult)
                v.engine_nop().then_inc(s["exp_in"], 1)
                tt(th, col("lam_im"), dt, ALU.mult)
                reduce_angle(v, st, red, th, tmp)
                cos_argument(v, st, cred, red, tmp)
                v.engine_nop().then_inc(s["sin_in"], 1)
                ts(th8, red, float(J5), None, ALU.mult)
                reduce_angle(v, st, u2, th8, tmp)
                ts(u2, u2, 1.0 / TWO_PI, None, ALU.mult)
                ts(fhi, u2, ROUND13, None, ALU.add)
                ts(fhi, fhi, -ROUND13, None, ALU.add)
                tt(flo, u2, fhi, ALU.subtract)
                v.wait_ge(s["bc_in"], 32)
                gn = [P, G5, N5]
                per_g = lambda x: x.rearrange("p (g n) -> p g n", n=1).broadcast_to(gn)
                per_n = nvec[:].rearrange("p (g n) -> p g n", g=1).broadcast_to(gn)
                s3 = tabs.sin[:].rearrange("p (g n) -> p g n", n=N5)
                c3 = tabs.cos[:].rearrange("p (g n) -> p g n", n=N5)
                d3 = tabs.decay[:].rearrange("p (g n) -> p g n", n=N5)
                st.link(v.tensor_tensor(s3, per_g(fhi), per_n, ALU.mult))
                st.link(v.tensor_scalar(tabs.cos[:], tabs.sin[:], ROUND, None, ALU.add))
                st.link(v.tensor_scalar(tabs.cos[:], tabs.cos[:], -ROUND, None, ALU.add))
                st.link(v.tensor_tensor(s3, s3, c3, ALU.subtract))
                st.link(v.tensor_tensor(c3, per_g(flo), per_n, ALU.mult))
                st.link(v.tensor_tensor(s3, s3, c3, ALU.add))
                st.link(v.tensor_scalar(tabs.cos[:], tabs.sin[:], 0.25, None, ALU.add))
                st.link(v.tensor_scalar(tabs.decay[:], tabs.cos[:], 0.5, -1.0, ALU.is_gt, ALU.mult))
                st.link(v.tensor_tensor(tabs.cos[:], tabs.cos[:], tabs.decay[:], ALU.add))
                for x in (tabs.sin, tabs.cos):
                    st.link(v.tensor_scalar(x[:], x[:], 0.4999999, -0.4999999, ALU.min, ALU.max))
                v.engine_nop().then_inc(s["tab_in"], 1)
                v.wait_ge(s["exp_done"], 2)
                st.link(v.tensor_copy(d3, per_g(r8)))
                st.link(v.memset(tabs.decay[:, 0:G5 * N5:N5], 0.0))
                v.wait_ge(s["sin_done"], 2)
                tt(are, are, mag, ALU.mult)
                tt(aim, aim, mag, ALU.mult)
                tt(den, lr, lr, ALU.mult)
                tt(tmp, col("lam_im"), col("lam_im"), ALU.mult)
                tt(den, den, tmp, ALU.add)
                st.link(v.reciprocal(den, den))
                ts(u1, are, -1.0, None, ALU.add)
                tt(zre, u1, lr, ALU.mult)
                tt(tmp, aim, col("lam_im"), ALU.mult)
                tt(zre, zre, tmp, ALU.add)
                tt(zim, aim, lr, ALU.mult)
                tt(tmp, u1, col("lam_im"), ALU.mult)
                tt(zim, zim, tmp, ALU.subtract)
                tt(zre, zre, den, ALU.mult)
                tt(zim, zim, den, ALU.mult)
                def product(ore, oim, xre, xim, yre, yim, w):
                    wide = t[:, 20:20 + w, :]
                    tt(ore, xre, yre, ALU.mult)
                    tt(wide, xim, yim, ALU.mult)
                    tt(ore, ore, wide, ALU.subtract)
                    tt(oim, xre, yim, ALU.mult)
                    tt(wide, xim, yre, ALU.mult)
                    tt(oim, oim, wide, ALU.add)

                for re, im, slot in ((pr, pi, lambda lo, hi: slice(lo, hi + 1)), (fr, fi, lambda lo, hi: slice(J5 - hi, J5 - lo + 1))):
                    st.link(v.memset(re[:, slot(0, 0), :], 1.0))
                    st.link(v.memset(im[:, slot(0, 0), :], 0.0))
                    st.link(v.tensor_copy(re[:, slot(1, 1), :], t[:, 8:9, :]))
                    st.link(v.tensor_copy(im[:, slot(1, 1), :], t[:, 9:10, :]))
                    for k in (1, 2, 4):
                        y = lambda z: z[:, slot(k, k), :].broadcast_to([P, k, G5])
                        new, old = slot(k + 1, 2 * k), slot(1, k)
                        product(re[:, new, :], im[:, new, :], re[:, old, :], im[:, old, :], y(re), y(im), k)
                y = lambda z: z.broadcast_to([P, J5, G5])
                product(zr[:], zi[:], fr[:, 1:, :], fi[:, 1:, :], y(t[:, 18:19, :]), y(t[:, 19:20, :]), J5)
                fl = lambda i: bc[:, i].rearrange("p g c -> p (g c)")
                st.link(v.tensor_scalar(fl(1), fl(1), sgn, None, ALU.mult))
                st.link(v.tensor_scalar(fl(2), fl(2), nsgn, None, ALU.mult))
                st.link(v.tensor_scalar(fl(3), fl(3), -1.0, None, ALU.mult))
                gjc = [P, G5, J5, C5]
                coef = lambda x: x.rearrange("p (j c) g -> p g j c", c=1).broadcast_to(gjc)
                base = lambda i: bc[:, i].rearrange("p g (j c) -> p g j c", j=1).broadcast_to(gjc)
                st.then(v.memset(tabs.pc[:, :, 0:J5 - 1, :], 0.0))
                st.then(v.tensor_copy(tabs.pc[:, :, J5 - 1, :], bc[:, 2]))
                for dst, cr, ci, i in ((tabs.gb[:], zr[:], zi[:], 0), (tabs.pc[:, :, J5:, :], pr[:, 1:, :], pi[:, 1:, :], 2)):
                    st.then(v.tensor_tensor(dst, base(i), coef(cr), ALU.mult))
                    st.link(v.tensor_tensor(big[:], base(i + 1), coef(ci), ALU.mult))
                    st.link(v.tensor_tensor(dst, dst, big[:], ALU.add))
                v.wait_ge(s["tab_done"], 2)
                v.tensor_scalar(tabs.sin[:], tabs.sin[:], nsgn, None, ALU.mult).then_inc(s["dve_step"], 1)


def ssm_stage(nc, m, sm, tabs, u, work, spare, rows, psum):
    with ExitStack() as ctx, stage(nc, "dve_step", "rows_mm", "sorted_even", "sorted_odd", "turn_mm", "turn_copied", "w_mm", "w_copied",
                                   "inj_mm", "inj_turned", "scanned", "block_mm", "block_copied", "toep_in0", "toep_in1",
                                   "swap_mm", "states_in", "y_mm", "y_taken", "y_done", "yt_mm", "yt_copied",
                                   "out_mm", "out_copied") as s:
        sb = lambda n, sh, dt=F32: ctx.enter_context(buffer(nc, n, sh, dt))
        PER = 8
        NB = G5 // PER
        HALF = J5 // 2
        ug = rows.rearrange("n a f -> n (a f)").rearrange("n (g j c) -> n g j c", g=G5, j=J5)
        y64 = rows.rearrange("n a f -> n (a f)").rearrange("n (j f) -> n j f", j=J5)
        uc = sb("uc", [P, G5, N5])
        toep = sb("toep", [P, G5, J5 * C5])
        blocks = [x.rearrange("p a t -> p (a t)").rearrange("p (g k) -> p g k", g=PER)[0:C5] for x in (spare, u)]
        wmat = [sb(f"wmat{i}", [P, 2, 2, P]) for i in range(2)]
        om_, yb, st_ = (x.rearrange("p a t -> p (a t)").rearrange("p (g n) -> p g n", n=N5) for x in work)
        toep_in = (s["toep_in0"], s["toep_in1"])
        ALL_IN = 16 * J5
        f2 = lambda t: t[:].rearrange("p g n -> p (g n)")
        def sort_rows(copy, x):
            g0, j0 = (x // 2) * PER, (x % 2) * HALF
            return copy(ug[:, g0:g0 + PER, j0:j0 + HALF, :], psum[0:N5, x, :].rearrange("n (j g c) -> n g j c", j=HALF, g=PER))

        with nc.Block() as block:
            @block.sync
            def _(sp):
                for c in range(NB):
                    sp.wait_ge(s["block_copied"], 2 * c + 2)
                    for j in range(J5):
                        sp.dma_start(toep[j * C5:(j + 1) * C5, c * PER:(c + 1) * PER, :],
                                     blocks[c % 2][:, :, (J5 - 1 - j) * C5:(2 * J5 - 1 - j) * C5]).then_inc(toep_in[c % 2], 16)

            @block.tensor
            def _(pe):
                for x in range(2 * NB):
                    b, j0 = x // 2, (x % 2) * HALF
                    for j in range(HALF):
                        mm = nc.tensor.transpose(psum[0:N5, x, j * P:(j + 1) * P], u[:, b, j0 + j:T:J5], m.ident[:])
                    mm.then_inc(s["rows_mm"], 1)
                for b in range(NB):
                    pe.wait_ge(s["sorted_even"], b + 1)
                    pe.wait_ge(s["sorted_odd"], b + 1)
                    for g in range(b * PER, (b + 1) * PER):
                        mm = nc.tensor.transpose(psum[:, b, (g % PER) * N5:(g % PER + 1) * N5],
                                                 ug[:, g].rearrange("n j c -> n (j c)"), m.ident[0:N5, 0:N5])
                    mm.then_inc(s["turn_mm"], 1)
                for c in range(G5 // 2 + 1):
                    if c < G5 // 2:
                        b = c % 2
                        if c < 2:
                            pe.wait_ge(s["turn_copied"], NB)
                        else:
                            pe.wait_ge(s["w_copied"], c - 1)
                        for y in range(2):
                            wz = tabs.gb[:, 2 * c + y, :, :].rearrange("p j c -> p (j c)")
                            nc.tensor.transpose(psum[:, 6 + b, 2 * y * P:(2 * y + 1) * P], wz, m.ident[:])
                            mm = nc.tensor.matmul(psum[:, 6 + b, (2 * y + 1) * P:(2 * y + 2) * P], wz, m.perm[:], start=True, stop=True)
                        mm.then_inc(s["w_mm"], 1)
                    if c:
                        pe.wait_ge(s["w_copied"], c)
                        for g in (2 * c - 2, 2 * c - 1):
                            if g % 4 == 0 and g >= 8:
                                pe.wait_ge(s["inj_turned"], g // 4 - 1)
                            cols = slice((g % 4) * N5, (g % 4 + 1) * N5)
                            w = wmat[(c - 1) % 2]
                            nc.tensor.matmul(psum[:, (g // 4) % 2, cols], w[:, g % 2, 0, :], uc[:, g, :], start=True, stop=True)
                            nc.tensor.matmul(psum[:, 2 + (g // 4) % 2, cols], w[:, g % 2, 1, :], uc[:, g, :], start=True, stop=True).then_inc(s["inj_mm"], 1)
                for c in range(2 * NB):
                    bank = 4 + 2 * (c % 2)
                    if c < 2:
                        pe.wait_ge(s["w_copied"], G5 // 2)
                    else:
                        pe.wait_ge(s["block_copied"], c - 1)
                    for g in range(4 * c, 4 * c + 4):
                        mm = nc.tensor.matmul(psum[0:C5, bank + (g % 4) // 2, (g % 2) * 256:(g % 2 + 1) * 256], tabs.gb[:, g, J5 - 1, :],
                                              tabs.pc[:, g].rearrange("p k c -> p (k c)"), start=True, stop=True)
                    mm.then_inc(s["block_mm"], 1)
                pe.wait_ge(s["inj_turned"], G5 // 4)
                pe.wait_ge(s["scanned"], 1)
                for c in range(NB):
                    nc.tensor.matmul(psum[:, c, :], m.perm[:], f2(om_)[:, c * 512:(c + 1) * 512], start=True, stop=True).then_inc(s["swap_mm"], 1)
                pe.wait_ge(s["block_copied"], 2 * NB)
                for g in range(G5):
                    b = g // PER
                    if g % PER == 0:
                        pe.wait_ge(toep_in[b % 2], ALL_IN * (b // 2 + 1))
                        if b >= 2:
                            pe.wait_ge(s["y_taken"], b - 1)
                    if g == 0:
                        pe.wait_ge(s["states_in"], 1)
                    yp = psum[:, 4 + b % 2, (g % PER) * N5:(g % PER + 1) * N5]
                    nc.tensor.matmul(yp, toep[:, g, :], uc[:, g, :], start=True, stop=True, skip_group_check=True)
                    nc.tensor.matmul(yp[:, 1:], tabs.pc[:, g, J5:, :].rearrange("p j c -> p (j c)"), st_[:, g, 0:N5 - 1],
                                     start=False, stop=True, skip_group_check=True).then_inc(s["y_mm"], 1)

                def out(b):
                    pe.wait_ge(s["yt_copied"], 2 * b + 2)
                    if b >= 2:
                        pe.wait_ge(s["out_copied"], b - 1)
                    for j in range(J5):
                        mm = nc.tensor.transpose(psum[:, 6 + b % 2, j * N5:(j + 1) * N5], y64[:, j, b * P:(b + 1) * P], m.ident[0:N5, 0:N5])
                    mm.then_inc(s["out_mm"], 1)

                for k in range(G5 // 4):
                    pe.wait_ge(s["y_done"], k // 2 + 1)
                    if k >= 4:
                        pe.wait_ge(s["yt_copied"], k - 3)
                    for g in range(4 * k, 4 * k + 4):
                        mm = nc.tensor.transpose(psum[0:N5, k % 4, (g % 4) * P:(g % 4 + 1) * P], yb[:, g, :], m.ident[:])
                    mm.then_inc(s["yt_mm"], 1)
                    if k % 2 and k >= 3:
                        out(k // 2 - 1)
                out(NB - 1)

            @block.scalar
            def _(a):
                for b in range(NB):
                    a.wait_ge(s["rows_mm"], 2 * b + 1)
                    sort_rows(a.copy, 2 * b).then_inc(s["sorted_even"], 1)
                for c in range(NB):
                    a.wait_ge(s["turn_mm"], c + 1)
                    a.copy(f2(uc)[:, c * 512:(c + 1) * 512], psum[:, c, :]).then_inc(s["turn_copied"], 1)
                for c in range(G5 // 2):
                    a.wait_ge(s["w_mm"], c + 1)
                    if c >= 2:
                        a.wait_ge(s["inj_mm"], 2 * c - 2)
                    a.copy(wmat[c % 2][:].rearrange("p g a k -> p (g a k)"), psum[:, 6 + c % 2, :]).then_inc(s["w_copied"], 1)
                for c in range(2 * NB):
                    r = c // 2
                    a.wait_ge(s["block_mm"], c + 1)
                    if r >= 2 and c % 2 == 0:
                        a.wait_ge(toep_in[r % 2], ALL_IN * (r // 2))
                    a.copy(blocks[r % 2][:, (c % 2) * 4:(c % 2) * 4 + 4, :].rearrange("p g k -> p (g k)"),
                           psum[0:C5, 4 + 2 * (c % 2):6 + 2 * (c % 2), :].rearrange("p b k -> p (b k)")).then_inc(s["block_copied"], 1)
                for c in range(NB):
                    a.wait_ge(s["y_taken"], c + 1)
                    a.activation(f2(yb)[:, c * 512:(c + 1) * 512], f2(yb)[:, c * 512:(c + 1) * 512], ACT.Gelu_apprx_tanh).then_inc(s["y_done"], 1)
                for k in range(G5 // 4):
                    a.wait_ge(s["yt_mm"], k + 1)
                    a.copy(y64[:, :, k * 64:(k + 1) * 64].rearrange("n j (g c) -> n g j c", c=C5),
                           psum[0:N5, k % 4, :].rearrange("n (g j c) -> n g j c", g=4, j=J5)).then_inc(s["yt_copied"], 1)

            @block.vector
            def _(v):
                st = Steps(v, s["dve_step"])
                for b in range(NB):
                    v.wait_ge(s["rows_mm"], 2 * b + 2)
                    sort_rows(v.tensor_copy, 2 * b + 1).then_inc(s["sorted_odd"], 1)
                for c in range(G5 // 4):
                    v.wait_ge(s["inj_mm"], 4 * (c + 1))
                    cs = slice(c * 256, (c + 1) * 256)
                    st.then(v.tensor_tensor(f2(om_)[:, cs], psum[:, c % 2, 0:256], tabs.cos[:, cs], ALU.mult))
                    st.link(v.tensor_tensor(f2(st_)[:, cs], psum[:, 2 + c % 2, 0:256], tabs.sin[:, cs], ALU.mult))
                    v.tensor_tensor(f2(om_)[:, cs], f2(om_)[:, cs], f2(st_)[:, cs], ALU.add).then_inc(s["inj_turned"], 1)
                v.wait_ge(s["inj_turned"], G5 // 4)
                st.link(v.tensor_tensor_scan(f2(st_), tabs.decay[:], f2(om_), 0.0, ALU.mult, ALU.add))
                st.link(v.tensor_copy(f2(om_), f2(st_)))
                v.engine_nop().then_inc(s["scanned"], 1)
                st.link(v.tensor_tensor(f2(st_), f2(st_), tabs.cos[:], ALU.mult))
                for c in range(NB):
                    cs = slice(c * 512, (c + 1) * 512)
                    v.wait_ge(s["swap_mm"], c + 1)
                    st.then(v.tensor_tensor(f2(yb)[:, cs], psum[:, c, :], tabs.sin[:, cs], ALU.mult))
                st.settle()
                v.tensor_tensor(f2(st_), f2(st_), f2(yb), ALU.subtract).then_inc(s["states_in"], 1)
                v.wait_ge(s["states_in"], 1)
                d3 = sm[:, COL["s5_d"][0]:COL["s5_d"][1]].rearrange("p (g n) -> p g n", n=1)
                v.wait_ge(s["swap_mm"], NB)
                st.link(v.tensor_tensor(om_[:], uc[:], d3.broadcast_to([P, G5, N5]), ALU.mult))
                for c in range(NB):
                    cs = slice(c * 512, (c + 1) * 512)
                    v.wait_ge(s["y_mm"], PER * (c + 1))
                    v.tensor_tensor(f2(yb)[:, cs], psum[:, 4 + c % 2, :], f2(om_)[:, cs], ALU.add).then_inc(s["y_taken"], 1)
                v.wait_ge(s["y_taken"], NB)
                for b in range(NB):
                    v.wait_ge(s["out_mm"], b + 1)
                    v.tensor_copy(work[0][:, b, :].rearrange("p (n j) -> p n j", j=J5),
                                  psum[:, 6 + b % 2, :].rearrange("p (j n) -> p n j", j=J5)).then_inc(s["out_copied"], 1)


def glu_stage(nc, io, l, y, out, sm, psum):
    with ExitStack() as ctx, stage(nc, "w_in", "mm_done", "sig_done", "out_done") as s:
        w = ctx.enter_context(buffer(nc, "wglu", [P, 4, W], F32))
        c0 = COL["b_glu"][0]
        with nc.Block() as block:
            @block.sync
            def _(sp):
                sp.dma_start(w[:].rearrange("p k n -> p (k n)"), tile_at(io["w_glu"], l)).then_inc(s["w_in"], 16)

            @block.tensor
            def _(pe):
                pe.wait_ge(s["w_in"], 16)
                for b in range(4):
                    for k in range(4):
                        mm = nc.tensor.matmul(psum[:, b, :], w[:, k, b * P:(b + 1) * P], y[:, k, :], start=(k == 0), stop=(k == 3))
                    mm.then_inc(s["mm_done"], 1)

            @block.scalar
            def _(a):
                for b in range(4):
                    a.wait_ge(s["mm_done"], b + 1)
                    a.activation(out[:, b, :], psum[:, b, :], ACT.Sigmoid, bias=sm[:, c0 + b:c0 + b + 1]).then_inc(s["sig_done"], 1)

            @block.vector
            def _(v):
                for b in range(4):
                    v.wait_ge(s["sig_done"], b + 1)
                    v.tensor_tensor(out[:, b, :], out[:, b, :], y[:, b, :], ALU.mult).then_inc(s["out_done"], 1)


def gates_stage(nc, weights, h, sm, gates, psum):
    c0 = COL["b_gate"][0]

    def copy(t, b, bank):
        return nc.scalar.activation(gates[:, bass.ds(t * 4 + b, 1), :].rearrange("p a n -> p (a n)"), bank, ACT.Sigmoid,
                                    bias=sm[:, bass.ds(t * 4 + b + c0, 1)])
    linear_stage(nc, "fm", weights, h, 4, T, psum, copy)


@contextmanager
def hi_lo(nc, name, shape):
    with buffer(nc, name + "_hi", shape, F32R) as hi, buffer(nc, name + "_lo", shape, F32R) as lo:
        yield hi, lo


def merge_stage(nc, io, l, branches, gates, merged, psum):
    with ExitStack() as ctx, stage(nc, "w_even", "w_odd", "mm_done", "weighed", "added") as s:
        wb = [ctx.enter_context(buffer(nc, f"wm{i}", [P, 4, W], F32)) for i in range(2)]
        part = ctx.enter_context(buffer(nc, "part", [P, 2, T], F32))
        ready = (s["w_even"], s["w_odd"])
        tiles = [(half, br) for half in range(2) for br in range(3)]
        with nc.Block() as block:
            @block.sync
            def _(sp):
                for t, _ in enumerate(tiles):
                    if t >= 2:
                        sp.wait_ge(s["mm_done"], 4 * (t - 1))
                    sp.dma_start(wb[t % 2][:].rearrange("p k n -> p (k n)"), tile_at(io["w_branch"], l * 6 + t)).then_inc(ready[t % 2], 16)

            @block.tensor
            def _(pe):
                for t, (half, br) in enumerate(tiles):
                    pe.wait_ge(ready[t % 2], 16 * (t // 2 + 1))
                    for b in range(4):
                        if t >= 2:
                            pe.wait_ge(s["weighed"], 4 * (t - 2) + b + 1)
                        for k in range(4):
                            mm = nc.tensor.matmul(psum[:, 4 * (t % 2) + b, :], wb[t % 2][:, k, b * P:(b + 1) * P], branches[br][:, k, :],
                                                  start=(k == 0), stop=(k == 3))
                        mm.then_inc(s["mm_done"], 1)

            @block.vector
            def _(v):
                added = 0
                for t, (half, br) in enumerate(tiles):
                    for b in range(4):
                        n = 4 * t + b
                        v.wait_ge(s["mm_done"], n + 1)
                        d = half * 4 + b
                        bank, gate = psum[:, 4 * (t % 2) + b, :], gates[:, br * KD + d, :]
                        if br == 0:
                            v.tensor_tensor(merged(d), bank, gate, ALU.mult).then_inc(s["weighed"], 1)
                        else:
                            v.tensor_tensor(part[:, b % 2, :], bank, gate, ALU.mult).then_inc(s["weighed"], 1)
                            v.wait_ge(s["weighed"], n + 1)
                            v.tensor_tensor(merged(d), merged(d), part[:, b % 2, :], ALU.add).then_inc(s["added"], 1)
                            added += 1
                            v.wait_ge(s["added"], added)


def attend_stage(nc, m, q, k, v_tm, out, psum):
    XH, XD = 4, 2
    scale = float(XD * P) ** -0.5
    with ExitStack() as ctx, stage(nc, "score_mm", "max_done", "neg_done", "exp_done", "dve_step", "p_ready", "turned", "pt_copied", "o_mm", "o_copied") as s:
        sb = lambda n, sh, dt=F32: ctx.enter_context(buffer(nc, n, sh, dt))
        pr = [sb(f"prob{i}", [P, TB, MEM]) for i in range(2)]
        pt = [sb(f"probT{i}", [P, MB, T]) for i in range(2)]
        mx, sm_, rc = sb("mx", [P, XH, TB]), sb("sme", [P, XH, TB]), sb("rc", [P, XH, TB])
        with nc.Block() as block:
            @block.tensor
            def _(pe):
                def scores(h):
                    if h >= 2:
                        pe.wait_ge(s["exp_done"], TB * (h - 1))
                    for b in range(TB):
                        for kk in range(XD):
                            mm = nc.tensor.matmul(psum[:, 2 * (h % 2) + b // 2, (b % 2) * MEM:(b % 2 + 1) * MEM],
                                                  q[:, XD * h + kk, b * P:(b + 1) * P], k[:, XD * h + kk, 0:MEM], start=(kk == 0), stop=(kk == XD - 1))
                    mm.then_inc(s["score_mm"], 1)

                scores(0)
                for h in range(XH):
                    if h + 1 < XH:
                        scores(h + 1)
                    pe.wait_ge(s["p_ready"], h + 1)
                    if h >= 1:
                        pe.wait_ge(s["pt_copied"], MB * h)
                    for j in range(MB):
                        for b in range(TB):
                            mm = nc.tensor.transpose(psum[:, 4 + j, b * P:(b + 1) * P], pr[h % 2][:, b, j * P:(j + 1) * P], m.ident[:])
                        mm.then_inc(s["turned"], 1)
                    pe.wait_ge(s["pt_copied"], MB * (h + 1))
                    for e in range(XD):
                        if h >= 1:
                            pe.wait_ge(s["o_copied"], XD * (h - 1) + e + 1)
                        for j in range(MB):
                            mm = nc.tensor.matmul(psum[:, 6 + e, :], v_tm[:, j, (XD * h + e) * P:(XD * h + e + 1) * P], pt[h % 2][:, j, :],
                                                  start=(j == 0), stop=(j == MB - 1))
                        mm.then_inc(s["o_mm"], 1)

            @block.vector
            def _(v):
                st = Steps(v, s["dve_step"])
                for h in range(XH):
                    v.wait_ge(s["score_mm"], h + 1)
                    bank = psum[:, 2 * (h % 2):2 * (h % 2) + 2, :].rearrange("p a (b n) -> p (a b) n", n=MEM)
                    st.link(v.tensor_reduce(mx[:, h, :], bank, AX, ALU.max))
                    v.tensor_scalar(mx[:, h, :], mx[:, h, :], -scale, None, ALU.mult).then_inc(s["neg_done"], 1)
                    v.wait_ge(s["exp_done"], TB * (h + 1))
                    st.link(v.reciprocal(rc[:, h, :], sm_[:, h, :]))
                    v.tensor_tensor(pr[h % 2][:], pr[h % 2][:], rc[:, h, :].rearrange("p (b n) -> p b n", n=1).broadcast_to([P, TB, MEM]), ALU.mult).then_inc(s["p_ready"], 1)

            @block.scalar
            def _(a):
                def exps(h):
                    a.wait_ge(s["neg_done"], h + 1)
                    if h >= 2:
                        a.wait_ge(s["turned"], MB * (h - 1))
                    for b in range(TB):
                        a.activation(pr[h % 2][:, b, :], psum[:, 2 * (h % 2) + b // 2, (b % 2) * MEM:(b % 2 + 1) * MEM], ACT.Exp,
                                     bias=mx[:, h, b:b + 1], scale=scale, accum_out=sm_[:, h, b:b + 1]).then_inc(s["exp_done"], 1)

                exps(0)
                for h in range(XH):
                    if h + 1 < XH:
                        exps(h + 1)
                    for j in range(MB):
                        a.wait_ge(s["turned"], MB * h + j + 1)
                        if h >= 2:
                            a.wait_ge(s["o_mm"], XD * (h - 1))
                        a.copy(pt[h % 2][:, j, :], psum[:, 4 + j, :]).then_inc(s["pt_copied"], 1)
                    for e in range(XD):
                        a.wait_ge(s["o_mm"], XD * h + e + 1)
                        a.copy(out[:, XD * h + e, :], psum[:, 6 + e, :]).then_inc(s["o_copied"], 1)


def top16(v, st, values, index, src, rest):
    st.link(v.max(values[:, 0:8], src))
    st.then(v.max_index(index[:, 0:8], values[:, 0:8], src))
    st.link(v.match_replace(rest, values[:, 0:8], src, -3.0e38))
    st.link(v.max(values[:, 8:16], rest))
    st.then(v.max_index(index[:, 8:16], values[:, 8:16], rest))


def keys_stage(nc, io, l, weights, h, val, idx, psum):
    NT = 2 * PH // 4
    with ExitStack() as ctx, stage(nc, *LINEAR_SEMS, "keys_in", "score_mm", "score_copied", "chosen", "dve_step", weights=weights) as s:
        sb = lambda n, sh, dt=F32: ctx.enter_context(buffer(nc, n, sh, dt))
        keys = sb("keys", [P, 2 * PH, PK])
        qT = sb("qT", [P, 2, 4, T])
        sc = sb("sc", [P, TB, 4, PK])
        rest = sb("rest", [P, PK])
        lin = Linear(nc, ctx, s, "fm", weights, h, 4, T, psum)
        units = [(t, q) for t in range(NT) for q in range(4)]
        with nc.Block() as block:
            @block.sync
            def _(sp):
                sp.dma_start(keys[:].rearrange("p a k -> p (a k)"), tile_at(io["keys"], l)).then_inc(s["keys_in"], 16)
                lin.sync(sp)

            @block.tensor
            def _(pe):
                def scores(t):
                    for tb in range(TB):
                        if t:
                            pe.wait_ge(s["score_copied"], TB * (t - 1) + tb + 1)
                        for x in range(4):
                            mm = nc.tensor.matmul(psum[:, 4 + tb, x * PK:(x + 1) * PK], qT[:, t % 2, x, tb * P:(tb + 1) * P], keys[:, 4 * t + x, :], start=True, stop=True)
                        mm.then_inc(s["score_mm"], 1)

                pe.wait_ge(s["keys_in"], 16)
                for t, q in units:
                    lin.unit(pe, t, t % 2, t < 2, q)
                    if t and q == 0:
                        pe.wait_ge(s["evac_done"], 4 * t)
                        scores(t - 1)
                pe.wait_ge(s["evac_done"], 4 * NT)
                scores(NT - 1)

            @block.scalar
            def _(a):
                def query(t, b, bank):
                    if t >= 2:
                        a.wait_ge(s["score_mm"], TB * (t - 1))
                    return a.copy(qT[:, t % 2, b, :], bank)

                def score(t, tb):
                    a.wait_ge(s["score_mm"], TB * t + tb + 1)
                    if t:
                        a.wait_ge(s["chosen"], TB * (t - 1) + tb + 1)
                    a.copy(sc[:, tb].rearrange("p a k -> p (a k)"), psum[:, 4 + tb, :]).then_inc(s["score_copied"], 1)

                for t, q in units:
                    lin.high(a, t, t % 2, t < 2, q)
                    lin.blocks_behind(a, t, t % 2, t < 2, q, query)
                    if t and q:
                        score(t - 1, q - 1)
                    if t and q == 3:
                        score(t - 1, 3)
                lin.last_blocks(a, query)
                for tb in range(TB):
                    score(NT - 1, tb)

            @block.vector
            def _(v):
                st = Steps(v, s["dve_step"])

                def choose(t, tb):
                    v.wait_ge(s["score_copied"], TB * t + tb + 1)
                    for x in range(4):
                        top16(v, st, val[:, tb, 4 * t + x, :], idx[:, tb, 4 * t + x, :], sc[:, tb, x, :], rest[:])
                    st.settle()
                    v.engine_nop().then_inc(s["chosen"], 1)

                for n, (t, q) in enumerate(units):
                    lin.low(v, t, t % 2, t < 2, q)
                    if n >= 6:
                        choose((n - 6) // 4, (n - 6) % 4)
                for n in range(4 * NT - 6, 4 * NT):
                    choose(n // 4, n % 4)


def choose_stage(nc, m, io, val, idx, lists, psum):
    with ExitStack() as ctx, stage(nc, "iota_in", "dve_step", "best_in", "exp_done", "listed", "turned", "list_copied", "gate_lo") as s:
        sb = lambda n, sh, dt=F32: ctx.enter_context(buffer(nc, n, sh, dt))
        rest = sb("rest", [P, 256])
        cand = sb("cand", [P, PH, TOPK * TOPK])
        pos = sb("pos", [P, PH, TOPK], U32)
        idxf = sb("idxf", [P, PH, 2, TOPK], F16)
        best = [sb(f"best{i}", [P, PH, TOPK]) for i in range(2)]
        ab_i = sb("ab_i", [P, 2, SLOTS], U32)
        ab = sb("ab", [P, 2, SLOTS], F16)
        hot = sb("hot", [P, PH, TOPK, TOPK], F16)
        numbers = sb("numbers", [P, TOPK])
        i16 = sb("i16", [P, TOPK], F16)
        den = sb("den", [P, PH])
        out3 = [sb(f"out3{i}", [P, 3, SLOTS]) for i in range(2)]
        with nc.Block() as block:
            @block.sync
            def _(sp):
                sp.dma_start(numbers[:], io["c_nvec"][:, 0:TOPK]).then_inc(s["iota_in"], 16)

            @block.tensor
            def _(pe):
                for tb in range(TB):
                    pe.wait_ge(s["listed"], tb + 1)
                    if tb >= 2:
                        pe.wait_ge(s["gate_lo"], tb - 1)
                    for i in range(3):
                        mm = nc.tensor.transpose(psum[:, 4 + tb % 2, i * P:(i + 1) * P], out3[tb % 2][:, i, :], m.ident[:])
                    mm.then_inc(s["turned"], 1)

            @block.scalar
            def _(a):
                def exps(tb):
                    a.wait_ge(s["best_in"], tb + 1)
                    a.activation(best[tb % 2][:], best[tb % 2][:], ACT.Exp).then_inc(s["exp_done"], 1)

                exps(0)
                for tb in range(TB):
                    a.wait_ge(s["turned"], tb + 1)
                    bank, ts = psum[:, 4 + tb % 2, :], slice(tb * P, (tb + 1) * P)
                    a.copy(lists[:, 0:2, ts], bank[:, 0:2 * P].rearrange("p (a t) -> p a t", a=2)).then_inc(s["list_copied"], 1)
                    a.mul(lists[:, 2, ts], bank[:, 2 * P:3 * P], GSCALE).then_inc(s["list_copied"], 1)
                    if tb + 1 < TB:
                        exps(tb + 1)

            @block.vector
            def _(v):
                st = Steps(v, s["dve_step"])
                v.wait_ge(s["iota_in"], 16)
                st.then(v.tensor_copy(i16[:], numbers[:]))
                hkk = [P, PH, TOPK, TOPK]

                def low_part(tb):
                    v.wait_ge(s["list_copied"], 2 * tb + 2)
                    ts = slice(tb * P, (tb + 1) * P)
                    v.scalar_tensor_tensor(lists[:, 3, ts], psum[:, 4 + tb % 2, 2 * P:3 * P], GSCALE, lists[:, 2, ts], ALU.mult, ALU.subtract).then_inc(s["gate_lo"], 1)

                for tb in range(TB):
                    bt, o3 = best[tb % 2], out3[tb % 2]
                    c4 = cand[:].rearrange("p h (a b) -> p h a b", b=TOPK)
                    v4 = val[:, tb].rearrange("p (h s) k -> p h s k", s=2)
                    left = v4[:, :, 0, :].rearrange("p h (a b) -> p h a b", b=1).broadcast_to(hkk)
                    right = v4[:, :, 1, :].rearrange("p h (a b) -> p h a b", a=1).broadcast_to(hkk)
                    st.then(v.tensor_copy(idxf[:].rearrange("p h s k -> p (h s) k"), idx[:, tb]))
                    st.link(v.tensor_tensor(c4, left, right, ALU.add))
                    if tb >= 2:
                        v.wait_ge(s["turned"], tb - 1)
                    for h in range(PH):
                        top16(v, st, bt[:, h, :], pos[:, h, :], cand[:, h, :], rest[:])
                    st.settle()
                    fp = pos[:].rearrange("p h k -> p (h k)")
                    st.then(v.tensor_scalar(ab_i[:, 0, :], fp, 4, None, ALU.logical_shift_right))
                    st.then(v.tensor_scalar(ab_i[:, 1, :], fp, TOPK - 1, None, ALU.bitwise_and))
                    st.link(v.tensor_copy(den[:], bt[:, :, 0]))
                    v.tensor_tensor(bt[:], bt[:], den[:].rearrange("p (h k) -> p h k", k=1).broadcast_to([P, PH, TOPK]), ALU.subtract).then_inc(s["best_in"], 1)
                    st.link(v.tensor_copy(ab[:], ab_i[:]))
                    for i in range(2):
                        want = ab[:, i, :].rearrange("p (h k c) -> p h k c", h=PH, c=1).broadcast_to(hkk)
                        have = i16[:].rearrange("p (h k c) -> p h k c", h=1, k=1).broadcast_to(hkk)
                        index = idxf[:, :, i, :].rearrange("p h (k c) -> p h k c", k=1).broadcast_to(hkk)
                        st.link(v.tensor_tensor(hot[:], want, have, ALU.is_equal))
                        st.link(v.tensor_tensor(hot[:], hot[:], index, ALU.mult))
                        st.link(v.tensor_reduce(o3[:, i, :].rearrange("p (h k) -> p h k", h=PH), hot[:], AX, ALU.add))
                    v.wait_ge(s["exp_done"], tb + 1)
                    st.link(v.tensor_reduce(den[:], bt[:], AX, ALU.add))
                    st.link(v.reciprocal(den[:], den[:]))
                    v.tensor_tensor(o3[:, 2, :].rearrange("p (h k) -> p h k", h=PH), bt[:],
                                    den[:].rearrange("p (h k) -> p h k", k=1).broadcast_to([P, PH, TOPK]), ALU.mult).then_inc(s["listed"], 1)
                    v.wait_ge(s["listed"], tb + 1)
                    if tb:
                        low_part(tb - 1)
                low_part(TB - 1)


def expert_gates_stage(nc, m, io, lists, psum):
    BT = 16
    SPC = GCH // BT
    with ExitStack() as ctx, stage(nc, "iota_in", "iota_made", "hot", "weighed", "gate_mm", "gate_copied", "gate_out0", "gate_out1") as s:
        sb = lambda n, sh, dt=F16: ctx.enter_context(buffer(nc, n, sh, dt))
        iota = sb("iota", [P, P], F32)
        ids = sb("ids", [P, P, BT])
        hot_j = [sb(f"hot_j{i}", [P, P, BT]) for i in range(2)]
        hot_i = [sb(f"hot_i{i}", [P, P, BT]) for i in range(2)]
        part = [sb(f"part{i}", [P, 2, P, BT]) for i in range(2)]
        held = [sb(f"held{i}", [P, P, GCH], F32) for i in range(2)]
        out_sem = (s["gate_out0"], s["gate_out1"])
        with nc.Block() as block:
            @block.sync
            def _(sp):
                sp.dma_start(iota[:], io["c_iota"]).then_inc(s["iota_in"], 16)

                def store(c, p, first):
                    sp.wait_ge(s["gate_copied"], (c + 1) * SPC)
                    sp.dma_start(tile_at(io["g_scratch"], c), held[p][:].rearrange("p i t -> p (i t)")).then_inc(out_sem[p], 16)
                over_pairs(sp, T // GCH, store)
                for q in out_sem:
                    sp.wait_ge(q, 16 * (T // GCH // 2))

            @block.vector
            def _(v):
                v.wait_ge(s["iota_in"], 16)
                v.tensor_copy(ids[:], iota[:].rearrange("p (i t) -> p i t", t=1).broadcast_to([P, P, BT])).then_inc(s["iota_made"], 1)
                v.wait_ge(s["iota_made"], 1)

                def make(c, p, first):
                    for k in range(SPC):
                        n, b = c * SPC + k, k % 2
                        if not (first and p == 0 and k < 2):
                            v.wait_ge(s["gate_mm"], n - 1)
                        row = lambda x: lists[:, x:x + 1, bass.ds(c * GCH + k * BT, BT)].broadcast_to([P, P, BT])
                        v.tensor_tensor(hot_i[b][:], ids[:], row(0), ALU.is_equal).then_inc(s["hot"], 1)
                        v.tensor_tensor(hot_j[b][:], ids[:], row(1), ALU.is_equal).then_inc(s["hot"], 1)
                        v.wait_ge(s["hot"], n * 2 + 2)
                        for x in range(2):
                            v.tensor_tensor(part[b][:, x], hot_i[b][:], row(2 + x), ALU.mult).then_inc(s["weighed"], 1)
                over_pairs(v, T // GCH, make)

            @block.tensor
            def _(pe):
                def products(c, p, first):
                    for k in range(SPC):
                        n, b = c * SPC + k, k % 2
                        pe.wait_ge(s["weighed"], n * 2 + 2)
                        if not (first and p == 0 and k < 2):
                            pe.wait_ge(s["gate_copied"], n - 1)
                        for t in range(BT):
                            for x in range(2):
                                mm = nc.tensor.matmul(psum[:, 4 * b + t // 4, (t % 4) * P:(t % 4 + 1) * P], hot_j[b][:, :, t], part[b][:, x, :, t],
                                                      start=(x == 0), stop=(x == 1))
                        mm.then_inc(s["gate_mm"], 1)
                over_pairs(pe, T // GCH, products)

            @block.scalar
            def _(a):
                def copy(c, p, first):
                    if not first:
                        a.wait_ge(out_sem[p], (c - p) * 8)
                    for k in range(SPC):
                        n, b = c * SPC + k, k % 2
                        a.wait_ge(s["gate_mm"], n + 1)
                        a.activation(held[p][:, :, k * BT:(k + 1) * BT].rearrange("p i t -> p t i"),
                                     psum[:, 4 * b:4 * b + 4, :].rearrange("p a (t i) -> p (a t) i", i=P), ACT.Copy, scale=1.0 / GSCALE).then_inc(s["gate_copied"], 1)
                over_pairs(a, T // GCH, copy)


def experts_stage(nc, m, io, l, h_hi, h_lo, psum):
    NG = PK // GE
    with ExitStack() as ctx, stage(nc, "u_in0", "u_in1", "v_in0", "v_in1", "g_in0", "g_in1", "u_hi", "u_lo", "v_hi", "v_lo",
                                   "dot_mm", "gelu_done", "gated", "act_hi", "act_lo", "y_mm", "y_added") as s:
        sb = lambda n, sh, dt=F32: ctx.enter_context(buffer(nc, n, sh, dt))
        u = [sb(f"u{i}", [P, D]) for i in range(2)]
        uh = [sb(f"uh{i}", [P, KD, P], F32R) for i in range(2)]
        ul = [sb(f"ul{i}", [P, KD, P], F32R) for i in range(2)]
        vv = [sb(f"v{i}", [P, D]) for i in range(2)]
        vh = [sb(f"vh{i}", [P, GE, D], F32R) for i in range(2)]
        vl = [sb(f"vl{i}", [P, GE, D], F32R) for i in range(2)]
        ah = [sb(f"ah{i}", [P, GE, T], F32R) for i in range(2)]
        al = [sb(f"al{i}", [P, GE, T], F32R) for i in range(2)]
        ge = [sb(f"ge{i}", [P, T]) for i in range(2)]
        gate = [sb(f"gate{i}", [P, T // GCH, GE, GCH]) for i in range(2)]
        u_in, v_in, g_in = (s["u_in0"], s["u_in1"]), (s["v_in0"], s["v_in1"]), (s["g_in0"], s["g_in1"])
        row0 = l * PK
        fw = lambda t: t[:].rearrange("p k e -> p (k e)")
        flat = lambda t, r: t[:, r, :]
        with nc.Block() as block:
            @block.sync
            def _(sp):
                def load_u(n, early, par):
                    if not early:
                        sp.wait_ge(s["u_lo"], n - 1)
                    sp.dma_start(u[par][:], tile_at(io["peer_u"], row0 + n)).then_inc(u_in[par], 16)

                def load(g, p, first, last):
                    if first and p == 0:
                        load_u(0, True, 0)
                    if not first:
                        sp.wait_ge(s["gated"], (g - 1) * GE)
                    sp.dma_start(gate[p][:].rearrange("p c r t -> p c (r t)"),
                                 io["g_scratch"].rearrange("c p (i t) -> p c i t", t=GCH)[:, :, bass.ds(g * GE, GE), :].rearrange("p c i t -> p c (i t)")
                                 ).then_inc(g_in[p], 16)
                    for r in range(GE):
                        n = g * GE + r
                        if not (last and r == GE - 1):
                            load_u(n + 1, first and p == 0 and r == 0, (r + 1) % 2)
                        if not (first and p == 0 and r < 2):
                            sp.wait_ge(s["v_lo"], n - 1)
                        sp.dma_start(vv[r % 2][:], tile_at(io["peer_v"], row0 + n)).then_inc(v_in[r % 2], 16)
                over_groups(sp, NG, load)

            @block.tensor
            def _(pe):
                def dots(g, p, first):
                    for r in range(GE):
                        n = g * GE + r
                        pe.wait_ge(s["u_lo"], n + 1)
                        if not (first and p == 0):
                            pe.wait_ge(s["gelu_done"], n - 3)
                        three = [(uh, h_lo), (ul, h_hi), (uh, h_hi)]
                        for x, (w, h) in enumerate(three):
                            for k in range(KD):
                                mm = nc.tensor.matmul(psum[:, r, :], w[r % 2][:, k, :], h[:, k, :], start=(x == 0 and k == 0), stop=(x == 2 and k == KD - 1))
                        mm.then_inc(s["dot_mm"], 1)

                def sums(g, p, early):
                    pe.wait_ge(s["v_lo"], g * GE + GE)
                    pe.wait_ge(s["act_lo"], g * GE + GE)
                    for o in range(8):
                        b, half = o // 2, o % 2
                        if not (early and o < 4):
                            pe.wait_ge(s["y_added"], g * 8 + o - 3)
                        for r in range(GE):
                            for x, (w, q) in enumerate([(ah, vl), (al, vh), (ah, vh)]):
                                mm = nc.tensor.matmul(psum[:, 4 + o % 4, :], w[p][:, r, b * P:(b + 1) * P], q[p][:, r, half * W:(half + 1) * W],
                                                      start=(r == 0 and x == 0), stop=(r == GE - 1 and x == 2))
                        mm.then_inc(s["y_mm"], 1)

                def group(g, p, first, last):
                    dots(g, p, first)
                    if not (first and p == 0):
                        sums(g - 1, 1 - p, first)
                over_groups(pe, NG, group)
                sums(NG - 1, (NG - 1) % 2, False)

            @block.scalar
            def _(a):
                def high_u(n, k, early, par):
                    a.wait_ge(u_in[par], k)
                    if not early:
                        a.wait_ge(s["dot_mm"], n - 1)
                    a.copy(fw(uh[par]), u[par][:]).then_inc(s["u_hi"], 1)

                def group(g, p, first, last):
                    if first and p == 0:
                        high_u(0, 16, True, 0)
                    for r in range(GE):
                        n = g * GE + r
                        if not (last and r == GE - 1):
                            high_u(n + 1, g * 32 + 16 * ((r + 1) // 2) + 16, first and p == 0 and r == 0, (r + 1) % 2)
                        a.wait_ge(v_in[r % 2], g * 32 + 16 * (r // 2) + 16)
                        if not first:
                            a.wait_ge(s["y_mm"], (g - 1) * 8)
                        a.copy(vh[p][:, r, :], vv[r % 2][:]).then_inc(s["v_hi"], 1)
                        a.wait_ge(s["dot_mm"], n + 1)
                        if not (first and p == 0 and r < 2):
                            a.wait_ge(s["act_lo"], n - 1)
                        a.activation(ge[r % 2][:], psum[:, r, :], ACT.Gelu_apprx_tanh).then_inc(s["gelu_done"], 1)
                        a.wait_ge(s["gated"], n + 1)
                        a.copy(ah[p][:, r, :], ge[r % 2][:]).then_inc(s["act_hi"], 1)
                over_groups(a, NG, group)

            @block.vector
            def _(v):
                def low_u(n, par):
                    v.wait_ge(s["u_hi"], n + 1)
                    v.tensor_tensor(fw(ul[par]), u[par][:], fw(uh[par]).bitcast(F32), ALU.subtract).then_inc(s["u_lo"], 1)

                def add(g, early):
                    for o in range(8):
                        b, half = o // 2, o % 2
                        v.wait_ge(s["y_mm"], g * 8 + o + 1)
                        if not early:
                            v.wait_ge(s["y_added"], (g - 1) * 8 + o + 1)
                        x = m.X[:, b, half * W:(half + 1) * W]
                        v.tensor_tensor(x, psum[:, 4 + o % 4, :], x, ALU.add).then_inc(s["y_added"], 1)

                def group(g, p, first, last):
                    if first and p == 0:
                        low_u(0, 0)
                    v.wait_ge(g_in[p], 16 if first else (g - p) * 8 + 16)
                    for r in range(GE):
                        n = g * GE + r
                        if not (last and r == GE - 1):
                            low_u(n + 1, (r + 1) % 2)
                        v.wait_ge(s["v_hi"], n + 1)
                        v.tensor_tensor(vl[p][:, r, :], vv[r % 2][:], vh[p][:, r, :].bitcast(F32), ALU.subtract).then_inc(s["v_lo"], 1)
                        v.wait_ge(s["gelu_done"], n + 1)
                        act = ge[r % 2][:].rearrange("p (c t) -> p c t", t=GCH)
                        v.tensor_tensor(act, act, gate[p][:, :, r, :], ALU.mult).then_inc(s["gated"], 1)
                        v.wait_ge(s["act_hi"], n + 1)
                        v.tensor_tensor(al[p][:, r, :], ge[r % 2][:], ah[p][:, r, :].bitcast(F32), ALU.subtract).then_inc(s["act_lo"], 1)
                    if not (first and p == 0):
                        add(g - 1, first)
                over_groups(v, NG, group)
                add(NG - 1, False)


def final_stage(nc, m, io):
    with ExitStack() as ctx, stage(nc, "gain_in", "sumsq", "dve_step", "root", "ready", "stored") as s:
        gain = ctx.enter_context(buffer(nc, "gain", [P, D], F32))
        junk = ctx.enter_context(buffer(nc, "junk", [P, D], F32))
        ss = ctx.enter_context(buffer(nc, "fss", [P, 2, TB], F32))
        with nc.Block() as block:
            @block.sync
            def _(sp):
                sp.dma_start(gain[:], io["norm_final"].partition_broadcast(P)).then_inc(s["gain_in"], 16)
                for b in range(TB):
                    sp.wait_ge(s["ready"], b + 1)
                    sp.dma_start(io["out"][b * P:(b + 1) * P, :], m.X[:, b, :]).then_inc(s["stored"], 16)
                sp.wait_ge(s["stored"], 16 * TB)

            @block.scalar
            def _(a):
                for b in range(TB):
                    if b:
                        a.wait_ge(s["sumsq"], b)
                    a.activation(junk[:], m.X[:, b, :], ACT.Square, accum_out=ss[:, 0, b:b + 1]).then_inc(s["sumsq"], 1)
                a.wait_ge(s["dve_step"], 1)
                a.activation(ss[:, 1, :], ss[:, 0, :], ACT.Sqrt).then_inc(s["root"], 1)

            @block.vector
            def _(v):
                st = Steps(v, s["dve_step"])
                v.wait_ge(s["sumsq"], TB)
                st.then(v.tensor_scalar(ss[:, 0, :], ss[:, 0, :], 1.0 / D, EPS, ALU.mult, ALU.add))
                v.wait_ge(s["root"], 1)
                v.wait_ge(s["gain_in"], 16)
                st.link(v.reciprocal(ss[:, 0, :], ss[:, 1, :]))
                for b in range(TB):
                    v.scalar_tensor_tensor(m.X[:, b, :], m.X[:, b, :], ss[:, 0, b:b + 1], gain[:], ALU.mult, ALU.mult).then_inc(s["ready"], 1)


def copy_to(a, dst):
    def copy(t, b, bank):
        n = bank.shape[-1]
        return a.copy(dst[:, bass.ds(t * 4 + b, 1), 0:n].rearrange("p a n -> p (a n)"), bank)
    return copy


def load_small_stage(nc, io, l, sm):
    with stage(nc, "small_in") as s:
        with nc.Block() as block:
            @block.sync
            def _(sp):
                sp.dma_start(sm[:], tile_at(io["small"], l)).then_inc(s["small_in"], 16)
                sp.wait_ge(s["small_in"], 16)


def mixer_layer(nc, m, io, l, sm, psum):
    a = nc.scalar
    part = lambda t, i: t[:, 4 * i:4 * i + 4, :]
    with buffer(nc, "fm", [P, 28, T], F32) as fm:
        with buffer(nc, "tm", [P, 2 * TB, W], F32) as tm:
            with hi_lo(nc, "hT", [P, KD, T]) as h, ExitStack() as ctx:
                raw = two_tiles(nc, ctx)
                w_fm = Weights(m, raw, 0, 7, lambda t: tile_at(io["w_fm"], l * 7 + t))
                w_tm = Weights(m, raw, 1, 2, lambda t: tile_at(io["w_tm"], l * 2 + t))
                norm_stage(nc, m, m.X, TB, sm[:, 0:KD], h, psum, w_fm)
                linear_stage(nc, "fm", w_fm, h, 4, T, psum, copy_to(a, fm), following=w_tm)
                linear_stage(nc, "tm", w_tm, h, 4, T, psum, copy_to(a, tm))
            hgrn_stage(nc, m, l, part(fm, 0), part(fm, 1), part(fm, 2), part(tm, 0), part(fm, 0), psum, io, sm)
            retention_stage(nc, m, part(fm, 3), part(fm, 4), part(fm, 5), part(tm, 1), part(fm, 4), psum, io)
            with ExitStack() as ctx:
                sb = lambda n, sh: ctx.enter_context(buffer(nc, n, sh, F32))
                tabs = SsmTables(sin=sb("tsin", [P, G5 * N5]), cos=sb("tcos", [P, G5 * N5]), decay=sb("tdec", [P, G5 * N5]),
                                       gb=sb("gb", [P, G5, J5, C5]), pc=sb("pc", [P, G5, 2 * J5, C5]))
                ssm_tables_stage(nc, m, io, l, sm, tabs)
                ssm_stage(nc, m, sm, tabs, part(fm, 6), [part(fm, i) for i in (1, 3, 5)], part(fm, 2),
                          tm[0:N5, :, :], psum)
        glu_stage(nc, io, l, part(fm, 1), part(fm, 2), sm, psum)
        merged = lambda d: fm[:, d + (4 if d < 4 else 8), :]
        with buffer(nc, "gates", [P, 3 * KD, T], F32) as gates:
            with hi_lo(nc, "hT", [P, KD, T]) as h, ExitStack() as ctx:
                w_gate = Weights(m, two_tiles(nc, ctx), 0, 6, lambda t: tile_at(io["w_gate"], l * 6 + t))
                norm_stage(nc, m, m.X, TB, sm[:, 0:KD], h, psum, w_gate)
                gates_stage(nc, w_gate, h, sm, gates, psum)
            merge_stage(nc, io, l, [part(fm, 0), part(fm, 2), part(fm, 4)], gates, merged, psum)
        with hi_lo(nc, "merged", [P, KD, T]) as parts, ExitStack() as ctx:
            w_out = Weights(m, two_tiles(nc, ctx), 1, 2, lambda t: tile_at(io["w_out"], l * 2 + t))
            split_stage(nc, merged, parts, w_out)
            residual_stage(nc, m, w_out, parts, psum)


def split_stage(nc, src, dst, weights=None):
    hi, lo = dst
    with stage(nc, "hi_done", "lo_done") as s:
        with nc.Block() as block:
            @block.sync
            def _(sp):
                if weights is not None:
                    weights.start(sp)

            @block.scalar
            def _(a):
                for k in range(KD):
                    a.copy(hi[:, k, :], src(k)).then_inc(s["hi_done"], 1)

            @block.vector
            def _(v):
                for k in range(KD):
                    v.wait_ge(s["hi_done"], k + 1)
                    v.tensor_tensor(lo[:, k, :], src(k), hi[:, k, :].bitcast(F32), ALU.subtract).then_inc(s["lo_done"], 1)


def residual_stage(nc, m, weights, act, psum):
    v = nc.vector

    def add(t, b, bank):
        x = m.X[:, b, t * W:(t + 1) * W]
        return v.tensor_tensor(x, bank, x, ALU.add)
    linear_stage(nc, "tm", weights, act, TB, W, psum, add, on="vector")


def cross_layer(nc, m, io, l, sm, psum):
    a = nc.scalar
    with ExitStack() as ctx:
        sb = lambda n, sh, dt=F32: ctx.enter_context(buffer(nc, n, sh, dt))
        kT = sb("kT", [P, KD, MEM])
        v_tm = sb("v_tm", [P, MB, D])
        qT = sb("qT", [P, KD, T])
        raw = two_tiles(nc, ctx)
        w_k, w_v, w_q, w_o = (Weights(m, raw, i, 2, lambda t, name=name: tile_at(io[name], l * 2 + t))
                              for i, name in enumerate(("xa_k", "xa_v", "xa_q", "xa_o")))
        c = COL["norm_mem"][0]
        with hi_lo(nc, "memT", [P, KD, MEM]) as memT:
            with buffer(nc, "mem", [P, MB, D], F32) as mem:
                norm_stage(nc, m, mem, MB, sm[:, c:c + KD], memT, psum, w_k, load=[(mem[:], io["mem"])])
            linear_stage(nc, "fm", w_k, memT, 4, MEM, psum, copy_to(a, kT), following=w_v)

            def v_copy(t, b, bank):
                return a.copy(v_tm[:, b, t * W:(t + 1) * W], bank)
            linear_stage(nc, "tm", w_v, memT, MB, W, psum, v_copy, following=w_q)
        c = COL["norm_cross"][0]
        with hi_lo(nc, "hT", [P, KD, T]) as h:
            norm_stage(nc, m, m.X, TB, sm[:, c:c + KD], h, psum, None)
            linear_stage(nc, "fm", w_q, h, 4, T, psum, copy_to(a, qT), following=w_o)
        with hi_lo(nc, "oT", [P, KD, T]) as o_parts:
            with buffer(nc, "oT", [P, KD, T], F32) as oT:
                attend_stage(nc, m, qT, kT, v_tm, oT, psum)
                split_stage(nc, lambda k: oT[:, k, :], o_parts)
            residual_stage(nc, m, w_o, o_parts, psum)


def expert_layer(nc, m, io, l, sm, psum):
    a = nc.scalar
    c = COL["norm_ffn"][0]
    with hi_lo(nc, "h", [P, KD, T]) as h:
        with buffer(nc, "lists", [P, 4, T], F16) as lists:
            with buffer(nc, "val", [P, TB, 2 * PH, TOPK], F32) as val, buffer(nc, "idx", [P, TB, 2 * PH, TOPK], U32) as idx:
                with ExitStack() as ctx:
                    w_query = Weights(m, two_tiles(nc, ctx), 0, 4, lambda t: tile_at(io["peer_wq"], l * 4 + t))
                    norm_stage(nc, m, m.X, TB, sm[:, c:c + KD], h, psum, w_query)
                    keys_stage(nc, io, l, w_query, h, val, idx, psum)
                choose_stage(nc, m, io, val, idx, lists, psum)
            expert_gates_stage(nc, m, io, lists, psum)
        experts_stage(nc, m, io, l, h[0], h[1], psum)


def trunk(nc, io):
    m = Resident()
    m.X = nc.alloc_sbuf_tensor("X", [P, TB, D], F32)
    m.ident = nc.alloc_sbuf_tensor("ident", [P, P], F32)
    m.perm = nc.alloc_sbuf_tensor("perm", [P, P], F32)
    m.ones = nc.alloc_sbuf_tensor("ones", [P, P], F32)
    m.cols = nc.alloc_sbuf_tensor("cols", [P, 3], F32)
    m.sin = nc.alloc_sbuf_tensor("sin", [P, T], F32)
    m.cos = nc.alloc_sbuf_tensor("cos", [P, T], F32)
    m.lb_all = nc.alloc_sbuf_tensor("lb_all", [P, L, H], F32)
    sm = nc.alloc_sbuf_tensor("small", [P, NSMALL], F32)
    psum = nc.alloc_psum_tensor("psum", [P, 8, 512], F32)
    _pool[:] = [nc.alloc_semaphore(f"stage_sem{i}") for i in range(28)]
    m.weights_in = [[nc.alloc_semaphore(f"weights_in{i}{p}") for p in range(2)] for i in range(2)]
    setup_stage(nc, io, m)
    with nc.Fori(0, L) as l:
        load_small_stage(nc, io, l, sm)
        mixer_layer(nc, m, io, l, sm, psum)
        cross_layer(nc, m, io, l, sm, psum)
        expert_layer(nc, m, io, l, sm, psum)
    final_stage(nc, m, io)



def _constants():
    f = np.float32
    half = P // 2
    inv = (np.float32(10000.0) ** (-np.arange(half, dtype=f) / f(half))).astype(f)
    p = np.arange(P)
    perm = np.zeros((P, P), f)
    perm[p, (p + half) % P] = 1
    sign = np.where(p < half, -1.0, 1.0).astype(f)
    s_, t_ = np.meshgrid(p, p, indexing="ij")
    masks = [s_ == t_]
    for w in LEVELS:
        masks.append((s_ // (2 * w) == t_ // (2 * w)) & (s_ % (2 * w) < w) & (t_ % (2 * w) >= w))
    masks = np.stack(masks, 1).astype(np.int32)
    rel = np.arange(T)[None, :] - p[:, None]
    log_g = np.log1p(-np.exp2(-5.0 - np.arange(H)))
    dmat = np.stack([np.where(rel >= 0, np.exp(lg * np.maximum(rel, 0)), 0.0) for lg in log_g], 1) * P ** -0.5
    return {"c_ident": np.eye(P, dtype=f), "c_perm": perm, "c_cols": np.stack([np.tile(inv, 2), sign, -sign], 1),
            "c_masks": masks, "c_dmat": dmat.astype(f), "c_nvec": np.tile(np.arange(N5, dtype=f), (P, 1)),
            "c_iota": np.tile(np.arange(P, dtype=f), (P, 1))}


def _layout(a):
    def tiles(w, order=None):
        w = w.reshape(L, -1, P, w.shape[2] // W, W).transpose(0, 3, 2, 1, 4)
        w = w if order is None else w[:, order]
        return np.ascontiguousarray(w).reshape(w.shape[0] * w.shape[1], P, -1)

    def cols(v):
        return v.reshape(L, -1, P).transpose(0, 2, 1)
    both = lambda v: np.concatenate([v, v], 1)
    lam = lambda v: both(v.transpose(0, 2, 1))
    small = np.concatenate([
        cols(a["norm_mix"]), cols(a["norm_cross"]), cols(a["norm_mem"]), cols(a["norm_ffn"]), cols(a["b_gate"]),
        cols(a["hgrn_norm"]), cols(a["s5_b_glu"]),
        np.tile(a["s5_d"].reshape(L, G5, C5).transpose(0, 2, 1), (1, J5, 1)),
        lam(a["s5_lambda_re"]), lam(a["s5_lambda_im"]), np.repeat(a["s5_log_step"][:, None, :], P, 1)], 2)
    br, bi = (a[f"s5_b_{x}"].transpose(0, 2, 1, 3) for x in ("re", "im"))
    cr, ci = (a[f"s5_c_{x}"].transpose(0, 3, 1, 2) for x in ("re", "im"))
    cat = lambda x, y: np.concatenate([x, y], 1)
    bc = np.stack([cat(br, bi), cat(bi, br), cat(cr, ci), cat(ci, cr)], 2).reshape(L, P, -1)
    w_in = a["w_in"]
    rows = lambda v: v.reshape(-1, P, v.shape[-1]).transpose(1, 0, 2)
    wbr = a["w_branch"].reshape(L, 3, 4, P, 2, W).transpose(0, 4, 1, 3, 2, 5).reshape(L * 6, P, -1)
    u = a["peer_u"].reshape(L * PK, P, KD, P).transpose(0, 3, 2, 1).reshape(L * PK, P, -1)
    return {
        "x": rows(a["x"][0]), "mem": rows(a["mem"][0]), "positions": a["positions"][0],
        "hgrn_lb": a["hgrn_lb"].reshape(L, H, P).transpose(2, 0, 1), "small": small, "s5_bc": bc,
        "w_fm": tiles(w_in[:, :, :15 * W], [0, 1, 3, 5, 6, 8, 4]), "w_tm": tiles(w_in[:, :, :15 * W], [2, 7]),
        "w_gate": tiles(w_in[:, :, 9 * W:]), "w_glu": tiles(a["s5_w_glu"]), "w_branch": wbr, "w_out": tiles(a["w_out"]),
        "xa_q": tiles(a["xa_wq"]), "xa_k": tiles(a["xa_wkv"][:, :, :D]), "xa_v": tiles(a["xa_wkv"][:, :, D:]),
        "xa_o": tiles(a["xa_wo"]), "peer_wq": tiles(a["peer_wq"]),
        "keys": a["peer_keys"].reshape(L, 2 * PH, PK, P).transpose(0, 3, 1, 2).reshape(L, P, -1),
        "peer_u": u, "peer_v": a["peer_v"].reshape(L * PK, P, D), "norm_final": a["norm_final"],
    }


def kernel(**inputs):
    import concourse.bacc as bacc
    from concourse.bass_utils import run_bass_kernel_spmd

    nc = bacc.Bacc("TRN2", target_bir_lowering=False, num_devices=1)
    arrays = {}
    laid = _layout({k: np.asarray(v) for k, v in inputs.items()})
    laid.update(_constants())
    aps = {}
    for name, a in laid.items():
        a = np.ascontiguousarray(a)
        arrays[f"in_{name}"] = a
        aps[name] = nc.dram_tensor(f"in_{name}", a.shape, mybir.dt.from_np(a.dtype), kind="ExternalInput").ap()
    aps["out"] = nc.dram_tensor("out_x", (T, D), F32, kind="ExternalOutput").ap()
    aps["g_scratch"] = nc.dram_tensor("g_scratch", (T // GCH, P, P * GCH), F32, kind="Internal").ap()
    trunk(nc, aps)
    r = run_bass_kernel_spmd(nc, [arrays], core_ids=[0])
    return np.asarray(r.results[0]["out_x"]).reshape(1, T, D)
```

```python
import itertools
from contextlib import ExitStack, contextmanager

import numpy as np

import concourse.bass as bass
from concourse import mybir

P = 128
D = 1024
T = 512
L = 2
TB = T // P
KD = D // P
W = 512
H = 4
MEM = 256
MB = MEM // P
EPS = 1e-6
G5, C5, S5P = 32, 16, 64
J5, N5 = 8, T // 8
PH, PK, TOPK = 8, 128, 16
SLOTS = PH * TOPK
GCH = 64
GSCALE = 4096.0
GE = 4
LEVELS = [64, 32, 16, 8, 4, 2, 1]

F32 = mybir.dt.float32
F32R = mybir.dt.float32r
F16 = mybir.dt.float16
I32 = mybir.dt.int32
U32 = mybir.dt.uint32
ALU = mybir.AluOpType
ACT = mybir.ActivationFunctionType
AX = mybir.AxisListType.X

TWO_PI = 2.0 * np.pi
C1 = 6.28125
C2 = float(np.float32(round((TWO_PI - C1) * 2**21) / 2**21))
C3 = float(np.float32(TWO_PI - C1 - C2))
ROUND = 1.5 * 2.0**23
ROUND13 = 1.5 * 2.0**10
PI_IN = 3.1415925

_SMALL = [("norm_mix", KD), ("norm_cross", KD), ("norm_mem", KD), ("norm_ffn", KD), ("b_gate", 3 * KD),
          ("hgrn_norm", H), ("b_glu", H), ("s5_d", G5), ("lam_re", G5), ("lam_im", G5), ("log_step", G5)]
COL, _n = {}, 0
for _name, _w in _SMALL:
    COL[_name] = (_n, _n + _w)
    _n += _w
NSMALL = _n


HC = H * TB

_serial = itertools.count()
_pool = []


def buffer(nc, name, shape, dtype):
    return nc.sbuf_tensor(f"{name}_{next(_serial)}", shape, dtype)


@contextmanager
def stage(nc, *names, weights=None):
    assert len(names) <= len(_pool)
    yield dict(zip(names, _pool))
    with nc.Block() as block:
        @block.sync
        def _(sp):
            sp.sem_clear(range(_pool[0].num, _pool[len(names) - 1].num + 1))
            if weights is not None:
                sp.sem_clear(range(weights.arrived[0].num, weights.arrived[1].num + 1))


class Resident:
    pass


def sums_of_head(nc, m, bank, x, h):
    for c in range(TB):
        row = h * TB + c
        mm = nc.tensor.matmul(bank, m.one_col[:, HC - 1 - row:2 * HC - 1 - row], x[:, c * P:(c + 1) * P], start=(row == 0), stop=(row == HC - 1))
    return mm


def spread_head(nc, m, bank, rows, h):
    for c in range(TB):
        row = h * TB + c
        mm = nc.tensor.matmul(bank[:, c * P:(c + 1) * P], m.ident[0:HC, row:row + 1].broadcast_to([HC, P]), rows, start=True, stop=True)
    return mm


class SsmTables:

    def __init__(self, sin, cos, decay, gb, pc):
        self.sin, self.cos, self.decay, self.gb, self.pc = sin, cos, decay, gb, pc


class Steps:

    def __init__(self, eng, sem):
        self.eng, self.sem, self.n = eng, sem, 0

    def then(self, ins):
        ins.then_inc(self.sem, 1)
        self.n += 1
        return self.n

    def settle(self):
        self.eng.wait_ge(self.sem, self.n)

    def reach(self, n):
        self.eng.wait_ge(self.sem, n)

    def link(self, ins):
        self.then(ins)
        self.settle()


def tile_at(dram, index):
    return dram[bass.ds(index, 1)].rearrange("a p n -> (a p) n")


def over_pairs(eng, n, body):
    for p in range(min(2, n)):
        body(p, p, True)
    pairs = n // 2
    if pairs > 1:
        with eng.Fori(1, pairs) as i:
            for p in range(2):
                body(i * 2 + p, p, False)
    if n > 2 and n % 2:
        body(n - 1, 0, False)


def over_groups(eng, n, body):
    for p in range(2):
        body(p, p, True, False)
    with eng.Fori(1, n // 2 - 1) as i:
        for p in range(2):
            body(i * 2 + p, p, False, False)
    for p in range(2):
        body(n - 2 + p, p, False, p == 1)


class Weights:

    def __init__(self, m, raw, turn, n, src, depth=KD):
        self.raw, self.arrived, self.n, self.src = [x[:, 0:depth, :] for x in raw], m.weights_in[turn % 2], n, src

    def load(self, sp, t, p):
        sp.dma_start(self.raw[p].rearrange("p k n -> p (k n)"), self.src(t)).then_inc(self.arrived[p], 16)

    def start(self, sp):
        for p in range(2):
            self.load(sp, p, p)


def two_tiles(nc, ctx):
    return [ctx.enter_context(buffer(nc, f"w{i}", [P, KD, W], F32)) for i in range(2)]


class Linear:

    def __init__(self, nc, ctx, s, kind, weights, act, nb, N, psum):
        self.nc, self.s, self.kind, self.n, self.weights = nc, s, kind, weights.n, weights
        self.act, self.nb, self.N, self.ps = act, nb, N, psum
        self.raw, self.ready = weights.raw, weights.arrived
        self.hi = [ctx.enter_context(buffer(nc, f"w_hi{i}", [P, KD * P], F32R)) for i in range(2)]
        self.lo = [ctx.enter_context(buffer(nc, f"w_lo{i}", [P, KD * P], F32R)) for i in range(2)]

    def unit_of(self, p, q):
        return self.raw[p][:, :, q * P:(q + 1) * P] if self.kind == "fm" else self.raw[p][:, 2 * q:2 * q + 2, :]

    def shaped(self, x):
        return x[:].rearrange("p (k n) -> p k n", n=P if self.kind == "fm" else W)

    def arrivals(self, t, p, first):
        return 16 if first else (t - p) * 8 + 16

    def sync(self, sp, following=None):
        def load(t, p, first):
            if not first:
                sp.wait_ge(self.s["lo_done"], (t - 1) * 4)
                self.weights.load(sp, t, p)
        over_pairs(sp, self.n, load)
        if following is not None:
            for t in (self.n, self.n + 1):
                sp.wait_ge(self.s["lo_done"], (t - 1) * 4)
                following.load(sp, t % 2, t % 2)

    def tensor(self, pe):
        def tile(t, p, first):
            for q in range(4):
                self.unit(pe, t, p, first, q)
        over_pairs(pe, self.n, tile)

    def unit(self, pe, t, p, first, q):
        matmul = self.nc.tensor.matmul
        a_hi, a_lo = self.act
        pe.wait_ge(self.s["lo_done"], t * 4 + q + 1)
        w_hi, w_lo = self.shaped(self.hi[q % 2]), self.shaped(self.lo[q % 2])
        if self.kind == "fm":
            if not (first and p == 0):
                pe.wait_ge(self.s["evac_done"], (t - 1) * 4 + q + 1)
            three = [(w_hi, a_lo), (w_lo, a_hi), (w_hi, a_hi)]
            for x, (w, a) in enumerate(three):
                for k in range(KD):
                    mm = matmul(self.ps[:, q, 0:self.N], w[:, k, :], a[:, k, 0:self.N],
                                start=(x == 0 and k == 0), stop=(x == 2 and k == KD - 1))
        else:
            three = [(w_lo, a_hi), (w_hi, a_lo), (w_hi, a_hi)]
            for b in range(self.nb):
                if q == 0 and not first:
                    pe.wait_ge(self.s["evac_done"], (t - 2) * self.nb + b + 1)
                for x, (w, a) in enumerate(three):
                    for k in range(2):
                        mm = matmul(self.ps[:, 4 * p + b, :], a[:, 2 * q + k, b * P:(b + 1) * P], w[:, k, :],
                                    start=(q == 0 and x == 0 and k == 0), stop=(q == 3 and x == 2 and k == 1))
        mm.then_inc(self.s["unit_mm"], 1)

    def high(self, a, t, p, first, q):
        if q == 0:
            a.wait_ge(self.ready[p], self.arrivals(t, p, first))
        if not (first and p == 0 and q < 2):
            a.wait_ge(self.s["unit_mm"], t * 4 + q - 1)
        a.copy(self.shaped(self.hi[q % 2]), self.unit_of(p, q)).then_inc(self.s["hi_done"], 1)

    def low(self, v, t, p, first, q):
        v.wait_ge(self.s["hi_done"], t * 4 + q + 1)
        v.tensor_tensor(self.shaped(self.lo[q % 2]), self.unit_of(p, q), self.shaped(self.hi[q % 2]).bitcast(F32),
                        ALU.subtract).then_inc(self.s["lo_done"], 1)

    def block_out(self, eng, t, p, b, copy):
        eng.wait_ge(self.s["unit_mm"], t * 4 + (b + 1 if self.kind == "fm" else 4))
        bank = b if self.kind == "fm" else 4 * p + b
        copy(t, b, self.ps[:, bank, 0:self.N]).then_inc(self.s["evac_done"], 1)

    def blocks_behind(self, eng, t, p, first, q, copy):
        if copy is None:
            return
        if self.kind == "fm" and q:
            self.block_out(eng, t, p, q - 1, copy)
        elif not (first and p == 0):
            if self.kind == "fm":
                self.block_out(eng, t - 1, 1 - p, 3, copy)
            elif q < self.nb:
                self.block_out(eng, t - 1, 1 - p, q, copy)

    def last_blocks(self, eng, copy):
        if copy is not None:
            for b in range(3 if self.kind == "fm" else 0, self.nb):
                self.block_out(eng, self.n - 1, (self.n - 1) % 2, b, copy)

    def scalar(self, a, copy=None):
        def tile(t, p, first):
            for q in range(4):
                self.high(a, t, p, first, q)
                self.blocks_behind(a, t, p, first, q, copy)
        over_pairs(a, self.n, tile)
        self.last_blocks(a, copy)

    def vector(self, v, copy=None):
        def tile(t, p, first):
            for q in range(4):
                self.low(v, t, p, first, q)
                self.blocks_behind(v, t, p, first, q, copy)
        over_pairs(v, self.n, tile)
        self.last_blocks(v, copy)


LINEAR_SEMS = ("hi_done", "lo_done", "unit_mm", "evac_done")


def reduce_angle(v, st, out, ang, tmp):
    st.link(v.tensor_scalar(tmp, ang, 1.0 / TWO_PI, ROUND, ALU.mult, ALU.add))
    st.link(v.tensor_scalar(tmp, tmp, -ROUND, None, ALU.add))
    st.link(v.scalar_tensor_tensor(out, tmp, -C1, ang, ALU.mult, ALU.add))
    st.link(v.scalar_tensor_tensor(out, tmp, -C2, out, ALU.mult, ALU.add))
    st.link(v.scalar_tensor_tensor(out, tmp, -C3, out, ALU.mult, ALU.add))
    st.link(v.tensor_scalar(out, out, PI_IN, -PI_IN, ALU.min, ALU.max))


def cos_argument(v, st, out, red, tmp):
    st.link(v.tensor_scalar(out, red, float(np.pi / 2), None, ALU.add))
    st.link(v.tensor_scalar(tmp, out, float(np.pi), -TWO_PI, ALU.is_gt, ALU.mult))
    st.link(v.tensor_tensor(out, out, tmp, ALU.add))
    st.link(v.tensor_scalar(out, out, PI_IN, -PI_IN, ALU.min, ALU.max))


def setup_stage(nc, io, m):
    with ExitStack() as ctx, stage(nc, "loaded", "dve_step", "angles_ready", "trig_ready") as s:
        pos_i = ctx.enter_context(buffer(nc, "pos_i", [P, T], I32))
        ang = ctx.enter_context(buffer(nc, "ang", [P, T], F32))
        tmp = ctx.enter_context(buffer(nc, "tmp", [P, T], F32))
        red = ctx.enter_context(buffer(nc, "red", [P, T], F32))
        cred = ctx.enter_context(buffer(nc, "cred", [P, T], F32))
        lbs = ctx.enter_context(buffer(nc, "lbs", [P, L, H], F32))
        lbt = ctx.enter_context(buffer(nc, "lbt", [P, 2, H], F32))
        loads = [(pos_i[:], io["positions"].partition_broadcast(P)), (m.X[:], io["x"]), (m.ident[:], io["c_ident"]), (m.perm[:], io["c_perm"]),
                 (m.cols[:], io["c_cols"]), (lbs[:], io["hgrn_lb"])]
        with nc.Block() as block:
            @block.sync
            def _(sp):
                for dst, src in loads:
                    sp.dma_start(dst, src).then_inc(s["loaded"], 16)

            @block.vector
            def _(v):
                st = Steps(v, s["dve_step"])
                v.wait_ge(s["loaded"], 16 * len(loads))
                st.then(v.memset(m.ones[:], 1.0))
                st.link(v.memset(m.one_col[:], 0.0))
                st.then(v.memset(m.one_col[:, HC - 1:HC], 1.0))
                st.link(v.tensor_copy(ang[:], pos_i[:]))
                st.link(v.tensor_scalar(ang[:], ang[:], m.cols[:, 0:1], None, ALU.mult))
                reduce_angle(v, st, red[:], ang[:], tmp[:])
                cos_argument(v, st, cred[:], red[:], tmp[:])
                st.link(v.tensor_tensor(lbt[:, 0, :], lbs[:, 0, :], lbs[:, 1, :], ALU.max))
                st.then(v.tensor_tensor(lbs[:, 0, :], lbs[:, 0, :], lbt[:, 0, :], ALU.subtract))
                v.tensor_tensor(lbs[:, 1, :], lbs[:, 1, :], lbt[:, 0, :], ALU.subtract).then_inc(s["angles_ready"], 1)
                v.wait_ge(s["trig_ready"], 4)
                st.link(v.tensor_tensor(lbt[:, 0, :], lbs[:, 0, :], lbs[:, 1, :], ALU.add))
                st.link(v.reciprocal(lbt[:, 1, :], lbt[:, 0, :]))
                st.link(v.memset(m.lb_all[:, 0, :], 0.0))
                st.link(v.tensor_tensor(m.lb_all[:, 1, :], lbs[:, 1, :], lbt[:, 1, :], ALU.mult))
                st.link(v.tensor_scalar(m.sin[:], m.sin[:], m.cols[:, 1:2], None, ALU.mult))

            @block.scalar
            def _(a):
                a.wait_ge(s["angles_ready"], 1)
                a.activation(m.sin[:], red[:], ACT.Sin).then_inc(s["trig_ready"], 1)
                a.activation(m.cos[:], cred[:], ACT.Sin).then_inc(s["trig_ready"], 1)
                a.activation(lbs[:, 0, :], lbs[:, 0, :], ACT.Exp).then_inc(s["trig_ready"], 1)
                a.activation(lbs[:, 1, :], lbs[:, 1, :], ACT.Exp).then_inc(s["trig_ready"], 1)


def norm_stage(nc, m, src, nblk, gain, dst, psum, weights, load=()):
    d_hi, d_lo = dst
    with ExitStack() as ctx, stage(nc, "x_ready", "sumsq", "dve_step", "root", "scaled", "turned", "hi_done") as s:
        xn = ctx.enter_context(buffer(nc, "xn", [P, nblk, D], F32))
        ss = ctx.enter_context(buffer(nc, "ss", [P, TB], F32))
        rs = ctx.enter_context(buffer(nc, "rs", [P, TB], F32))
        with nc.Block() as block:
            @block.sync
            def _(sp):
                for dst_, src_ in load:
                    sp.dma_start(dst_, src_).then_inc(s["x_ready"], 16)
                if weights is not None:
                    weights.start(sp)

            @block.scalar
            def _(a):
                if load:
                    a.wait_ge(s["x_ready"], 16 * len(load))
                for b in range(nblk):
                    a.activation(xn[:, b, :], src[:, b, :], ACT.Square, accum_out=ss[:, b:b + 1]).then_inc(s["sumsq"], 1)
                a.wait_ge(s["dve_step"], 1)
                a.activation(rs[:, 0:nblk], ss[:, 0:nblk], ACT.Sqrt).then_inc(s["root"], 1)
                for k in range(KD):
                    a.wait_ge(s["turned"], k + 1)
                    a.activation(d_hi[:, k, 0:nblk * P], psum[:, k, 0:nblk * P], ACT.Copy, scale=gain[:, k:k + 1]).then_inc(s["hi_done"], 1)

            @block.vector
            def _(v):
                v.wait_ge(s["sumsq"], nblk)
                if load:
                    v.wait_ge(s["x_ready"], 16 * len(load))
                st = Steps(v, s["dve_step"])
                st.then(v.tensor_scalar(ss[:, 0:nblk], ss[:, 0:nblk], 1.0 / D, EPS, ALU.mult, ALU.add))
                v.wait_ge(s["root"], 1)
                st.link(v.reciprocal(ss[:, 0:nblk], rs[:, 0:nblk]))
                for b in range(nblk):
                    v.tensor_scalar(xn[:, b, :], src[:, b, :], ss[:, b:b + 1], None, ALU.mult).then_inc(s["scaled"], 1)
                for k in range(KD):
                    v.wait_ge(s["hi_done"], k + 1)
                    st.then(v.scalar_tensor_tensor(d_lo[:, k, 0:nblk * P], psum[:, k, 0:nblk * P], gain[:, k:k + 1],
                                                   d_hi[:, k, 0:nblk * P].bitcast(F32), ALU.mult, ALU.subtract))

            @block.tensor
            def _(pe):
                pe.wait_ge(s["scaled"], nblk)
                for k in range(KD):
                    for b in range(nblk):
                        mm = nc.tensor.transpose(psum[:, k, b * P:(b + 1) * P], xn[:, b, k * P:(k + 1) * P], m.ident[:])
                    mm.then_inc(s["turned"], 1)


def linear_stage(nc, kind, weights, act, nb, N, psum, copy, on="scalar", following=None):
    with ExitStack() as ctx, stage(nc, *LINEAR_SEMS, weights=weights) as s:
        lin = Linear(nc, ctx, s, kind, weights, act, nb, N, psum)
        with nc.Block() as block:
            block.sync(lambda sp: lin.sync(sp, following))
            block.tensor(lin.tensor)
            block.scalar(lambda a: lin.scalar(a, copy if on == "scalar" else None))
            block.vector(lambda v: lin.vector(v, copy if on == "vector" else None))


def hgrn_stage(nc, m, l, q, z, g, vtm, out, psum, io, sm):
    n2 = H * T
    with ExitStack() as ctx, stage(nc, "masks_in", "dve_step", "sig_done", "f_ready", "log_done", "summed", "exp_in", "exp_done",
                                   "mix_ready", "mm_done", "level_taken", "inter_ready", "inter_mm", "inter_copied",
                                   "o_mm", "o_copied", "sq_done", "ss_mm", "root_in", "root_done", "inverse", "spread_mm", "silu_done") as s:
        sb = lambda n, sh, dt=F32: ctx.enter_context(buffer(nc, n, sh, dt))
        masks = sb("masks", [P, len(LEVELS) + 1, P], I32)
        lb, om = sb("lb", [P, H]), sb("om", [P, H])
        root = sb("root", [P, P])
        sg, k, b, reset = sb("sg", [P, H, T]), sb("kk", [P, H, T]), sb("bb", [P, H, T]), sb("reset", [P, H, T])
        dlt = [reset, sb("dlt", [P, H, T])]
        mix = [sb("mix0", [P, H, T]), sb("mix1", [P, H, T])]
        att = sb("att", [P, H, T])
        near = sb("near", [P, H, 2, P])
        far = sb("far", [P, H, 2, 2 * P])
        qfar, k0far, eb = sb("qfar", [P, H, 2 * P]), sb("k0far", [P, H, P]), sb("eb", [P, H, TB])
        f2 = lambda t: t[:].rearrange("p h t -> p (h t)")
        NL = len(LEVELS)
        with nc.Block() as block:
            @block.sync
            def _(sp):
                sp.dma_start(masks[:], io["c_masks"]).then_inc(s["masks_in"], 16)

            @block.scalar
            def _(a):
                a.activation(f2(sg), f2(z), ACT.Sigmoid).then_inc(s["sig_done"], 1)
                a.activation(f2(k), f2(z), ACT.Sigmoid, scale=-1.0).then_inc(s["sig_done"], 1)
                a.wait_ge(s["f_ready"], 1)
                a.activation(f2(sg), f2(sg), ACT.Ln).then_inc(s["log_done"], 1)
                for i in range(NL):
                    a.wait_ge(s["exp_in"], 2 * i + 2)
                    a.activation(f2(dlt[i % 2]), f2(dlt[i % 2]), ACT.Exp).then_inc(s["exp_done"], 1)
                a.wait_ge(s["exp_in"], 2 * NL + 1)
                a.activation(f2(dlt[NL % 2]), f2(dlt[NL % 2]), ACT.Exp).then_inc(s["exp_done"], 1)
                a.activation(f2(b), f2(b), ACT.Exp).then_inc(s["exp_done"], 1)
                for h in range(H):
                    a.wait_ge(s["inter_mm"], 2 * h + 1)
                    a.copy(near[:, h].rearrange("p c t -> p (c t)"), psum[:, 4 + h % 2, 0:2 * P]).then_inc(s["inter_copied"], 1)
                    a.wait_ge(s["inter_mm"], 2 * h + 2)
                    a.copy(far[:, h].rearrange("p c t -> p (c t)"), psum[:, 6 + h % 2, :]).then_inc(s["inter_copied"], 1)
                a.activation(f2(g), f2(g), ACT.Silu).then_inc(s["silu_done"], 1)
                for h in range(H):
                    a.wait_ge(s["o_mm"], h + 1)
                    a.mul(out[:, h, :], psum[:, h, :], float(P) ** -0.5).then_inc(s["o_copied"], 1)
                    a.wait_ge(s["o_copied"], h + 1)
                    a.activation(mix[0][:, h, :], out[:, h, :], ACT.Square).then_inc(s["sq_done"], 1)
                a.wait_ge(s["root_in"], 1)
                a.activation(root[0:HC, :], root[0:HC, :], ACT.Sqrt).then_inc(s["root_done"], 1)

            @block.gpsimd
            def _(pool):
                pool.wait_ge(s["summed"], 1)
                for i, half in enumerate(LEVELS):
                    bv = f2(b).rearrange("p (n w) -> p n w", w=2 * half)
                    dv = f2(dlt[i % 2]).rearrange("p (n w) -> p n w", w=2 * half)
                    ref = bv[:, :, half - 1:half].broadcast_to([P, n2 // (2 * half), half])
                    if i >= 2:
                        pool.wait_ge(s["mix_ready"], i - 1)
                    pool.tensor_tensor(dv[:, :, 0:half], ref, bv[:, :, 0:half], ALU.subtract).then_inc(s["exp_in"], 1)
                    pool.tensor_tensor(dv[:, :, half:], bv[:, :, half:], ref, ALU.subtract).then_inc(s["exp_in"], 1)
                bv, dv = (f2(x).rearrange("p (n w) -> p n w", w=P) for x in (b, dlt[NL % 2]))
                pool.wait_ge(s["mix_ready"], NL - 1)
                pool.tensor_tensor(dv, bv[:, :, P - 1:P].broadcast_to([P, H * TB, P]), bv, ALU.subtract).then_inc(s["exp_in"], 1)

            @block.vector
            def _(v):
                st = Steps(v, s["dve_step"])
                st.link(v.tensor_copy(lb[:].rearrange("p (a h) -> p a h", a=1), m.lb_all[:, bass.ds(l, 1), :]))
                st.link(v.tensor_scalar(om[:], lb[:], -1.0, 1.0, ALU.mult, ALU.add))
                st.link(v.memset(reset[:], 1.0))
                st.link(v.memset(f2(reset)[:, 0:n2:P], 0.0))
                v.wait_ge(s["sig_done"], 2)
                for h in range(H):
                    st.then(v.tensor_scalar(sg[:, h, :], sg[:, h, :], om[:, h:h + 1], lb[:, h:h + 1], ALU.mult, ALU.add))
                    st.then(v.tensor_scalar(k[:, h, :], k[:, h, :], om[:, h:h + 1], None, ALU.mult))
                st.settle()
                v.tensor_scalar(f2(sg), f2(sg), 1e-6, 1.0, ALU.max, ALU.min).then_inc(s["f_ready"], 1)
                v.wait_ge(s["log_done"], 1)
                v.tensor_tensor_scan(f2(b), f2(reset), f2(sg), 0.0, ALU.mult, ALU.add).then_inc(s["summed"], 1)
                st.link(v.memset(att[:], 0.0))
                v.wait_ge(s["masks_in"], 16)

                def take(i):
                    for h in range(H):
                        v.wait_ge(s["mm_done"], H * i + h + 1)
                        if i:
                            v.wait_ge(s["level_taken"], H * (i - 1) + h + 1)
                        mk = masks[:, i:i + 1, :].broadcast_to([P, TB, P])
                        v.copy_predicated(att[:, h, :].rearrange("p (c t) -> p c t", c=TB), mk,
                                          psum[:, 4 * (i % 2) + h, :].rearrange("p (c t) -> p c t", c=TB)).then_inc(s["level_taken"], 1)

                take(0)
                for i, half in enumerate(LEVELS):
                    v.wait_ge(s["exp_done"], i + 1)
                    if i >= 2:
                        v.wait_ge(s["mm_done"], H * i)
                    sh = lambda t: f2(t).rearrange("p (n w) -> p n w", w=2 * half)
                    e, mx = sh(dlt[i % 2]), sh(mix[i % 2])
                    st.link(v.tensor_tensor(mx[:, :, 0:half], sh(k)[:, :, 0:half], e[:, :, 0:half], ALU.mult))
                    v.tensor_tensor(mx[:, :, half:], sh(q)[:, :, half:], e[:, :, half:], ALU.mult).then_inc(s["mix_ready"], 1)
                    if i >= 1:
                        take(i)
                d = dlt[NL % 2]
                take(NL)
                v.wait_ge(s["exp_done"], NL + 2)
                st.then(v.tensor_copy(eb[:].rearrange("p h c -> p (h c)"), f2(b)[:, P - 1:n2:P]))
                st.settle()
                v.wait_ge(s["mm_done"], H * (NL + 1))
                st.then(v.tensor_tensor(f2(mix[0]), f2(k), f2(d), ALU.mult))
                st.link(v.tensor_tensor(f2(mix[1]), f2(q), f2(b), ALU.mult))
                for h in range(H):
                    st.then(v.tensor_scalar(k0far[:, h, :], mix[0][:, h, 0:P], eb[:, h, 1:2], None, ALU.mult))
                    st.then(v.tensor_copy(qfar[:, h, 0:P], mix[1][:, h, 2 * P:3 * P]))
                    st.then(v.tensor_scalar(qfar[:, h, P:], mix[1][:, h, 3 * P:], eb[:, h, 2:3], None, ALU.mult))
                st.settle()
                v.engine_nop().then_inc(s["inter_ready"], 1)
                v.wait_ge(s["ss_mm"], H)
                v.tensor_scalar(root[0:HC, :], psum[0:HC, 4, 0:P], 1.0 / P, EPS, ALU.mult, ALU.add).then_inc(s["root_in"], 1)
                v.wait_ge(s["root_done"], 1)
                v.reciprocal(root[0:HC, :], root[0:HC, :]).then_inc(s["inverse"], 1)
                c0 = COL["hgrn_norm"][0]
                for h in range(H):
                    v.wait_ge(s["spread_mm"], h + 1)
                    st.then(v.tensor_tensor(out[:, h, :], out[:, h, :], psum[:, 4 + h, :], ALU.mult))
                st.settle()
                v.wait_ge(s["silu_done"], 1)
                for h in range(H):
                    st.then(v.scalar_tensor_tensor(out[:, h, :], out[:, h, :], sm[:, c0 + h:c0 + h + 1], g[:, h, :], ALU.mult, ALU.mult))

            @block.tensor
            def _(pe):
                pe.wait_ge(s["f_ready"], 1)
                for i in range(NL + 1):
                    if i:
                        pe.wait_ge(s["mix_ready"], i)
                    for h in range(H):
                        if i >= 2:
                            pe.wait_ge(s["level_taken"], H * (i - 2) + h + 1)
                        for c in range(TB):
                            cs = slice(c * P, (c + 1) * P)
                            lhs, rhs = (k, q) if i == 0 else (mix[(i - 1) % 2], mix[(i - 1) % 2])
                            mm = nc.tensor.matmul(psum[:, 4 * (i % 2) + h, cs], lhs[:, h, cs], rhs[:, h, cs], start=True, stop=True)
                        mm.then_inc(s["mm_done"], 1)
                pe.wait_ge(s["inter_ready"], 1)
                kd, qd = mix
                pe.wait_ge(s["level_taken"], H * (NL + 1))
                for h in range(H):
                    if h >= 2:
                        pe.wait_ge(s["inter_copied"], 2 * (h - 2) + 1)
                    nb_, fb = psum[:, 4 + h % 2, :], psum[:, 6 + h % 2, :]
                    nc.tensor.matmul(nb_[:, 0:P], kd[:, h, 0:P], qd[:, h, P:2 * P], start=True, stop=True)
                    nc.tensor.matmul(nb_[:, P:2 * P], kd[:, h, 2 * P:3 * P], qd[:, h, 3 * P:], start=True, stop=True).then_inc(s["inter_mm"], 1)
                    if h >= 2:
                        pe.wait_ge(s["inter_copied"], 2 * (h - 2) + 2)
                    nc.tensor.matmul(fb[:, 0:2 * P], k0far[:, h, :], qfar[:, h, :], start=True, stop=True)
                    nc.tensor.matmul(fb[:, 2 * P:], kd[:, h, P:2 * P], qfar[:, h, :], start=True, stop=True).then_inc(s["inter_mm"], 1)
                for h in range(H):
                    pe.wait_ge(s["inter_copied"], 2 * h + 2)
                    o = psum[:, h, :]
                    vt = lambda c: vtm[:, c, h * P:(h + 1) * P]
                    prods = [(o[:, c * P:(c + 1) * P], vt(c), att[:, h, c * P:(c + 1) * P]) for c in range(TB)]
                    prods += [(o[:, P:2 * P], vt(0), near[:, h, 0, :]), (o[:, 3 * P:], vt(2), near[:, h, 1, :]),
                              (o[:, 2 * P:], vt(0), far[:, h, 0, :]), (o[:, 2 * P:], vt(1), far[:, h, 1, :])]
                    for n, (dst, lhsT, rhs) in enumerate(prods):
                        mm = nc.tensor.matmul(dst, lhsT, rhs, start=(n == 0), stop=True, skip_group_check=True)
                    mm.then_inc(s["o_mm"], 1)
                pe.wait_ge(s["inter_copied"], 2 * H)
                for h in range(H):
                    pe.wait_ge(s["sq_done"], h + 1)
                    sums_of_head(nc, m, psum[0:HC, 4, 0:P], mix[0][:, h, :], h).then_inc(s["ss_mm"], 1)
                pe.wait_ge(s["inverse"], 1)
                for h in range(H):
                    spread_head(nc, m, psum[:, 4 + h, :], root[0:HC, :], h).then_inc(s["spread_mm"], 1)


def retention_stage(nc, m, q, k, g, vtm, out, psum, io):
    with ExitStack() as ctx, stage(nc, "dmat_in", "dve_step", "swapped", "times_cos", "rope_done", "score_mm", "decayed", "o_mm", "o_copied",
                                   "mean_mm", "centred", "sq_done", "var_mm", "root_in", "root_done", "inverse", "spread_mm", "silu_done") as s:
        sb = lambda n, sh, dt=F32: ctx.enter_context(buffer(nc, n, sh, dt))
        dmat = sb("dmat", [P, H, T])
        tmp = sb("rtmp", [P, 2, T])
        att = [sb(f"ratt{i}", [P, TB, T]) for i in range(2)]
        sq, root = sb("sq", [P, H, T]), sb("rroot", [P, P])
        f2 = lambda t: t[:].rearrange("p h t -> p (h t)")
        rows = [(x, h) for h in range(H) for x in (q, k)]
        with nc.Block() as block:
            @block.sync
            def _(sp):
                sp.dma_start(dmat[:], io["c_dmat"]).then_inc(s["dmat_in"], 16)

            @block.tensor
            def _(pe):
                for n, (x, h) in enumerate(rows):
                    nc.tensor.matmul(psum[:, n, :], m.perm[:], x[:, h, :], start=True, stop=True).then_inc(s["swapped"], 1)

                def scores(h):
                    pe.wait_ge(s["rope_done"], 2 * h + 2)
                    for c in range(TB):
                        n = H * h + c
                        if n >= 4:
                            pe.wait_ge(s["decayed"], n - 3)
                        else:
                            pe.wait_ge(s["rope_done"], n + 1)
                        nc.tensor.matmul(psum[:, n % 4, 0:T - c * P], k[:, h, c * P:(c + 1) * P], q[:, h, c * P:], start=True, stop=True).then_inc(s["score_mm"], 1)

                scores(0)
                for h in range(H):
                    if h + 1 < H:
                        scores(h + 1)
                    if h == 0:
                        pe.wait_ge(s["rope_done"], 2 * H)
                    pe.wait_ge(s["decayed"], TB * (h + 1))
                    for c in range(TB):
                        mm = nc.tensor.matmul(psum[:, 4 + h, c * P:], vtm[:, c, h * P:(h + 1) * P], att[h % 2][:, c, 0:T - c * P],
                                              start=(c == 0), stop=True, skip_group_check=True)
                    mm.then_inc(s["o_mm"], 1)
                for h in range(H):
                    pe.wait_ge(s["o_copied"], h + 1)
                    nc.tensor.matmul(psum[:, h, :], m.ones[:], out[:, h, :], start=True, stop=True).then_inc(s["mean_mm"], 1)
                for h in range(H):
                    pe.wait_ge(s["sq_done"], h + 1)
                    sums_of_head(nc, m, psum[0:HC, 4, 0:P], sq[:, h, :], h).then_inc(s["var_mm"], 1)
                pe.wait_ge(s["inverse"], 1)
                for h in range(H):
                    spread_head(nc, m, psum[:, h, :], root[0:HC, :], h).then_inc(s["spread_mm"], 1)

            @block.scalar
            def _(a):
                a.activation(f2(g), f2(g), ACT.Silu).then_inc(s["silu_done"], 1)
                for h in range(H):
                    a.wait_ge(s["o_mm"], h + 1)
                    a.copy(out[:, h, :], psum[:, 4 + h, :]).then_inc(s["o_copied"], 1)
                for h in range(H):
                    a.wait_ge(s["centred"], h + 1)
                    a.activation(sq[:, h, :], out[:, h, :], ACT.Square).then_inc(s["sq_done"], 1)
                a.wait_ge(s["root_in"], 1)
                a.activation(root[0:HC, :], root[0:HC, :], ACT.Sqrt).then_inc(s["root_done"], 1)

            @block.gpsimd
            def _(pool):
                for n, (x, h) in enumerate(rows):
                    pool.wait_ge(s["swapped"], n + 1)
                    pool.tensor_tensor(x[:, h, :], x[:, h, :], m.cos[:], ALU.mult).then_inc(s["times_cos"], 1)

            @block.vector
            def _(v):
                st = Steps(v, s["dve_step"])
                for n, (x, h) in enumerate(rows):
                    v.wait_ge(s["swapped"], n + 1)
                    st.link(v.tensor_tensor(tmp[:, n % 2, :], psum[:, n, :], m.sin[:], ALU.mult))
                    v.wait_ge(s["times_cos"], n + 1)
                    v.tensor_tensor(x[:, h, :], x[:, h, :], tmp[:, n % 2, :], ALU.add).then_inc(s["rope_done"], 1)
                v.wait_ge(s["dmat_in"], 16)
                for h in range(H):
                    for c in range(TB):
                        v.wait_ge(s["score_mm"], H * h + c + 1)
                        if h >= 2:
                            v.wait_ge(s["o_mm"], h - 1)
                        w = T - c * P
                        v.tensor_tensor(att[h % 2][:, c, 0:w], psum[:, (H * h + c) % 4, 0:w], dmat[:, h, 0:w], ALU.mult).then_inc(s["decayed"], 1)
                for h in range(H):
                    v.wait_ge(s["mean_mm"], h + 1)
                    v.scalar_tensor_tensor(out[:, h, :], psum[:, h, :], -1.0 / P, out[:, h, :], ALU.mult, ALU.add).then_inc(s["centred"], 1)
                v.wait_ge(s["var_mm"], H)
                v.tensor_scalar(root[0:HC, :], psum[0:HC, 4, 0:P], 1.0 / P, EPS, ALU.mult, ALU.add).then_inc(s["root_in"], 1)
                v.wait_ge(s["root_done"], 1)
                v.reciprocal(root[0:HC, :], root[0:HC, :]).then_inc(s["inverse"], 1)
                for h in range(H):
                    v.wait_ge(s["spread_mm"], h + 1)
                    st.then(v.tensor_tensor(out[:, h, :], out[:, h, :], psum[:, h, :], ALU.mult))
                st.settle()
                v.wait_ge(s["silu_done"], 1)
                st.link(v.tensor_tensor(f2(out), f2(out), f2(g), ALU.mult))


def ssm_tables_stage(nc, m, io, l, sm, tabs, spare):
    with ExitStack() as ctx, stage(nc, "bc_in", "dve_step", "dt_in", "exp_in", "exp_done", "sin_in", "sin_done", "tab_in", "tab_done",
                                   "powers_in", "pool_step") as s:
        sb = lambda n, sh, dt=F32: ctx.enter_context(buffer(nc, n, sh, dt))
        bc = sb("bc", [P, 4, G5, C5])
        nvec = sb("nvec", [P, N5])
        t = sb("t5", [P, 18 + J5, G5])
        pr, pi = sb("pr", [P, J5 + 1, G5]), sb("pi", [P, J5 + 1, G5])
        fr, fi = sb("fr", [P, J5 + 1, G5]), sb("fi", [P, J5 + 1, G5])
        zr, zi = sb("zr", [P, J5, G5]), sb("zi", [P, J5, G5])
        halves = [x.rearrange("p a t -> p (a t)").rearrange("p (g j c) -> p g j c", j=J5, c=C5) for x in spare]
        gjc = [P, G5 // 2, J5, C5]
        coef = lambda x, gs: x.rearrange("p (j c) g -> p g j c", c=1)[:, gs].broadcast_to(gjc)
        base = lambda i, gs: bc[:, i].rearrange("p g (j c) -> p g j c", j=1)[:, gs].broadcast_to(gjc)

        def combine(eng, st, dst, re, im, i, h, scratch):
            gs = slice(h * G5 // 2, (h + 1) * G5 // 2)
            st.then(eng.tensor_tensor(dst[:, gs], base(i, gs), coef(re, gs), ALU.mult))
            st.link(eng.tensor_tensor(scratch, base(i + 1, gs), coef(im, gs), ALU.mult))
            st.link(eng.tensor_tensor(dst[:, gs], dst[:, gs], scratch, ALU.add))

        col = lambda n: sm[:, COL[n][0]:COL[n][1]]
        sgn = m.cols[:, 1:2]
        nsgn = m.cols[:, 2:3]
        lr, dt, th, th8, red, cred, mag, are, aim, den, tmp, r8, fhi, flo, u1, u2, zre, zim = (t[:, i, :] for i in range(18))
        with nc.Block() as block:
            @block.sync
            def _(sp):
                sp.dma_start(bc[:].rearrange("p a g c -> p (a g c)"), tile_at(io["s5_bc"], l)).then_inc(s["bc_in"], 16)
                sp.dma_start(nvec[:], io["c_nvec"]).then_inc(s["bc_in"], 16)

            @block.scalar
            def _(a):
                a.activation(dt, col("log_step"), ACT.Exp).then_inc(s["dt_in"], 1)
                a.wait_ge(s["exp_in"], 1)
                a.activation(mag, u1, ACT.Exp).then_inc(s["exp_done"], 1)
                a.activation(r8, u1, ACT.Exp, scale=float(J5)).then_inc(s["exp_done"], 1)
                a.wait_ge(s["sin_in"], 1)
                a.activation(aim, red, ACT.Sin).then_inc(s["sin_done"], 1)
                a.activation(are, cred, ACT.Sin).then_inc(s["sin_done"], 1)
                a.wait_ge(s["tab_in"], 1)
                a.activation(tabs.sin[:], tabs.sin[:], ACT.Sin, scale=TWO_PI).then_inc(s["tab_done"], 1)
                a.activation(tabs.cos[:], tabs.cos[:], ACT.Sin, scale=TWO_PI).then_inc(s["tab_done"], 1)

            @block.gpsimd
            def _(pool):
                st = Steps(pool, s["pool_step"])
                st.then(pool.memset(tabs.pc[:, :, 0:J5 - 1, :], 0.0))
                pool.wait_ge(s["powers_in"], 1)
                st.then(pool.tensor_copy(tabs.pc[:, :, J5 - 1, :], bc[:, 2]))
                for h in range(2):
                    combine(pool, st, tabs.pc[:, :, J5:, :], pr[:, 1:, :], pi[:, 1:, :], 2, h, halves[1 + h])
                pool.wait_ge(s["powers_in"], 2)
                combine(pool, st, tabs.gb, zr[:], zi[:], 0, 1, halves[1])

            @block.vector
            def _(v):
                st = Steps(v, s["dve_step"])
                tt = lambda o, x, y, op: st.link(v.tensor_tensor(o, x, y, op))
                ts = lambda o, x, c, d, op, op2=ALU.bypass: st.link(v.tensor_scalar(o, x, c, d, op, op2))
                v.wait_ge(s["dt_in"], 1)
                ts(lr, col("lam_re"), -1e-4, None, ALU.min)
                tt(u1, lr, dt, ALU.mult)
                v.engine_nop().then_inc(s["exp_in"], 1)
                tt(th, col("lam_im"), dt, ALU.mult)
                reduce_angle(v, st, red, th, tmp)
                cos_argument(v, st, cred, red, tmp)
                v.engine_nop().then_inc(s["sin_in"], 1)
                v.wait_ge(s["exp_done"], 2)
                v.wait_ge(s["bc_in"], 32)
                v.wait_ge(s["sin_done"], 2)
                tt(are, are, mag, ALU.mult)
                tt(aim, aim, mag, ALU.mult)
                tt(den, lr, lr, ALU.mult)
                tt(tmp, col("lam_im"), col("lam_im"), ALU.mult)
                tt(den, den, tmp, ALU.add)
                st.link(v.reciprocal(den, den))
                ts(u1, are, -1.0, None, ALU.add)
                tt(zre, u1, lr, ALU.mult)
                tt(tmp, aim, col("lam_im"), ALU.mult)
                tt(zre, zre, tmp, ALU.add)
                tt(zim, aim, lr, ALU.mult)
                tt(tmp, u1, col("lam_im"), ALU.mult)
                tt(zim, zim, tmp, ALU.subtract)
                tt(zre, zre, den, ALU.mult)
                tt(zim, zim, den, ALU.mult)

                def product(ore, oim, xre, xim, yre, yim, w):
                    wide = t[:, 18:18 + w, :]
                    tt(ore, xre, yre, ALU.mult)
                    tt(wide, xim, yim, ALU.mult)
                    tt(ore, ore, wide, ALU.subtract)
                    tt(oim, xre, yim, ALU.mult)
                    tt(wide, xim, yre, ALU.mult)
                    tt(oim, oim, wide, ALU.add)

                fl = lambda i: bc[:, i].rearrange("p g c -> p (g c)")
                st.then(v.tensor_scalar(fl(1), fl(1), sgn, None, ALU.mult))
                st.then(v.tensor_scalar(fl(2), fl(2), nsgn, None, ALU.mult))
                st.then(v.tensor_scalar(fl(3), fl(3), -1.0, None, ALU.mult))
                rising, falling = (lambda lo, hi: slice(lo, hi + 1)), (lambda lo, hi: slice(J5 - hi, J5 - lo + 1))

                per_power = lambda x: x.rearrange("p (j g) -> p j g", j=1)

                def powers(re, im, slot):
                    st.link(v.memset(re[:, slot(0, 0), :], 1.0))
                    st.link(v.memset(im[:, slot(0, 0), :], 0.0))
                    st.link(v.tensor_copy(re[:, slot(1, 1), :], per_power(are)))
                    st.link(v.tensor_copy(im[:, slot(1, 1), :], per_power(aim)))
                    for k in (1, 2, 4):
                        y = lambda z: z[:, slot(k, k), :].broadcast_to([P, k, G5])
                        new, old = slot(k + 1, 2 * k), slot(1, k)
                        product(re[:, new, :], im[:, new, :], re[:, old, :], im[:, old, :], y(re), y(im), k)

                powers(pr, pi, rising)
                v.engine_nop().then_inc(s["powers_in"], 1)
                ts(th8, red, float(J5), None, ALU.mult)
                reduce_angle(v, st, u2, th8, tmp)
                ts(u2, u2, 1.0 / TWO_PI, None, ALU.mult)
                ts(fhi, u2, ROUND13, None, ALU.add)
                ts(fhi, fhi, -ROUND13, None, ALU.add)
                tt(flo, u2, fhi, ALU.subtract)
                gn = [P, G5, N5]
                per_g = lambda x: x.rearrange("p (g n) -> p g n", n=1).broadcast_to(gn)
                per_n = nvec[:].rearrange("p (g n) -> p g n", g=1).broadcast_to(gn)
                s3 = tabs.sin[:].rearrange("p (g n) -> p g n", n=N5)
                c3 = tabs.cos[:].rearrange("p (g n) -> p g n", n=N5)
                d3 = tabs.decay[:].rearrange("p (g n) -> p g n", n=N5)
                st.link(v.tensor_tensor(s3, per_g(fhi), per_n, ALU.mult))
                st.link(v.tensor_scalar(tabs.cos[:], tabs.sin[:], ROUND, None, ALU.add))
                st.link(v.tensor_scalar(tabs.cos[:], tabs.cos[:], -ROUND, None, ALU.add))
                st.link(v.tensor_tensor(s3, s3, c3, ALU.subtract))
                st.link(v.tensor_tensor(c3, per_g(flo), per_n, ALU.mult))
                st.link(v.tensor_tensor(s3, s3, c3, ALU.add))
                st.link(v.tensor_scalar(tabs.cos[:], tabs.sin[:], 0.25, None, ALU.add))
                st.link(v.tensor_scalar(tabs.decay[:], tabs.cos[:], 0.5, -1.0, ALU.is_gt, ALU.mult))
                st.link(v.tensor_tensor(tabs.cos[:], tabs.cos[:], tabs.decay[:], ALU.add))
                for x in (tabs.sin, tabs.cos):
                    st.link(v.tensor_scalar(x[:], x[:], 0.4999999, -0.4999999, ALU.min, ALU.max))
                v.engine_nop().then_inc(s["tab_in"], 1)
                st.link(v.tensor_copy(d3, per_g(r8)))
                st.link(v.memset(tabs.decay[:, 0:G5 * N5:N5], 0.0))
                powers(fr, fi, falling)
                y = lambda z: z.broadcast_to([P, J5, G5])
                product(zr[:], zi[:], fr[:, 1:, :], fi[:, 1:, :], y(per_power(zre)), y(per_power(zim)), J5)
                v.engine_nop().then_inc(s["powers_in"], 1)
                combine(v, st, tabs.gb, zr[:], zi[:], 0, 0, halves[0])
                v.wait_ge(s["tab_done"], 2)
                v.tensor_scalar(tabs.sin[:], tabs.sin[:], nsgn, None, ALU.mult).then_inc(s["dve_step"], 1)


def ssm_stage(nc, m, sm, tabs, u, work, spare, rows, w_glu, psum):
    with ExitStack() as ctx, stage(nc, "dve_step", "rows_mm", "sorted_even", "sorted_odd", "turn_mm", "turn_copied", "w_mm", "w_copied",
                                   "inj_mm", "inj_turned", "scanned", "block_mm", "block_copied", "toep_in0", "toep_in1",
                                   "swap_mm", "states_in", "y_mm", "y_taken", "y_done", "yt_mm", "yt_copied",
                                   "out_mm", "out_copied", "glu_in") as s:
        sb = lambda n, sh, dt=F32: ctx.enter_context(buffer(nc, n, sh, dt))
        PER = 8
        NB = G5 // PER
        HALF = J5 // 2
        ug = rows.rearrange("n a f -> n (a f)").rearrange("n (g j c) -> n g j c", g=G5, j=J5)
        y64 = rows.rearrange("n a f -> n (a f)").rearrange("n (j f) -> n j f", j=J5)
        uc = sb("uc", [P, G5, N5])
        toep = sb("toep", [P, G5, J5 * C5])
        blocks = [x.rearrange("p a t -> p (a t)").rearrange("p (g k) -> p g k", g=PER)[0:C5] for x in (spare, u)]
        wmat = [sb(f"wmat{i}", [P, 2, 2, P]) for i in range(2)]
        om_, yb, st_ = (x.rearrange("p a t -> p (a t)").rearrange("p (g n) -> p g n", n=N5) for x in work)
        toep_in = (s["toep_in0"], s["toep_in1"])
        ALL_IN = 16 * J5
        f2 = lambda t: t[:].rearrange("p g n -> p (g n)")
        def sort_rows(copy, x):
            g0, j0 = (x // 2) * PER, (x % 2) * HALF
            return copy(ug[:, g0:g0 + PER, j0:j0 + HALF, :], psum[0:N5, x, :].rearrange("n (j g c) -> n g j c", j=HALF, g=PER))

        with nc.Block() as block:
            @block.sync
            def _(sp):
                for c in range(NB):
                    sp.wait_ge(s["block_copied"], 2 * c + 2)
                    for j in range(J5):
                        sp.dma_start(toep[j * C5:(j + 1) * C5, c * PER:(c + 1) * PER, :],
                                     blocks[c % 2][:, :, (J5 - 1 - j) * C5:(2 * J5 - 1 - j) * C5]).then_inc(toep_in[c % 2], 16)
                sp.wait_ge(toep_in[1], ALL_IN * (NB // 2))
                sp.dma_start(u.rearrange("p a t -> p (a t)"), w_glu).then_inc(s["glu_in"], 16)
                sp.wait_ge(s["glu_in"], 16)

            @block.tensor
            def _(pe):
                for x in range(2 * NB):
                    b, j0 = x // 2, (x % 2) * HALF
                    for j in range(HALF):
                        mm = nc.tensor.transpose(psum[0:N5, x, j * P:(j + 1) * P], u[:, b, j0 + j:T:J5], m.ident[:])
                    mm.then_inc(s["rows_mm"], 1)
                for b in range(NB):
                    pe.wait_ge(s["sorted_even"], b + 1)
                    pe.wait_ge(s["sorted_odd"], b + 1)
                    for g in range(b * PER, (b + 1) * PER):
                        mm = nc.tensor.transpose(psum[:, b, (g % PER) * N5:(g % PER + 1) * N5],
                                                 ug[:, g].rearrange("n j c -> n (j c)"), m.ident[0:N5, 0:N5])
                    mm.then_inc(s["turn_mm"], 1)
                for c in range(G5 // 2 + 1):
                    if c < G5 // 2:
                        b = c % 2
                        if c < 2:
                            pe.wait_ge(s["turn_copied"], NB)
                        else:
                            pe.wait_ge(s["w_copied"], c - 1)
                        for y in range(2):
                            wz = tabs.gb[:, 2 * c + y, :, :].rearrange("p j c -> p (j c)")
                            nc.tensor.transpose(psum[:, 6 + b, 2 * y * P:(2 * y + 1) * P], wz, m.ident[:])
                            mm = nc.tensor.matmul(psum[:, 6 + b, (2 * y + 1) * P:(2 * y + 2) * P], wz, m.perm[:], start=True, stop=True)
                        mm.then_inc(s["w_mm"], 1)
                    if c:
                        pe.wait_ge(s["w_copied"], c)
                        for g in (2 * c - 2, 2 * c - 1):
                            if g % 4 == 0 and g >= 8:
                                pe.wait_ge(s["inj_turned"], g // 4 - 1)
                            cols = slice((g % 4) * N5, (g % 4 + 1) * N5)
                            w = wmat[(c - 1) % 2]
                            nc.tensor.matmul(psum[:, (g // 4) % 2, cols], w[:, g % 2, 0, :], uc[:, g, :], start=True, stop=True)
                            nc.tensor.matmul(psum[:, 2 + (g // 4) % 2, cols], w[:, g % 2, 1, :], uc[:, g, :], start=True, stop=True).then_inc(s["inj_mm"], 1)
                def toeplitz_blocks(c):
                    bank = 4 + 2 * (c % 2)
                    if c < 2:
                        pe.wait_ge(s["w_copied"], G5 // 2)
                    else:
                        pe.wait_ge(s["block_copied"], c - 1)
                    for g in range(4 * c, 4 * c + 4):
                        mm = nc.tensor.matmul(psum[0:C5, bank + (g % 4) // 2, (g % 2) * 256:(g % 2 + 1) * 256], tabs.gb[:, g, J5 - 1, :],
                                              tabs.pc[:, g].rearrange("p k c -> p (k c)"), start=True, stop=True)
                    mm.then_inc(s["block_mm"], 1)

                for c in range(NB):
                    toeplitz_blocks(c)
                pe.wait_ge(s["inj_turned"], G5 // 4)
                pe.wait_ge(s["scanned"], 1)
                for c in range(NB):
                    nc.tensor.matmul(psum[:, c, :], m.perm[:], f2(om_)[:, c * 512:(c + 1) * 512], start=True, stop=True).then_inc(s["swap_mm"], 1)
                for c in range(NB, 2 * NB):
                    toeplitz_blocks(c)
                pe.wait_ge(s["block_copied"], 2 * NB)
                for g in range(G5):
                    b = g // PER
                    if g % PER == 0:
                        pe.wait_ge(toep_in[b % 2], ALL_IN * (b // 2 + 1))
                        if b >= 2:
                            pe.wait_ge(s["y_taken"], b - 1)
                    if g == 0:
                        pe.wait_ge(s["states_in"], 1)
                    yp = psum[:, 4 + b % 2, (g % PER) * N5:(g % PER + 1) * N5]
                    nc.tensor.matmul(yp, toep[:, g, :], uc[:, g, :], start=True, stop=True, skip_group_check=True)
                    nc.tensor.matmul(yp[:, 1:], tabs.pc[:, g, J5:, :].rearrange("p j c -> p (j c)"), st_[:, g, 0:N5 - 1],
                                     start=False, stop=True, skip_group_check=True).then_inc(s["y_mm"], 1)

                def out(b):
                    pe.wait_ge(s["yt_copied"], 2 * b + 2)
                    if b >= 2:
                        pe.wait_ge(s["out_copied"], b - 1)
                    for j in range(J5):
                        mm = nc.tensor.transpose(psum[:, 6 + b % 2, j * N5:(j + 1) * N5], y64[:, j, b * P:(b + 1) * P], m.ident[0:N5, 0:N5])
                    mm.then_inc(s["out_mm"], 1)

                for k in range(G5 // 4):
                    pe.wait_ge(s["y_done"], k // 2 + 1)
                    if k >= 4:
                        pe.wait_ge(s["yt_copied"], k - 3)
                    for g in range(4 * k, 4 * k + 4):
                        mm = nc.tensor.transpose(psum[0:N5, k % 4, (g % 4) * P:(g % 4 + 1) * P], yb[:, g, :], m.ident[:])
                    mm.then_inc(s["yt_mm"], 1)
                    if k % 2 and k >= 3:
                        out(k // 2 - 1)
                out(NB - 1)

            @block.scalar
            def _(a):
                for b in range(NB):
                    a.wait_ge(s["rows_mm"], 2 * b + 1)
                    sort_rows(a.copy, 2 * b).then_inc(s["sorted_even"], 1)
                for c in range(NB):
                    a.wait_ge(s["turn_mm"], c + 1)
                    a.copy(f2(uc)[:, c * 512:(c + 1) * 512], psum[:, c, :]).then_inc(s["turn_copied"], 1)
                for c in range(G5 // 2):
                    a.wait_ge(s["w_mm"], c + 1)
                    if c >= 2:
                        a.wait_ge(s["inj_mm"], 2 * c - 2)
                    a.copy(wmat[c % 2][:].rearrange("p g a k -> p (g a k)"), psum[:, 6 + c % 2, :]).then_inc(s["w_copied"], 1)
                for c in range(2 * NB):
                    r = c // 2
                    a.wait_ge(s["block_mm"], c + 1)
                    if r >= 2 and c % 2 == 0:
                        a.wait_ge(toep_in[r % 2], ALL_IN * (r // 2))
                    a.copy(blocks[r % 2][:, (c % 2) * 4:(c % 2) * 4 + 4, :].rearrange("p g k -> p (g k)"),
                           psum[0:C5, 4 + 2 * (c % 2):6 + 2 * (c % 2), :].rearrange("p b k -> p (b k)")).then_inc(s["block_copied"], 1)
                for c in range(NB):
                    a.wait_ge(s["y_taken"], c + 1)
                    a.activation(f2(yb)[:, c * 512:(c + 1) * 512], f2(yb)[:, c * 512:(c + 1) * 512], ACT.Gelu_apprx_tanh).then_inc(s["y_done"], 1)
                for k in range(G5 // 4):
                    a.wait_ge(s["yt_mm"], k + 1)
                    a.copy(y64[:, :, k * 64:(k + 1) * 64].rearrange("n j (g c) -> n g j c", c=C5),
                           psum[0:N5, k % 4, :].rearrange("n (g j c) -> n g j c", g=4, j=J5)).then_inc(s["yt_copied"], 1)

            @block.vector
            def _(v):
                st = Steps(v, s["dve_step"])
                for b in range(NB):
                    v.wait_ge(s["rows_mm"], 2 * b + 2)
                    sort_rows(v.tensor_copy, 2 * b + 1).then_inc(s["sorted_odd"], 1)
                for c in range(G5 // 4):
                    v.wait_ge(s["inj_mm"], 4 * (c + 1))
                    cs = slice(c * 256, (c + 1) * 256)
                    st.then(v.tensor_tensor(f2(om_)[:, cs], psum[:, c % 2, 0:256], tabs.cos[:, cs], ALU.mult))
                    st.link(v.tensor_tensor(f2(st_)[:, cs], psum[:, 2 + c % 2, 0:256], tabs.sin[:, cs], ALU.mult))
                    v.tensor_tensor(f2(om_)[:, cs], f2(om_)[:, cs], f2(st_)[:, cs], ALU.add).then_inc(s["inj_turned"], 1)
                v.wait_ge(s["inj_turned"], G5 // 4)
                st.link(v.tensor_tensor_scan(f2(st_), tabs.decay[:], f2(om_), 0.0, ALU.mult, ALU.add))
                st.link(v.tensor_copy(f2(om_), f2(st_)))
                v.engine_nop().then_inc(s["scanned"], 1)
                st.link(v.tensor_tensor(f2(st_), f2(st_), tabs.cos[:], ALU.mult))
                for c in range(NB):
                    cs = slice(c * 512, (c + 1) * 512)
                    v.wait_ge(s["swap_mm"], c + 1)
                    st.then(v.tensor_tensor(f2(yb)[:, cs], psum[:, c, :], tabs.sin[:, cs], ALU.mult))
                st.settle()
                v.tensor_tensor(f2(st_), f2(st_), f2(yb), ALU.subtract).then_inc(s["states_in"], 1)
                v.wait_ge(s["states_in"], 1)
                d3 = sm[:, COL["s5_d"][0]:COL["s5_d"][1]].rearrange("p (g n) -> p g n", n=1)
                v.wait_ge(s["swap_mm"], NB)
                st.link(v.tensor_tensor(om_[:], uc[:], d3.broadcast_to([P, G5, N5]), ALU.mult))
                for c in range(NB):
                    cs = slice(c * 512, (c + 1) * 512)
                    v.wait_ge(s["y_mm"], PER * (c + 1))
                    v.tensor_tensor(f2(yb)[:, cs], psum[:, 4 + c % 2, :], f2(om_)[:, cs], ALU.add).then_inc(s["y_taken"], 1)
                v.wait_ge(s["y_taken"], NB)
                for b in range(NB):
                    v.wait_ge(s["out_mm"], b + 1)
                    v.tensor_copy(work[0][:, b, :].rearrange("p (n j) -> p n j", j=J5),
                                  psum[:, 6 + b % 2, :].rearrange("p (j n) -> p n j", j=J5)).then_inc(s["out_copied"], 1)


def glu_stage(nc, w, y, out, sm, psum):
    with stage(nc, "mm_done", "sig_done", "out_done") as s:
        c0 = COL["b_glu"][0]
        with nc.Block() as block:
            @block.tensor
            def _(pe):
                for b in range(4):
                    for k in range(4):
                        mm = nc.tensor.matmul(psum[:, b, :], w[:, k, b * P:(b + 1) * P], y[:, k, :], start=(k == 0), stop=(k == 3))
                    mm.then_inc(s["mm_done"], 1)

            @block.scalar
            def _(a):
                for b in range(4):
                    a.wait_ge(s["mm_done"], b + 1)
                    a.activation(out[:, b, :], psum[:, b, :], ACT.Sigmoid, bias=sm[:, c0 + b:c0 + b + 1]).then_inc(s["sig_done"], 1)

            @block.vector
            def _(v):
                for b in range(4):
                    v.wait_ge(s["sig_done"], b + 1)
                    v.tensor_tensor(out[:, b, :], out[:, b, :], y[:, b, :], ALU.mult).then_inc(s["out_done"], 1)


def gates_stage(nc, weights, h, sm, gates, psum, following):
    c0 = COL["b_gate"][0]

    def copy(t, b, bank):
        return nc.scalar.activation(gates[:, bass.ds(t * 4 + b, 1), :].rearrange("p a n -> p (a n)"), bank, ACT.Sigmoid,
                                    bias=sm[:, bass.ds(t * 4 + b + c0, 1)])
    linear_stage(nc, "fm", weights, h, 4, T, psum, copy, following=following)


@contextmanager
def hi_lo(nc, name, shape):
    with buffer(nc, name + "_hi", shape, F32R) as hi, buffer(nc, name + "_lo", shape, F32R) as lo:
        yield hi, lo


def merge_stage(nc, weights, branches, gates, parts, following, psum):
    NBR, HALF = 3, 4
    with ExitStack() as ctx, stage(nc, "branch_hi", "branch_lo", "w_hi", "w_lo", "unit_mm", "weighed", "added",
                                   "sum_hi", "sum_lo", weights=weights) as s:
        hi = [ctx.enter_context(buffer(nc, f"wm_hi{i}", [P, 4, P], F32R)) for i in range(2)]
        lo = [ctx.enter_context(buffer(nc, f"wm_lo{i}", [P, 4, P], F32R)) for i in range(2)]
        raw, ready = weights.raw, weights.arrived
        p_hi, p_lo = parts
        NU = NBR * KD
        operand = lambda x, br: x[:, HALF:KD, :] if br % 2 == 0 else x[:, 0:HALF, :]
        unit_of = lambda n: raw[n // HALF % 2][:, :, (n % HALF) * P:(n % HALF + 1) * P]
        early = {0: 0, 6: 1, 12: 2}
        with nc.Block() as block:
            @block.sync
            def _(sp):
                for t in range(2, weights.n + 2):
                    sp.wait_ge(s["w_lo"], HALF * (t - 1))
                    if t < weights.n:
                        weights.load(sp, t, t % 2)
                    else:
                        following.load(sp, t - weights.n, t % 2)

            @block.tensor
            def _(pe):
                for n in range(NU):
                    br = n // KD
                    pe.wait_ge(s["w_lo"], n + 1)
                    if n % KD == 0:
                        pe.wait_ge(s["branch_lo"], br + 1)
                    if n >= 8:
                        pe.wait_ge(s["weighed"], n - 7)
                    w_hi, w_lo = hi[n % 2], lo[n % 2]
                    b_hi, b_lo = operand(p_hi, br), operand(p_lo, br)
                    for x, (w, v) in enumerate([(w_hi, b_lo), (w_lo, b_hi), (w_hi, b_hi)]):
                        for k in range(4):
                            mm = nc.tensor.matmul(psum[:, n % 8, :], w[:, k, :], v[:, k, :], start=(x == 0 and k == 0), stop=(x == 2 and k == 3))
                    mm.then_inc(s["unit_mm"], 1)

            @block.scalar
            def _(a):
                def sum_high(d):
                    a.wait_ge(s["added"], KD * (NBR - 2) + d + 1)
                    if d >= HALF:
                        a.wait_ge(s["unit_mm"], NU)
                    a.copy(p_hi[:, d, :], gates[:, d, :]).then_inc(s["sum_hi"], 1)

                for n in range(NU):
                    if n in early:
                        br = early[n]
                        if br == 2:
                            a.wait_ge(s["unit_mm"], KD)
                        a.copy(operand(p_hi, br), branches[br]).then_inc(s["branch_hi"], 1)
                    if n % HALF == 0:
                        t = n // HALF
                        a.wait_ge(ready[t % 2], 16 * (t // 2 + 1))
                    if n >= 2:
                        a.wait_ge(s["unit_mm"], n - 1)
                    a.copy(hi[n % 2][:], unit_of(n)).then_inc(s["w_hi"], 1)
                    if 0 <= n - 18 < HALF:
                        sum_high(n - 18)
                for d in range(HALF, KD):
                    sum_high(d)

            @block.vector
            def _(v):
                def weigh(n):
                    d = n % KD
                    v.wait_ge(s["unit_mm"], n + 1)
                    g = gates[:, n, :]
                    v.tensor_tensor(g, psum[:, n % 8, :], g, ALU.mult).then_inc(s["weighed"], 1)
                    if n >= KD:
                        v.wait_ge(s["weighed"], n + 1)
                        if n >= 2 * KD:
                            v.wait_ge(s["added"], n - 2 * KD + 1)
                        v.tensor_tensor(gates[:, d, :], gates[:, d, :], g, ALU.add).then_inc(s["added"], 1)

                def sum_low(d):
                    v.wait_ge(s["sum_hi"], d + 1)
                    v.tensor_tensor(p_lo[:, d, :], gates[:, d, :], p_hi[:, d, :].bitcast(F32), ALU.subtract).then_inc(s["sum_lo"], 1)

                for n in range(NU):
                    if n in early:
                        br = early[n]
                        v.wait_ge(s["branch_hi"], br + 1)
                        v.tensor_tensor(operand(p_lo, br), branches[br], operand(p_hi, br).bitcast(F32), ALU.subtract).then_inc(s["branch_lo"], 1)
                    v.wait_ge(s["w_hi"], n + 1)
                    v.tensor_tensor(lo[n % 2][:], unit_of(n), hi[n % 2][:].bitcast(F32), ALU.subtract).then_inc(s["w_lo"], 1)
                    if n:
                        weigh(n - 1)
                    if 0 <= n - 19 < HALF:
                        sum_low(n - 19)
                weigh(NU - 1)
                for d in range(HALF, KD):
                    sum_low(d)


def attend_stage(nc, m, q, k, v_tm, out, psum):
    XH, XD = 4, 2
    scale = float(XD * P) ** -0.5
    with ExitStack() as ctx, stage(nc, "score_mm", "neg_done", "exp_done", "dve_step", "p_ready", "turned", "pt_copied", "o_mm", "o_hi", "o_lo") as s:
        sb = lambda n, sh, dt=F32: ctx.enter_context(buffer(nc, n, sh, dt))
        out_hi, out_lo = out
        pr = [sb(f"prob{i}", [P, TB, MEM]) for i in range(2)]
        pt = [sb(f"probT{i}", [P, MB, T]) for i in range(2)]
        mx, sm_, rc = sb("mx", [P, XH, TB]), sb("sme", [P, XH, TB]), sb("rc", [P, XH, TB])
        with nc.Block() as block:
            @block.tensor
            def _(pe):
                def scores(h):
                    if h >= 2:
                        pe.wait_ge(s["exp_done"], TB * (h - 1))
                    for b in range(TB):
                        for kk in range(XD):
                            mm = nc.tensor.matmul(psum[:, 2 * (h % 2) + b // 2, (b % 2) * MEM:(b % 2 + 1) * MEM],
                                                  q[:, XD * h + kk, b * P:(b + 1) * P], k[:, XD * h + kk, 0:MEM], start=(kk == 0), stop=(kk == XD - 1))
                    mm.then_inc(s["score_mm"], 1)

                scores(0)
                for h in range(XH):
                    if h + 1 < XH:
                        scores(h + 1)
                    pe.wait_ge(s["p_ready"], h + 1)
                    if h >= 1:
                        pe.wait_ge(s["pt_copied"], MB * h)
                    for j in range(MB):
                        for b in range(TB):
                            mm = nc.tensor.transpose(psum[:, 4 + j, b * P:(b + 1) * P], pr[h % 2][:, b, j * P:(j + 1) * P], m.ident[:])
                        mm.then_inc(s["turned"], 1)
                    pe.wait_ge(s["pt_copied"], MB * (h + 1))
                    for e in range(XD):
                        if h >= 1:
                            pe.wait_ge(s["o_lo"], XD * (h - 1) + e + 1)
                        for j in range(MB):
                            mm = nc.tensor.matmul(psum[:, 6 + e, :], v_tm[:, j, (XD * h + e) * P:(XD * h + e + 1) * P], pt[h % 2][:, j, :],
                                                  start=(j == 0), stop=(j == MB - 1))
                        mm.then_inc(s["o_mm"], 1)

            @block.vector
            def _(v):
                st = Steps(v, s["dve_step"])

                def largest(h):
                    v.wait_ge(s["score_mm"], h + 1)
                    bank = psum[:, 2 * (h % 2):2 * (h % 2) + 2, :].rearrange("p a (b n) -> p (a b) n", n=MEM)
                    st.link(v.tensor_reduce(mx[:, h, :], bank, AX, ALU.max))
                    v.tensor_scalar(mx[:, h, :], mx[:, h, :], -scale, None, ALU.mult).then_inc(s["neg_done"], 1)

                def low(h):
                    for o in range(XD * h, XD * h + XD):
                        v.wait_ge(s["o_hi"], o + 1)
                        v.tensor_tensor(out_lo[:, o, :], psum[:, 6 + o % XD, :], out_hi[:, o, :].bitcast(F32), ALU.subtract).then_inc(s["o_lo"], 1)

                largest(0)
                for h in range(XH):
                    if h + 1 < XH:
                        largest(h + 1)
                    v.wait_ge(s["exp_done"], TB * (h + 1))
                    st.link(v.reciprocal(rc[:, h, :], sm_[:, h, :]))
                    v.tensor_tensor(pr[h % 2][:], pr[h % 2][:], rc[:, h, :].rearrange("p (b n) -> p b n", n=1).broadcast_to([P, TB, MEM]), ALU.mult).then_inc(s["p_ready"], 1)
                    if h:
                        low(h - 1)
                low(XH - 1)

            @block.scalar
            def _(a):
                def exps(h):
                    a.wait_ge(s["neg_done"], h + 1)
                    if h >= 2:
                        a.wait_ge(s["turned"], MB * (h - 1))
                    for b in range(TB):
                        a.activation(pr[h % 2][:, b, :], psum[:, 2 * (h % 2) + b // 2, (b % 2) * MEM:(b % 2 + 1) * MEM], ACT.Exp,
                                     bias=mx[:, h, b:b + 1], scale=scale, accum_out=sm_[:, h, b:b + 1]).then_inc(s["exp_done"], 1)

                exps(0)
                for h in range(XH):
                    if h + 1 < XH:
                        exps(h + 1)
                    for j in range(MB):
                        a.wait_ge(s["turned"], MB * h + j + 1)
                        if h >= 2:
                            a.wait_ge(s["o_mm"], XD * (h - 1))
                        a.copy(pt[h % 2][:, j, :], psum[:, 4 + j, :]).then_inc(s["pt_copied"], 1)
                    for e in range(XD):
                        a.wait_ge(s["o_mm"], XD * h + e + 1)
                        a.copy(out_hi[:, XD * h + e, :], psum[:, 6 + e, :]).then_inc(s["o_hi"], 1)


def top16(v, st, rows):
    first = [st.then(v.max(values[:, 0:8], src)) for values, index, src, rest in rows]
    replaced, second = [], []
    for n, (values, index, src, rest) in zip(first, rows):
        st.reach(n)
        st.then(v.max_index(index[:, 0:8], values[:, 0:8], src))
        replaced.append(st.then(v.match_replace(rest, values[:, 0:8], src, -3.0e38)))
    for n, (values, index, src, rest) in zip(replaced, rows):
        st.reach(n)
        second.append(st.then(v.max(values[:, 8:16], rest)))
    for n, (values, index, src, rest) in zip(second, rows):
        st.reach(n)
        st.then(v.max_index(index[:, 8:16], values[:, 8:16], rest))


def keys_stage(nc, io, l, weights, h, val, idx, psum):
    NT = 2 * PH // 4
    with ExitStack() as ctx, stage(nc, *LINEAR_SEMS, "keys_in", "score_mm", "score_copied", "chosen", "dve_step", weights=weights) as s:
        sb = lambda n, sh, dt=F32: ctx.enter_context(buffer(nc, n, sh, dt))
        keys = sb("keys", [P, 2 * PH, PK])
        qT = sb("qT", [P, 2, 4, T])
        sc = sb("sc", [P, TB, 4, PK])
        rest = sb("rest", [P, 4, PK])
        lin = Linear(nc, ctx, s, "fm", weights, h, 4, T, psum)
        units = [(t, q) for t in range(NT) for q in range(4)]
        with nc.Block() as block:
            @block.sync
            def _(sp):
                sp.dma_start(keys[:].rearrange("p a k -> p (a k)"), tile_at(io["keys"], l)).then_inc(s["keys_in"], 16)
                lin.sync(sp)

            @block.tensor
            def _(pe):
                def scores(t):
                    for tb in range(TB):
                        if t:
                            pe.wait_ge(s["score_copied"], TB * (t - 1) + tb + 1)
                        for x in range(4):
                            mm = nc.tensor.matmul(psum[:, 4 + tb, x * PK:(x + 1) * PK], qT[:, t % 2, x, tb * P:(tb + 1) * P], keys[:, 4 * t + x, :], start=True, stop=True)
                        mm.then_inc(s["score_mm"], 1)

                pe.wait_ge(s["keys_in"], 16)
                for t, q in units:
                    lin.unit(pe, t, t % 2, t < 2, q)
                    if t and q == 0:
                        pe.wait_ge(s["evac_done"], 4 * t)
                        scores(t - 1)
                pe.wait_ge(s["evac_done"], 4 * NT)
                scores(NT - 1)

            @block.scalar
            def _(a):
                def query(t, b, bank):
                    if t >= 2:
                        a.wait_ge(s["score_mm"], TB * (t - 1))
                    return a.copy(qT[:, t % 2, b, :], bank)

                def score(t, tb):
                    a.wait_ge(s["score_mm"], TB * t + tb + 1)
                    if t:
                        a.wait_ge(s["chosen"], TB * (t - 1) + tb + 1)
                    a.copy(sc[:, tb].rearrange("p a k -> p (a k)"), psum[:, 4 + tb, :]).then_inc(s["score_copied"], 1)

                for t, q in units:
                    lin.high(a, t, t % 2, t < 2, q)
                    lin.blocks_behind(a, t, t % 2, t < 2, q, query)
                    if t and q:
                        score(t - 1, q - 1)
                    if t and q == 3:
                        score(t - 1, 3)
                lin.last_blocks(a, query)
                for tb in range(TB):
                    score(NT - 1, tb)

            @block.vector
            def _(v):
                st = Steps(v, s["dve_step"])

                def choose(t, tb):
                    v.wait_ge(s["score_copied"], TB * t + tb + 1)
                    top16(v, st, [(val[:, tb, 4 * t + x, :], idx[:, tb, 4 * t + x, :], sc[:, tb, x, :], rest[:, x, :]) for x in range(4)])
                    st.settle()
                    v.engine_nop().then_inc(s["chosen"], 1)

                for n, (t, q) in enumerate(units):
                    lin.low(v, t, t % 2, t < 2, q)
                    if n >= 6:
                        choose((n - 6) // 4, (n - 6) % 4)
                for n in range(4 * NT - 6, 4 * NT):
                    choose(n // 4, n % 4)


def choose_stage(nc, m, io, val, idx, lists, gate_rest, psum):
    with ExitStack() as ctx, stage(nc, "iota_in", "dve_step", "sums_ready", "marked", "numbered", "added_up",
                                   "best_in", "exp_done", "listed", "turned", "list_copied", "gate_lo") as s:
        sb = lambda n, sh, dt=F32: ctx.enter_context(buffer(nc, n, sh, dt))
        two = lambda n, sh, dt=F32: [sb(f"{n}{i}", sh, dt) for i in range(2)]
        hkk = [P, PH, TOPK, TOPK]
        rest = sb("rest", [P, 4, 256])
        cand = two("cand", [P, PH, TOPK * TOPK])
        pos = sb("pos", [P, PH, TOPK], U32)
        idxf = two("idxf", [P, PH, 2, TOPK], F16)
        best = two("best", [P, PH, TOPK])
        ab_i = sb("ab_i", [P, 2, SLOTS], U32)
        ab = sb("ab", [P, 2, SLOTS], F16)
        hot = [two(f"hot{i}", hkk, F16) for i in range(2)]
        numbers = sb("numbers", [P, TOPK])
        which = sb("which", [P, TOPK, TOPK], F16)
        top, den = sb("top", [P, PH]), sb("den", [P, PH])
        out3 = two("out3", [P, 3, SLOTS])
        with nc.Block() as block:
            @block.sync
            def _(sp):
                sp.dma_start(numbers[:], io["c_nvec"][:, 0:TOPK]).then_inc(s["iota_in"], 16)

            @block.tensor
            def _(pe):
                for tb in range(TB):
                    pe.wait_ge(s["listed"], tb + 1)
                    if tb >= 2:
                        pe.wait_ge(s["gate_lo"], 2 * tb - 2)
                    for i in range(3):
                        mm = nc.tensor.transpose(psum[:, 4 + tb % 2, i * P:(i + 1) * P], out3[tb % 2][:, i, :], m.ident[:])
                    mm.then_inc(s["turned"], 1)

            @block.scalar
            def _(a):
                def exps(tb):
                    a.wait_ge(s["best_in"], tb + 1)
                    a.activation(best[tb % 2][:], best[tb % 2][:], ACT.Exp).then_inc(s["exp_done"], 1)

                exps(0)
                for tb in range(TB):
                    if tb + 1 < TB:
                        exps(tb + 1)
                    a.wait_ge(s["turned"], tb + 1)
                    bank, ts = psum[:, 4 + tb % 2, :], slice(tb * P, (tb + 1) * P)
                    a.copy(lists[:, 0:2, ts], bank[:, 0:2 * P].rearrange("p (a t) -> p a t", a=2)).then_inc(s["list_copied"], 1)
                    a.mul(lists[:, 2, ts], bank[:, 2 * P:3 * P], GSCALE).then_inc(s["list_copied"], 1)

            @block.gpsimd
            def _(pool):
                def sums(tb):
                    v4 = val[:, tb].rearrange("p (h s) k -> p h s k", s=2)
                    left = v4[:, :, 0, :].rearrange("p h (a b) -> p h a b", b=1).broadcast_to(hkk)
                    right = v4[:, :, 1, :].rearrange("p h (a b) -> p h a b", a=1).broadcast_to(hkk)
                    pool.tensor_tensor(cand[tb % 2][:].rearrange("p h (a b) -> p h a b", b=TOPK), left, right, ALU.add).then_inc(s["sums_ready"], 1)

                sums(0)
                sums(1)
                for tb in range(TB):
                    for i in range(2):
                        pool.wait_ge(s["marked"], 2 * tb + i + 1)
                        index = idxf[tb % 2][:, :, i, :].rearrange("p h (c k) -> p h c k", k=1).broadcast_to(hkk)
                        pool.tensor_tensor(hot[tb % 2][i][:], hot[tb % 2][i][:], index, ALU.mult).then_inc(s["numbered"], 1)
                    if tb + 2 < TB:
                        sums(tb + 2)

            @block.vector
            def _(v):
                st = Steps(v, s["dve_step"])

                def pick(tb):
                    bt = best[tb % 2]
                    v.wait_ge(s["sums_ready"], tb + 1)
                    for h0 in range(0, PH, 4):
                        top16(v, st, [(bt[:, h, :], pos[:, h, :], cand[tb % 2][:, h, :], rest[:, h % 4, :]) for h in range(h0, h0 + 4)])
                    if tb >= 2:
                        v.wait_ge(s["numbered"], 2 * tb - 2)
                    st.then(v.tensor_copy(idxf[tb % 2][:].rearrange("p h s k -> p (h s) k"), idx[:, tb]))
                    st.settle()
                    fp = pos[:].rearrange("p h k -> p (h k)")
                    st.then(v.tensor_scalar(ab_i[:, 0, :], fp, 4, None, ALU.logical_shift_right))
                    st.then(v.tensor_scalar(ab_i[:, 1, :], fp, TOPK - 1, None, ALU.bitwise_and))
                    st.link(v.tensor_copy(top[:], bt[:, :, 0]))
                    st.then(v.tensor_copy(ab[:], ab_i[:]))
                    v.tensor_tensor(bt[:], bt[:], top[:].rearrange("p (h k) -> p h k", k=1).broadcast_to([P, PH, TOPK]), ALU.subtract).then_inc(s["best_in"], 1)
                    st.settle()
                    if tb >= 2:
                        v.wait_ge(s["added_up"], 2 * tb - 2)
                    for i in range(2):
                        want = ab[:, i, :].rearrange("p (h c k) -> p h c k", h=PH, c=1).broadcast_to(hkk)
                        have = which[:].rearrange("p (h c) k -> p h c k", h=1).broadcast_to(hkk)
                        v.tensor_tensor(hot[tb % 2][i][:], want, have, ALU.is_equal).then_inc(s["marked"], 1)

                def finish(tb):
                    bt, o3 = best[tb % 2], out3[tb % 2]
                    v.wait_ge(s["exp_done"], tb + 1)
                    st.link(v.tensor_reduce(den[:], bt[:], AX, ALU.add))
                    st.link(v.reciprocal(den[:], den[:]))
                    if tb >= 2:
                        v.wait_ge(s["turned"], tb - 1)
                    st.then(v.tensor_tensor(o3[:, 2, :].rearrange("p (h k) -> p h k", h=PH), bt[:],
                                            den[:].rearrange("p (h k) -> p h k", k=1).broadcast_to([P, PH, TOPK]), ALU.mult))
                    for i in range(2):
                        v.wait_ge(s["numbered"], 2 * tb + i + 1)
                        v.tensor_reduce(o3[:, i, :].rearrange("p (h k) -> p h k", h=PH), hot[tb % 2][i][:].rearrange("p h c k -> p h k c"), AX, ALU.add).then_inc(s["added_up"], 1)
                    st.settle()
                    v.wait_ge(s["added_up"], 2 * tb + 2)
                    v.engine_nop().then_inc(s["listed"], 1)

                def low_part(tb):
                    v.wait_ge(s["list_copied"], 2 * tb + 2)
                    ts = slice(tb * P, (tb + 1) * P)
                    v.scalar_tensor_tensor(lists[:, 3, ts], psum[:, 4 + tb % 2, 2 * P:3 * P], GSCALE, lists[:, 2, ts], ALU.mult, ALU.subtract).then_inc(s["gate_lo"], 1)
                    v.scalar_tensor_tensor(gate_rest[:, ts], psum[:, 4 + tb % 2, 2 * P:3 * P], GSCALE, lists[:, 2, ts], ALU.mult, ALU.subtract).then_inc(s["gate_lo"], 1)

                v.wait_ge(s["iota_in"], 16)
                st.link(v.tensor_copy(which[:], numbers[:].rearrange("p (c k) -> p c k", k=1).broadcast_to([P, TOPK, TOPK])))
                for tb in range(TB):
                    pick(tb)
                    if tb >= 2:
                        low_part(tb - 2)
                    if tb:
                        finish(tb - 1)
                low_part(TB - 2)
                finish(TB - 1)
                low_part(TB - 1)


def expert_gates_stage(nc, io, lists, gate_rest, psum):
    BT = 16
    SPC = GCH // BT
    BA = BT // 2
    with ExitStack() as ctx, stage(nc, "iota_in", "iota_made", "hot", "weighed", "rest_weighed", "gate_mm", "gate_copied", "gate_out0", "gate_out1") as s:
        sb = lambda n, sh, dt=F16: ctx.enter_context(buffer(nc, n, sh, dt))
        iota = sb("iota", [P, P], F32)
        ids = sb("ids", [P, P, BT])
        hot_j = [sb(f"hot_j{i}", [P, P, BT]) for i in range(2)]
        hot_i = [sb(f"hot_i{i}", [P, P, BT]) for i in range(2)]
        part = [sb(f"part{i}", [P, 2, P, BT]) for i in range(2)]
        held = [sb(f"held{i}", [P, P, GCH], F32) for i in range(2)]
        out_sem = (s["gate_out0"], s["gate_out1"])
        with nc.Block() as block:
            @block.sync
            def _(sp):
                sp.dma_start(iota[:], io["c_iota"]).then_inc(s["iota_in"], 16)

                def store(c, p, first):
                    sp.wait_ge(s["gate_copied"], (c + 1) * SPC)
                    sp.dma_start(tile_at(io["g_scratch"], c), held[p][:].rearrange("p i t -> p (i t)")).then_inc(out_sem[p], 16)
                over_pairs(sp, T // GCH, store)
                for q in out_sem:
                    sp.wait_ge(q, 16 * (T // GCH // 2))

            @block.vector
            def _(v):
                v.wait_ge(s["iota_in"], 16)
                v.tensor_copy(ids[:], iota[:].rearrange("p (i t) -> p i t", t=1).broadcast_to([P, P, BT])).then_inc(s["iota_made"], 1)
                v.wait_ge(s["iota_made"], 1)

                def make(c, p, first):
                    for k in range(SPC):
                        n, b = c * SPC + k, k % 2
                        if not (first and p == 0 and k < 2):
                            v.wait_ge(s["gate_mm"], n - 1)
                        row = lambda x: lists[:, x:x + 1, bass.ds(c * GCH + k * BT, BT)].broadcast_to([P, P, BT])
                        v.tensor_tensor(hot_i[b][:], ids[:], row(0), ALU.is_equal).then_inc(s["hot"], 1)
                        v.tensor_tensor(hot_j[b][:], ids[:], row(1), ALU.is_equal).then_inc(s["hot"], 1)
                        v.wait_ge(s["hot"], n * 2 + 2)
                        v.tensor_tensor(part[b][:, 0], hot_i[b][:], row(2), ALU.mult).then_inc(s["weighed"], 1)
                        late = lists[:, 3:4, bass.ds(c * GCH + k * BT + BA, BT - BA)].broadcast_to([P, P, BT - BA])
                        v.tensor_tensor(part[b][:, 1, :, BA:], hot_i[b][:, :, BA:], late, ALU.mult).then_inc(s["weighed"], 1)
                over_pairs(v, T // GCH, make)

            @block.tensor
            def _(pe):
                def products(c, p, first):
                    for k in range(SPC):
                        n, b = c * SPC + k, k % 2
                        pe.wait_ge(s["weighed"], n * 2 + 2)
                        pe.wait_ge(s["rest_weighed"], n * BA + BA)
                        if not (first and p == 0 and k < 2):
                            pe.wait_ge(s["gate_copied"], n - 1)
                        for t in range(BT):
                            for x in range(2):
                                mm = nc.tensor.matmul(psum[:, 4 * b + t // 4, (t % 4) * P:(t % 4 + 1) * P], hot_j[b][:, :, t], part[b][:, x, :, t],
                                                      start=(x == 0), stop=(x == 1))
                        mm.then_inc(s["gate_mm"], 1)
                over_pairs(pe, T // GCH, products)

            @block.scalar
            def _(a):
                def weigh(n, k, t0):
                    a.wait_ge(s["hot"], n * 2 + 1)
                    for t in range(BA):
                        a.activation(part[k % 2][:, 1, :, t], hot_i[k % 2][:, :, t], ACT.Copy, scale=gate_rest[:, bass.ds(t0 + t, 1)]).then_inc(s["rest_weighed"], 1)

                def copy(n, k, p):
                    a.wait_ge(s["gate_mm"], n + 1)
                    a.activation(held[p][:, :, k * BT:(k + 1) * BT].rearrange("p i t -> p t i"),
                                 psum[:, 4 * (k % 2):4 * (k % 2) + 4, :].rearrange("p a (t i) -> p (a t) i", i=P), ACT.Copy, scale=1.0 / GSCALE).then_inc(s["gate_copied"], 1)

                def chunk(c, p, first):
                    for k in range(SPC):
                        n = c * SPC + k
                        weigh(n, k, c * GCH + k * BT)
                        if k == 1 and not first:
                            a.wait_ge(out_sem[p], (c - p) * 8)
                        if k:
                            copy(n - 1, k - 1, p)
                        elif not (first and p == 0):
                            copy(n - 1, SPC - 1, 1 - p)
                over_pairs(a, T // GCH, chunk)
                copy(T // BT - 1, SPC - 1, 1)


def experts_stage(nc, m, io, l, h_hi, h_lo, psum):
    NG = PK // GE
    with ExitStack() as ctx, stage(nc, "u_in0", "u_in1", "v_in0", "v_in1", "g_in0", "g_in1", "u_hi", "u_lo", "v_hi", "v_lo",
                                   "dot_mm", "gelu_done", "gated", "act_hi", "act_lo", "y_mm", "y_added") as s:
        sb = lambda n, sh, dt=F32: ctx.enter_context(buffer(nc, n, sh, dt))
        u = [sb(f"u{i}", [P, D]) for i in range(2)]
        uh = [sb(f"uh{i}", [P, KD, P], F32R) for i in range(2)]
        ul = [sb(f"ul{i}", [P, KD, P], F32R) for i in range(2)]
        vv = [sb(f"v{i}", [P, D]) for i in range(2)]
        vh = [sb(f"vh{i}", [P, GE, D], F32R) for i in range(2)]
        vl = [sb(f"vl{i}", [P, GE, D], F32R) for i in range(2)]
        ah = [sb(f"ah{i}", [P, GE, T], F32R) for i in range(2)]
        al = [sb(f"al{i}", [P, GE, T], F32R) for i in range(2)]
        ge = [sb(f"ge{i}", [P, T]) for i in range(2)]
        gate = [sb(f"gate{i}", [P, T // GCH, GE, GCH]) for i in range(2)]
        u_in, v_in, g_in = (s["u_in0"], s["u_in1"]), (s["v_in0"], s["v_in1"]), (s["g_in0"], s["g_in1"])
        row0 = l * PK
        fw = lambda t: t[:].rearrange("p k e -> p (k e)")
        with nc.Block() as block:
            @block.sync
            def _(sp):
                def load_u(n, early, par):
                    if not early:
                        sp.wait_ge(s["u_lo"], n - 1)
                    sp.dma_start(u[par][:], tile_at(io["peer_u"], row0 + n)).then_inc(u_in[par], 16)

                def load(g, p, first, last):
                    if first and p == 0:
                        load_u(0, True, 0)
                    if not first:
                        sp.wait_ge(s["gated"], (g - 1) * GE)
                    sp.dma_start(gate[p][:].rearrange("p c r t -> p c (r t)"),
                                 io["g_scratch"].rearrange("c p (i t) -> p c i t", t=GCH)[:, :, bass.ds(g * GE, GE), :].rearrange("p c i t -> p c (i t)")
                                 ).then_inc(g_in[p], 16)
                    for r in range(GE):
                        n = g * GE + r
                        if not (last and r == GE - 1):
                            load_u(n + 1, first and p == 0 and r == 0, (r + 1) % 2)
                        if not (first and p == 0 and r < 2):
                            sp.wait_ge(s["v_lo"], n - 1)
                        sp.dma_start(vv[r % 2][:], tile_at(io["peer_v"], row0 + n)).then_inc(v_in[r % 2], 16)
                over_groups(sp, NG, load)

            @block.tensor
            def _(pe):
                def dots(g, p, first):
                    for r in range(GE):
                        n = g * GE + r
                        pe.wait_ge(s["u_lo"], n + 1)
                        if not (first and p == 0):
                            pe.wait_ge(s["gelu_done"], n - 3)
                        three = [(uh, h_lo), (ul, h_hi), (uh, h_hi)]
                        for x, (w, h) in enumerate(three):
                            for k in range(KD):
                                mm = nc.tensor.matmul(psum[:, r, :], w[r % 2][:, k, :], h[:, k, :], start=(x == 0 and k == 0), stop=(x == 2 and k == KD - 1))
                        mm.then_inc(s["dot_mm"], 1)

                def sums(g, p, early):
                    pe.wait_ge(s["v_lo"], g * GE + GE)
                    pe.wait_ge(s["act_lo"], g * GE + GE)
                    for o in range(8):
                        b, half = o // 2, o % 2
                        if not (early and o < 4):
                            pe.wait_ge(s["y_added"], g * 8 + o - 3)
                        for r in range(GE):
                            for x, (w, q) in enumerate([(ah, vl), (al, vh), (ah, vh)]):
                                mm = nc.tensor.matmul(psum[:, 4 + o % 4, :], w[p][:, r, b * P:(b + 1) * P], q[p][:, r, half * W:(half + 1) * W],
                                                      start=(r == 0 and x == 0), stop=(r == GE - 1 and x == 2))
                        mm.then_inc(s["y_mm"], 1)

                def group(g, p, first, last):
                    dots(g, p, first)
                    if not (first and p == 0):
                        sums(g - 1, 1 - p, first)
                over_groups(pe, NG, group)
                sums(NG - 1, (NG - 1) % 2, False)

            @block.scalar
            def _(a):
                def high_u(n, k, early, par):
                    a.wait_ge(u_in[par], k)
                    if not early:
                        a.wait_ge(s["dot_mm"], n - 1)
                    a.copy(fw(uh[par]), u[par][:]).then_inc(s["u_hi"], 1)

                def group(g, p, first, last):
                    if first and p == 0:
                        high_u(0, 16, True, 0)
                    for r in range(GE):
                        n = g * GE + r
                        if not (last and r == GE - 1):
                            high_u(n + 1, g * 32 + 16 * ((r + 1) // 2) + 16, first and p == 0 and r == 0, (r + 1) % 2)
                        a.wait_ge(v_in[r % 2], g * 32 + 16 * (r // 2) + 16)
                        if not first:
                            a.wait_ge(s["y_mm"], (g - 1) * 8)
                        a.copy(vh[p][:, r, :], vv[r % 2][:]).then_inc(s["v_hi"], 1)
                        a.wait_ge(s["dot_mm"], n + 1)
                        if not (first and p == 0 and r < 2):
                            a.wait_ge(s["act_lo"], n - 1)
                        a.activation(ge[r % 2][:], psum[:, r, :], ACT.Gelu_apprx_tanh).then_inc(s["gelu_done"], 1)
                        a.wait_ge(s["gated"], n + 1)
                        a.copy(ah[p][:, r, :], ge[r % 2][:]).then_inc(s["act_hi"], 1)
                over_groups(a, NG, group)

            @block.vector
            def _(v):
                def low_u(n, par):
                    v.wait_ge(s["u_hi"], n + 1)
                    v.tensor_tensor(fw(ul[par]), u[par][:], fw(uh[par]).bitcast(F32), ALU.subtract).then_inc(s["u_lo"], 1)

                def add(g, early):
                    for o in range(8):
                        b, half = o // 2, o % 2
                        v.wait_ge(s["y_mm"], g * 8 + o + 1)
                        if not early:
                            v.wait_ge(s["y_added"], (g - 1) * 8 + o + 1)
                        x = m.X[:, b, half * W:(half + 1) * W]
                        v.tensor_tensor(x, psum[:, 4 + o % 4, :], x, ALU.add).then_inc(s["y_added"], 1)

                def group(g, p, first, last):
                    if first and p == 0:
                        low_u(0, 0)
                    v.wait_ge(g_in[p], 16 if first else (g - p) * 8 + 16)
                    for r in range(GE):
                        n = g * GE + r
                        if not (last and r == GE - 1):
                            low_u(n + 1, (r + 1) % 2)
                        v.wait_ge(s["v_hi"], n + 1)
                        v.tensor_tensor(vl[p][:, r, :], vv[r % 2][:], vh[p][:, r, :].bitcast(F32), ALU.subtract).then_inc(s["v_lo"], 1)
                        v.wait_ge(s["gelu_done"], n + 1)
                        act = ge[r % 2][:].rearrange("p (c t) -> p c t", t=GCH)
                        v.tensor_tensor(act, act, gate[p][:, :, r, :], ALU.mult).then_inc(s["gated"], 1)
                        v.wait_ge(s["act_hi"], n + 1)
                        v.tensor_tensor(al[p][:, r, :], ge[r % 2][:], ah[p][:, r, :].bitcast(F32), ALU.subtract).then_inc(s["act_lo"], 1)
                    if not (first and p == 0):
                        add(g - 1, first)
                over_groups(v, NG, group)
                add(NG - 1, False)


def final_stage(nc, m, io):
    with ExitStack() as ctx, stage(nc, "gain_in", "sumsq", "dve_step", "root", "ready", "stored") as s:
        gain = ctx.enter_context(buffer(nc, "gain", [P, D], F32))
        junk = ctx.enter_context(buffer(nc, "junk", [P, D], F32))
        ss = ctx.enter_context(buffer(nc, "fss", [P, 2, TB], F32))
        with nc.Block() as block:
            @block.sync
            def _(sp):
                sp.dma_start(gain[:], io["norm_final"].partition_broadcast(P)).then_inc(s["gain_in"], 16)
                for b in range(TB):
                    sp.wait_ge(s["ready"], b + 1)
                    sp.dma_start(io["out"][b * P:(b + 1) * P, :], m.X[:, b, :]).then_inc(s["stored"], 16)
                sp.wait_ge(s["stored"], 16 * TB)

            @block.scalar
            def _(a):
                for b in range(TB):
                    if b:
                        a.wait_ge(s["sumsq"], b)
                    a.activation(junk[:], m.X[:, b, :], ACT.Square, accum_out=ss[:, 0, b:b + 1]).then_inc(s["sumsq"], 1)
                a.wait_ge(s["dve_step"], 1)
                a.activation(ss[:, 1, :], ss[:, 0, :], ACT.Sqrt).then_inc(s["root"], 1)

            @block.vector
            def _(v):
                st = Steps(v, s["dve_step"])
                v.wait_ge(s["sumsq"], TB)
                st.then(v.tensor_scalar(ss[:, 0, :], ss[:, 0, :], 1.0 / D, EPS, ALU.mult, ALU.add))
                v.wait_ge(s["root"], 1)
                v.wait_ge(s["gain_in"], 16)
                st.link(v.reciprocal(ss[:, 0, :], ss[:, 1, :]))
                for b in range(TB):
                    v.scalar_tensor_tensor(m.X[:, b, :], m.X[:, b, :], ss[:, 0, b:b + 1], gain[:], ALU.mult, ALU.mult).then_inc(s["ready"], 1)


def copy_to(a, dst):
    def copy(t, b, bank):
        n = bank.shape[-1]
        return a.copy(dst[:, bass.ds(t * 4 + b, 1), 0:n].rearrange("p a n -> p (a n)"), bank)
    return copy


def load_small_stage(nc, io, l, sm):
    with stage(nc, "small_in") as s:
        with nc.Block() as block:
            @block.sync
            def _(sp):
                sp.dma_start(sm[:], tile_at(io["small"], l)).then_inc(s["small_in"], 16)
                sp.wait_ge(s["small_in"], 16)


def mixer_layer(nc, m, io, l, sm, psum):
    a = nc.scalar
    part = lambda t, i: t[:, 4 * i:4 * i + 4, :]
    with buffer(nc, "fm", [P, 28, T], F32) as fm:
        with buffer(nc, "tm", [P, 2 * TB, W], F32) as tm:
            with hi_lo(nc, "hT", [P, KD, T]) as h, ExitStack() as ctx:
                raw = two_tiles(nc, ctx)
                w_fm = Weights(m, raw, 0, 7, lambda t: tile_at(io["w_fm"], l * 7 + t))
                w_tm = Weights(m, raw, 1, 2, lambda t: tile_at(io["w_tm"], l * 2 + t))
                norm_stage(nc, m, m.X, TB, sm[:, 0:KD], h, psum, w_fm)
                linear_stage(nc, "fm", w_fm, h, 4, T, psum, copy_to(a, fm), following=w_tm)
                linear_stage(nc, "tm", w_tm, h, 4, T, psum, copy_to(a, tm))
            hgrn_stage(nc, m, l, part(fm, 0), part(fm, 1), part(fm, 2), part(tm, 0), part(fm, 0), psum, io, sm)
            retention_stage(nc, m, part(fm, 3), part(fm, 4), part(fm, 5), part(tm, 1), part(fm, 4), psum, io)
            with ExitStack() as ctx:
                sb = lambda n, sh: ctx.enter_context(buffer(nc, n, sh, F32))
                tabs = SsmTables(sin=sb("tsin", [P, G5 * N5]), cos=sb("tcos", [P, G5 * N5]), decay=sb("tdec", [P, G5 * N5]),
                                       gb=sb("gb", [P, G5, J5, C5]), pc=sb("pc", [P, G5, 2 * J5, C5]))
                ssm_tables_stage(nc, m, io, l, sm, tabs, [part(fm, i) for i in (1, 3, 5)])
                ssm_stage(nc, m, sm, tabs, part(fm, 6), [part(fm, i) for i in (1, 3, 5)], part(fm, 2),
                          tm[0:N5, :, :], tile_at(io["w_glu"], l), psum)
        glu_stage(nc, part(fm, 6), part(fm, 1), part(fm, 2), sm, psum)
        with buffer(nc, "gates", [P, 3 * KD, T], F32) as gates, ExitStack() as ctx:
            raw = two_tiles(nc, ctx)
            w_gate = Weights(m, raw, 0, 6, lambda t: tile_at(io["w_gate"], l * 6 + t))
            w_branch = Weights(m, raw, 1, 6, lambda t: tile_at(io["w_branch"], l * 6 + t), depth=4)
            w_out = Weights(m, raw, 0, 2, lambda t: tile_at(io["w_out"], l * 2 + t))
            with hi_lo(nc, "hT", [P, KD, T]) as h:
                norm_stage(nc, m, m.X, TB, sm[:, 0:KD], h, psum, w_gate)
                gates_stage(nc, w_gate, h, sm, gates, psum, w_branch)
            with hi_lo(nc, "merged", [P, KD, T]) as parts:
                merge_stage(nc, w_branch, [part(fm, i) for i in (0, 2, 4)], gates, parts, w_out, psum)
                residual_stage(nc, m, w_out, parts, psum)


def residual_stage(nc, m, weights, act, psum):
    v = nc.vector

    def add(t, b, bank):
        x = m.X[:, b, t * W:(t + 1) * W]
        return v.tensor_tensor(x, bank, x, ALU.add)
    linear_stage(nc, "tm", weights, act, TB, W, psum, add, on="vector")


def cross_layer(nc, m, io, l, sm, psum):
    a = nc.scalar
    with ExitStack() as ctx:
        sb = lambda n, sh, dt=F32: ctx.enter_context(buffer(nc, n, sh, dt))
        kT = sb("kT", [P, KD, MEM])
        v_tm = sb("v_tm", [P, MB, D])
        qT = sb("qT", [P, KD, T])
        raw = two_tiles(nc, ctx)
        w_k, w_v, w_q, w_o = (Weights(m, raw, i + 1, 2, lambda t, name=name: tile_at(io[name], l * 2 + t))
                              for i, name in enumerate(("xa_k", "xa_v", "xa_q", "xa_o")))
        c = COL["norm_mem"][0]
        with hi_lo(nc, "memT", [P, KD, MEM]) as memT:
            with buffer(nc, "mem", [P, MB, D], F32) as mem:
                norm_stage(nc, m, mem, MB, sm[:, c:c + KD], memT, psum, w_k, load=[(mem[:], io["mem"])])
            linear_stage(nc, "fm", w_k, memT, 4, MEM, psum, copy_to(a, kT), following=w_v)

            def v_copy(t, b, bank):
                return a.copy(v_tm[:, b, t * W:(t + 1) * W], bank)
            linear_stage(nc, "tm", w_v, memT, MB, W, psum, v_copy, following=w_q)
        c = COL["norm_cross"][0]
        with hi_lo(nc, "hT", [P, KD, T]) as h:
            norm_stage(nc, m, m.X, TB, sm[:, c:c + KD], h, psum, None)
            linear_stage(nc, "fm", w_q, h, 4, T, psum, copy_to(a, qT), following=w_o)
        with hi_lo(nc, "oT", [P, KD, T]) as o_parts:
            attend_stage(nc, m, qT, kT, v_tm, o_parts, psum)
            residual_stage(nc, m, w_o, o_parts, psum)


def expert_layer(nc, m, io, l, sm, psum):
    c = COL["norm_ffn"][0]
    with hi_lo(nc, "h", [P, KD, T]) as h:
        with buffer(nc, "lists", [P, 4, T], F16) as lists, buffer(nc, "gate_rest", [P, T], F32) as gate_rest:
            with buffer(nc, "val", [P, TB, 2 * PH, TOPK], F32) as val, buffer(nc, "idx", [P, TB, 2 * PH, TOPK], U32) as idx:
                with ExitStack() as ctx:
                    w_query = Weights(m, two_tiles(nc, ctx), 1, 4, lambda t: tile_at(io["peer_wq"], l * 4 + t))
                    norm_stage(nc, m, m.X, TB, sm[:, c:c + KD], h, psum, w_query)
                    keys_stage(nc, io, l, w_query, h, val, idx, psum)
                choose_stage(nc, m, io, val, idx, lists, gate_rest, psum)
            expert_gates_stage(nc, io, lists, gate_rest, psum)
        experts_stage(nc, m, io, l, h[0], h[1], psum)


def trunk(nc, io):
    m = Resident()
    m.X = nc.alloc_sbuf_tensor("X", [P, TB, D], F32)
    m.ident = nc.alloc_sbuf_tensor("ident", [P, P], F32)
    m.perm = nc.alloc_sbuf_tensor("perm", [P, P], F32)
    m.ones = nc.alloc_sbuf_tensor("ones", [P, P], F32)
    m.one_col = nc.alloc_sbuf_tensor("one_col", [P, 2 * HC - 1], F32)
    m.cols = nc.alloc_sbuf_tensor("cols", [P, 3], F32)
    m.sin = nc.alloc_sbuf_tensor("sin", [P, T], F32)
    m.cos = nc.alloc_sbuf_tensor("cos", [P, T], F32)
    m.lb_all = nc.alloc_sbuf_tensor("lb_all", [P, L, H], F32)
    sm = nc.alloc_sbuf_tensor("small", [P, NSMALL], F32)
    psum = nc.alloc_psum_tensor("psum", [P, 8, 512], F32)
    _pool[:] = [nc.alloc_semaphore(f"stage_sem{i}") for i in range(28)]
    m.weights_in = [[nc.alloc_semaphore(f"weights_in{i}{p}") for p in range(2)] for i in range(2)]
    setup_stage(nc, io, m)
    with nc.Fori(0, L) as l:
        load_small_stage(nc, io, l, sm)
        mixer_layer(nc, m, io, l, sm, psum)
        cross_layer(nc, m, io, l, sm, psum)
        expert_layer(nc, m, io, l, sm, psum)
    final_stage(nc, m, io)



def _constants():
    f = np.float32
    half = P // 2
    inv = (np.float32(10000.0) ** (-np.arange(half, dtype=f) / f(half))).astype(f)
    p = np.arange(P)
    perm = np.zeros((P, P), f)
    perm[p, (p + half) % P] = 1
    sign = np.where(p < half, -1.0, 1.0).astype(f)
    s_, t_ = np.meshgrid(p, p, indexing="ij")
    masks = [s_ == t_]
    for w in LEVELS:
        masks.append((s_ // (2 * w) == t_ // (2 * w)) & (s_ % (2 * w) < w) & (t_ % (2 * w) >= w))
    masks = np.stack(masks, 1).astype(np.int32)
    rel = np.arange(T)[None, :] - p[:, None]
    log_g = np.log1p(-np.exp2(-5.0 - np.arange(H)))
    dmat = np.stack([np.where(rel >= 0, np.exp(lg * np.maximum(rel, 0)), 0.0) for lg in log_g], 1) * P ** -0.5
    return {"c_ident": np.eye(P, dtype=f), "c_perm": perm, "c_cols": np.stack([np.tile(inv, 2), sign, -sign], 1),
            "c_masks": masks, "c_dmat": dmat.astype(f), "c_nvec": np.tile(np.arange(N5, dtype=f), (P, 1)),
            "c_iota": np.tile(np.arange(P, dtype=f), (P, 1))}


def _layout(a):
    def tiles(w, order=None):
        w = w.reshape(L, -1, P, w.shape[2] // W, W).transpose(0, 3, 2, 1, 4)
        w = w if order is None else w[:, order]
        return np.ascontiguousarray(w).reshape(w.shape[0] * w.shape[1], P, -1)

    def cols(v):
        return v.reshape(L, -1, P).transpose(0, 2, 1)
    both = lambda v: np.concatenate([v, v], 1)
    lam = lambda v: both(v.transpose(0, 2, 1))
    small = np.concatenate([
        cols(a["norm_mix"]), cols(a["norm_cross"]), cols(a["norm_mem"]), cols(a["norm_ffn"]), cols(a["b_gate"]),
        cols(a["hgrn_norm"]), cols(a["s5_b_glu"]),
        np.tile(a["s5_d"].reshape(L, G5, C5).transpose(0, 2, 1), (1, J5, 1)),
        lam(a["s5_lambda_re"]), lam(a["s5_lambda_im"]), np.repeat(a["s5_log_step"][:, None, :], P, 1)], 2)
    br, bi = (a[f"s5_b_{x}"].transpose(0, 2, 1, 3) for x in ("re", "im"))
    cr, ci = (a[f"s5_c_{x}"].transpose(0, 3, 1, 2) for x in ("re", "im"))
    cat = lambda x, y: np.concatenate([x, y], 1)
    bc = np.stack([cat(br, bi), cat(bi, br), cat(cr, ci), cat(ci, cr)], 2).reshape(L, P, -1)
    w_in = a["w_in"]
    rows = lambda v: v.reshape(-1, P, v.shape[-1]).transpose(1, 0, 2)
    wbr = a["w_branch"].reshape(L, 3, 4, P, 2, W).transpose(0, 1, 4, 3, 2, 5).reshape(L * 6, P, -1)
    u = a["peer_u"].reshape(L * PK, P, KD, P).transpose(0, 3, 2, 1).reshape(L * PK, P, -1)
    return {
        "x": rows(a["x"][0]), "mem": rows(a["mem"][0]), "positions": a["positions"][0],
        "hgrn_lb": a["hgrn_lb"].reshape(L, H, P).transpose(2, 0, 1), "small": small, "s5_bc": bc,
        "w_fm": tiles(w_in[:, :, :15 * W], [0, 1, 3, 5, 6, 8, 4]), "w_tm": tiles(w_in[:, :, :15 * W], [2, 7]),
        "w_gate": tiles(w_in[:, :, 9 * W:]), "w_glu": tiles(a["s5_w_glu"]), "w_branch": wbr, "w_out": tiles(a["w_out"]),
        "xa_q": tiles(a["xa_wq"]), "xa_k": tiles(a["xa_wkv"][:, :, :D]), "xa_v": tiles(a["xa_wkv"][:, :, D:]),
        "xa_o": tiles(a["xa_wo"]), "peer_wq": tiles(a["peer_wq"]),
        "keys": a["peer_keys"].reshape(L, 2 * PH, PK, P).transpose(0, 3, 1, 2).reshape(L, P, -1),
        "peer_u": u, "peer_v": a["peer_v"].reshape(L * PK, P, D), "norm_final": a["norm_final"],
    }


def kernel(**inputs):
    import concourse.bacc as bacc
    from concourse.bass_utils import run_bass_kernel_spmd

    nc = bacc.Bacc("TRN2", target_bir_lowering=False, num_devices=1)
    arrays = {}
    laid = _layout({k: np.asarray(v) for k, v in inputs.items()})
    laid.update(_constants())
    aps = {}
    for name, a in laid.items():
        a = np.ascontiguousarray(a)
        arrays[f"in_{name}"] = a
        aps[name] = nc.dram_tensor(f"in_{name}", a.shape, mybir.dt.from_np(a.dtype), kind="ExternalInput").ap()
    aps["out"] = nc.dram_tensor("out_x", (T, D), F32, kind="ExternalOutput").ap()
    aps["g_scratch"] = nc.dram_tensor("g_scratch", (T // GCH, P, P * GCH), F32, kind="Internal").ap()
    trunk(nc, aps)
    r = run_bass_kernel_spmd(nc, [arrays], core_ids=[0])
    return np.asarray(r.results[0]["out_x"]).reshape(1, T, D)
```
